# Optimizing a Trainium2 kernel written in Bass

```python
import jax, jax.numpy as jnp
from jax import lax
import numpy as np

D_MODEL = 1024
BATCH = 1
SEQ = 512
DEPTH = 2

CHUNK = 64
MIX_WIDTH = D_MODEL
ATT_HEADS = 8
ATT_HEAD_DIM = 64
ATT_WIDTH = ATT_HEADS * ATT_HEAD_DIM
LEFT_CHUNKS = 8
BAND = (LEFT_CHUNKS + 1) * CHUNK
REL_CLIP = 256
RET_HEADS = 4
RET_HEAD_DIM = 128
RET_WIDTH = RET_HEADS * RET_HEAD_DIM
SPLIT_WIDTHS = (ATT_WIDTH, ATT_WIDTH, ATT_WIDTH, ATT_WIDTH,
                RET_WIDTH, RET_WIDTH, RET_WIDTH, RET_WIDTH)
IN_WIDTH = sum(SPLIT_WIDTHS)
EPS = 1e-6
ROPE_BASE = 10000.0
NEG_INF = -1e30


def rms_norm(x, gain=None):
    xf = x.astype(jnp.float32)
    y = xf * lax.rsqrt(jnp.mean(xf * xf, axis=-1, keepdims=True) + EPS)
    if gain is not None:
        y = y * gain.astype(jnp.float32)
    return y.astype(x.dtype)

def rotary_tables(positions, dim):
    inv_freq = 1.0 / (ROPE_BASE ** jnp.linspace(0.0, 1.0, dim // 2, dtype=jnp.float32))
    ang = positions.astype(jnp.float32)[:, None] * inv_freq[None, :]
    return jnp.cos(ang), jnp.sin(ang)

def apply_rotary(t, cos, sin):
    t1, t2 = jnp.split(t, 2, axis=-1)
    c = cos[None, :, None, :]
    s = sin[None, :, None, :]
    return jnp.concatenate([t1 * c - t2 * s, t1 * s + t2 * c], axis=-1)

def chunked_rel_attention(q, k, v, rel_bias):
    b, s, h, dh = q.shape
    nc = s // CHUNK
    qc = q.astype(jnp.float32).reshape(b, nc, CHUNK, h, dh)
    pad = ((0, 0), (LEFT_CHUNKS * CHUNK, 0), (0, 0), (0, 0))
    kp = jnp.pad(k.astype(jnp.float32), pad).reshape(b, nc + LEFT_CHUNKS, CHUNK, h, dh)
    vp = jnp.pad(v.astype(jnp.float32), pad).reshape(b, nc + LEFT_CHUNKS, CHUNK, h, dh)
    kb = jnp.concatenate([kp[:, j:j + nc] for j in range(LEFT_CHUNKS + 1)], axis=2)
    vb = jnp.concatenate([vp[:, j:j + nc] for j in range(LEFT_CHUNKS + 1)], axis=2)
    scores = jnp.einsum("bnqhd,bnkhd->bnhqk", qc, kb) * (dh ** -0.5)
    q_off = jnp.arange(CHUNK)[:, None] + LEFT_CHUNKS * CHUNK
    k_off = jnp.arange(BAND)[None, :]
    dist = q_off - k_off
    bias = rel_bias.astype(jnp.float32)[:, jnp.clip(dist, -REL_CLIP, REL_CLIP) + REL_CLIP]
    key_pos = (jnp.arange(nc)[:, None] - LEFT_CHUNKS) * CHUNK + k_off
    valid = (key_pos >= 0)[None, :, None, None, :]
    scores = jnp.where(valid, scores + bias[None, None], NEG_INF)
    p = jax.nn.softmax(scores, axis=-1)
    out = jnp.einsum("bnhqk,bnkhd->bnqhd", p, vb)
    return out.reshape(b, s, h * dh)

def chunkwise_retention(q, k, v, cos, sin):
    b, s, h, dk = q.shape
    dv = v.shape[-1]
    nc = s // CHUNK
    q = apply_rotary(q.astype(jnp.float32), cos, sin)
    k = apply_rotary(k.astype(jnp.float32), cos, sin) * (dk ** -0.5)
    v = v.astype(jnp.float32)
    log_g = jnp.log1p(-jnp.exp2(-5.0 - jnp.arange(h, dtype=jnp.float32)))
    idx = jnp.arange(CHUNK, dtype=jnp.float32)
    intra_decay = jnp.exp(jnp.abs(idx[:, None] - idx[None, :])[None] * log_g[:, None, None])
    k_decay = jnp.exp((CHUNK - 1 - idx)[None, :] * log_g[:, None])
    q_decay = jnp.exp((idx + 1.0)[None, :] * log_g[:, None])
    chunk_decay = jnp.exp(CHUNK * log_g)
    qc = q.reshape(b, nc, CHUNK, h, dk)
    kc = k.reshape(b, nc, CHUNK, h, dk)
    vc = v.reshape(b, nc, CHUNK, h, dv)
    att = jnp.einsum("bnihd,bnjhd->bnhij", qc, kc) * intra_decay[None, None]
    o_intra = jnp.einsum("bnhij,bnjhe->bnihe", att, vc)
    kv = jnp.einsum("bnjhd,hj,bnjhe->bnhde", kc, k_decay, vc)

    def step(state, kv_n):
        return state * chunk_decay[None, :, None, None] + kv_n, state

    _, states = lax.scan(step, jnp.zeros((b, h, dk, dv), jnp.float32), jnp.moveaxis(kv, 1, 0))
    states = jnp.moveaxis(states, 0, 1)
    o_inter = jnp.einsum("bnihd,hi,bnhde->bnihe", qc, q_decay, states)
    o = rms_norm(o_intra + o_inter)
    return o.reshape(b, s, h * dv)

def hybrid_layer(x, norm_gain, w_in, w_out, rel_bias, cos, sin):
    b, s, _ = x.shape
    hn = rms_norm(x, norm_gain)
    proj = hn @ w_in.astype(hn.dtype)
    cuts = list(np.cumsum(SPLIT_WIDTHS)[:-1])
    aq, ak, av, ag, rq, rk, rv, rg = jnp.split(proj, cuts, axis=-1)
    ya = chunked_rel_attention(aq.reshape(b, s, ATT_HEADS, ATT_HEAD_DIM),
                               ak.reshape(b, s, ATT_HEADS, ATT_HEAD_DIM),
                               av.reshape(b, s, ATT_HEADS, ATT_HEAD_DIM), rel_bias)
    yr = chunkwise_retention(rq.reshape(b, s, RET_HEADS, RET_HEAD_DIM),
                             rk.reshape(b, s, RET_HEADS, RET_HEAD_DIM),
                             rv.reshape(b, s, RET_HEADS, RET_HEAD_DIM), cos, sin)
    y = jnp.concatenate([ya * jax.nn.silu(ag.astype(jnp.float32)),
                         yr * jax.nn.silu(rg.astype(jnp.float32))], axis=-1).astype(x.dtype)
    return x + y @ w_out.astype(x.dtype)

def first_inputs(seed: int = 0) -> dict:
    key = jax.random.key(seed)
    kx, kg, ki, ko, kb, kf = jax.random.split(key, 6)
    x = jax.random.normal(kx, (BATCH, SEQ, D_MODEL), jnp.float32)
    positions = jnp.arange(SEQ, dtype=jnp.int32)
    norm_gain = 1.0 + 0.02 * jax.random.normal(kg, (DEPTH, D_MODEL), jnp.float32)
    w_in = jax.random.normal(ki, (DEPTH, D_MODEL, IN_WIDTH), jnp.float32) * D_MODEL ** -0.5
    w_out = jax.random.normal(ko, (DEPTH, MIX_WIDTH, D_MODEL), jnp.float32) * MIX_WIDTH ** -0.5
    rel_bias = 0.1 * jax.random.normal(kb, (DEPTH, ATT_HEADS, 2 * REL_CLIP + 1), jnp.float32)
    final_gain = 1.0 + 0.02 * jax.random.normal(kf, (D_MODEL,), jnp.float32)
    return {"x": x, "positions": positions, "norm_gain": norm_gain, "w_in": w_in,
            "w_out": w_out, "rel_bias": rel_bias, "final_gain": final_gain}

def first_block(x, positions, norm_gain, w_in, w_out, rel_bias, final_gain):
    cos, sin = rotary_tables(positions, RET_HEAD_DIM)
    for layer in range(DEPTH):
        x = hybrid_layer(x, norm_gain[layer], w_in[layer], w_out[layer], rel_bias[layer], cos, sin)
    return rms_norm(x, final_gain)


DEPTH_2 = 1

D_MIX = D_MODEL
N_MIXERS = 4
GROUP_W = D_MIX // N_MIXERS
HEAD_DIM = 64
N_HEADS_GROUP = GROUP_W // HEAD_DIM
QK_SCALE = HEAD_DIM ** -0.5
POOL_WINDOWS = (2, 4, 8, 16)
POOL_CH = GROUP_W // len(POOL_WINDOWS)
MAX_WINDOW = 16
RWKV_DECAY_LORA = 64
RWKV_A_LORA = 64
RWKV_GATE_LORA = 128
RWKV_COLS = 3 * GROUP_W + RWKV_DECAY_LORA + RWKV_A_LORA + RWKV_GATE_LORA
RWKV_GN_EPS = 64e-5
GLA_GATE_LORA = 16
GLA_GATE_TAU = 16.0
GLA_COLS = 4 * GROUP_W + GLA_GATE_LORA
D_IN = GROUP_W + 4 * GROUP_W + RWKV_COLS + GLA_COLS
D_FF = 2816
NORM_EPS = 1e-6
GATE_FLOOR = 1e-30


def rms_norm_2(x, g, eps=NORM_EPS):
    xf = x.astype(jnp.float32)
    y = xf * lax.rsqrt(jnp.mean(xf * xf, axis=-1, keepdims=True) + eps)
    return (y * g.astype(jnp.float32)).astype(x.dtype)

def swiglu_ffn(x, w_in, w_out):
    gate, up = jnp.split(x @ w_in, 2, axis=-1)
    return (jax.nn.silu(gate) * up) @ w_out

def split_heads(t):
    return t.reshape(t.shape[:-1] + (N_HEADS_GROUP, HEAD_DIM))

def causal_multiscale_pool(p, w_pool, b_pool, scale):
    B, T, _ = p.shape
    cs = jnp.pad(jnp.cumsum(p, axis=1), ((0, 0), (MAX_WINDOW, 0), (0, 0)))
    pos = jnp.arange(T)
    pooled = []
    for gi, w in enumerate(POOL_WINDOWS):
        lo, hi = gi * POOL_CH, (gi + 1) * POOL_CH
        win_sum = cs[:, MAX_WINDOW:, lo:hi] - cs[:, MAX_WINDOW - w:MAX_WINDOW - w + T, lo:hi]
        count = jnp.minimum(pos + 1, w).astype(jnp.float32)[None, :, None]
        pooled.append(win_sum / count)
    pooled = jnp.stack(pooled, axis=2) - p.reshape(B, T, len(POOL_WINDOWS), POOL_CH)
    y = jnp.einsum('btgc,gcd->btgd', pooled, w_pool).reshape(B, T, GROUP_W) + b_pool
    return y * scale

def chunked_gated_linear_attention(q, k, v, log_a):
    B, T, H, K = q.shape
    V = v.shape[-1]
    n = T // CHUNK

    def to_chunks(t):
        return t.reshape(B, n, CHUNK, H, t.shape[-1]).transpose(1, 0, 3, 2, 4)

    causal = jnp.tril(jnp.ones((CHUNK, CHUNK), dtype=bool))[:, :, None]

    def step(S, inp):
        qc, kc, vc, gc = inp
        b = jnp.cumsum(gc, axis=-2)
        diff = b[:, :, :, None, :] - b[:, :, None, :, :]
        decay = jnp.where(causal, jnp.exp(jnp.where(causal, diff, 0.0)), 0.0)
        scores = jnp.einsum('bhtk,bhsk,bhtsk->bhts', qc, kc, decay)
        o = jnp.einsum('bhts,bhsv->bhtv', scores, vc) + jnp.einsum('bhtk,bhkv->bhtv', qc * jnp.exp(b), S)
        b_last = b[:, :, -1:, :]
        S_new = jnp.exp(b_last[:, :, 0, :])[..., None] * S + jnp.einsum('bhsk,bhsv->bhkv', kc * jnp.exp(b_last - b), vc)
        return S_new, o

    S0 = jnp.zeros((B, H, K, V), jnp.float32)
    _, o = lax.scan(step, S0, (to_chunks(q), to_chunks(k), to_chunks(v), to_chunks(log_a)))
    return o.transpose(1, 0, 3, 2, 4).reshape(B, T, H, V)

def rwkv7_scan(r, w, k, v, kk, a):
    B, T, H, N = r.shape

    def step(S, inp):
        r_t, w_t, k_t, v_t, kk_t, a_t = inp
        s_kk = jnp.einsum('bhvk,bhk->bhv', S, kk_t)
        S = (S * w_t[:, :, None, :] - s_kk[..., None] * (kk_t * a_t)[:, :, None, :]
             + v_t[..., :, None] * k_t[:, :, None, :])
        return S, jnp.einsum('bhvk,bhk->bhv', S, r_t)

    xs = tuple(jnp.moveaxis(t, 1, 0) for t in (r, w, k, v, kk, a))
    S0 = jnp.zeros((B, H, N, N), jnp.float32)
    _, out = lax.scan(step, S0, xs)
    return jnp.moveaxis(out, 0, 1)

def token_mixer(u, w_in, w_out, pool_w, pool_b, pool_scale, lb, hgrn_norm,
                rwkv_mu, rwkv_w0, rwkv_w2, rwkv_a0, rwkv_a2, rwkv_g2, rwkv_k_k, rwkv_k_a,
                rwkv_r_k, rwkv_ln_w, rwkv_ln_b, gla_w2, gla_b, gla_norm):
    B, T, _ = u.shape
    G = GROUP_W
    p = (u @ w_in).astype(jnp.float32)
    p_pool, p_hg, p_rw, p_gla = jnp.split(p, [G, 5 * G, 5 * G + RWKV_COLS], axis=-1)

    y_pool = causal_multiscale_pool(p_pool, pool_w, pool_b, pool_scale)

    hq, hf, hi, hg = jnp.split(p_hg, 4, axis=-1)
    f = lb + (1.0 - lb) * jax.nn.sigmoid(hf)
    log_f = jnp.log(jnp.maximum(f, GATE_FLOOR))
    o_h = chunked_gated_linear_attention(split_heads(jax.nn.silu(hq) * QK_SCALE),
                                         split_heads(1.0 - f),
                                         split_heads(hi), split_heads(log_f)).reshape(B, T, G)
    y_hgrn = rms_norm_2(o_h, hgrn_norm) * jax.nn.sigmoid(hg)

    prev = jnp.pad(p_rw, ((0, 0), (1, 0), (0, 0)))[:, :T]
    p_rw = p_rw + (prev - p_rw) * rwkv_mu
    rr, rk, rv, xw, xa, xg = jnp.split(
        p_rw, [G, 2 * G, 3 * G, 3 * G + RWKV_DECAY_LORA, 3 * G + RWKV_DECAY_LORA + RWKV_A_LORA], axis=-1)
    w_log = -jax.nn.softplus(-(rwkv_w0 + jnp.tanh(xw) @ rwkv_w2)) - 0.5
    decay = jnp.exp(-jnp.exp(w_log))
    a = jax.nn.sigmoid(rwkv_a0 + xa @ rwkv_a2)
    g_r = jax.nn.sigmoid(xg) @ rwkv_g2
    kk = split_heads(rk * rwkv_k_k)
    kk = kk / jnp.maximum(jnp.sqrt(jnp.sum(kk * kk, axis=-1, keepdims=True)), 1e-12)
    rk = rk * (1.0 + (a - 1.0) * rwkv_k_a)
    r_h, k_h, v_h = split_heads(rr), split_heads(rk), split_heads(rv)
    o_r = rwkv7_scan(r_h, split_heads(decay), k_h, v_h, kk, split_heads(a))
    mu = jnp.mean(o_r, axis=-1, keepdims=True)
    var = jnp.mean(jnp.square(o_r - mu), axis=-1, keepdims=True)
    gn = ((o_r - mu) * lax.rsqrt(var + RWKV_GN_EPS)).reshape(B, T, G) * rwkv_ln_w + rwkv_ln_b
    bonus = (jnp.sum(r_h * k_h * split_heads(rwkv_r_k), axis=-1, keepdims=True) * v_h).reshape(B, T, G)
    y_rwkv = (gn + bonus) * g_r

    gq, gk, gv, gg, ga = jnp.split(p_gla, [G, 2 * G, 3 * G, 4 * G], axis=-1)
    log_a = jax.nn.log_sigmoid(ga @ gla_w2 + gla_b) / GLA_GATE_TAU
    o_g = chunked_gated_linear_attention(split_heads(gq * QK_SCALE), split_heads(gk),
                                         split_heads(gv), split_heads(log_a))
    o_g = (o_g * lax.rsqrt(jnp.mean(o_g * o_g, axis=-1, keepdims=True) + NORM_EPS)).reshape(B, T, G)
    y_gla = o_g * gla_norm * jax.nn.silu(gg)

    y = jnp.concatenate([y_pool, y_hgrn, y_rwkv, y_gla], axis=-1).astype(u.dtype)
    return y @ w_out

def second_inputs(seed: int = 0) -> dict:
    key = jax.random.key(seed)
    ks = jax.random.split(key, 32)
    f32 = jnp.float32
    L, D, G = DEPTH_2, D_MODEL, GROUP_W

    def dense(k, shape, fan_in):
        return jax.random.normal(k, shape, f32) * fan_in ** -0.5

    def gain(k, shape):
        return 1.0 + 0.1 * jax.random.normal(k, shape, f32)

    def small(k, shape, s):
        return s * jax.random.normal(k, shape, f32)

    return {
        'x': jax.random.normal(ks[0], (BATCH, SEQ, D), f32),
        'norm_ffn1': gain(ks[1], (L, D)),
        'ffn1_w_in': dense(ks[2], (L, D, 2 * D_FF), D),
        'ffn1_w_out': dense(ks[3], (L, D_FF, D), D_FF),
        'norm_mix': gain(ks[4], (L, D)),
        'w_in': dense(ks[5], (L, D, D_IN), D),
        'w_out': dense(ks[6], (L, D_MIX, D), D_MIX),
        'pool_w': dense(ks[7], (L, len(POOL_WINDOWS), POOL_CH, POOL_CH), POOL_CH),
        'pool_b': small(ks[8], (L, G), 0.01),
        'pool_scale': gain(ks[9], (L, G)),
        'hgrn_lb_logits': small(ks[10], (L, G), 0.5),
        'hgrn_norm': gain(ks[11], (L, G)),
        'rwkv_mu': jax.random.uniform(ks[12], (L, RWKV_COLS), f32),
        'rwkv_w0': jax.random.uniform(ks[13], (L, G), f32, -4.0, 0.0),
        'rwkv_w2': dense(ks[14], (L, RWKV_DECAY_LORA, G), RWKV_DECAY_LORA),
        'rwkv_a0': small(ks[15], (L, G), 0.5),
        'rwkv_a2': dense(ks[16], (L, RWKV_A_LORA, G), RWKV_A_LORA),
        'rwkv_g2': dense(ks[17], (L, RWKV_GATE_LORA, G), RWKV_GATE_LORA),
        'rwkv_k_k': 0.85 + small(ks[18], (L, G), 0.1),
        'rwkv_k_a': gain(ks[19], (L, G)),
        'rwkv_r_k': small(ks[20], (L, G), 0.1),
        'rwkv_ln_w': gain(ks[21], (L, G)),
        'rwkv_ln_b': small(ks[22], (L, G), 0.01),
        'gla_w2': dense(ks[23], (L, GLA_GATE_LORA, G), GLA_GATE_LORA),
        'gla_b': small(ks[24], (L, G), 0.5),
        'gla_norm': gain(ks[25], (L, G)),
        'norm_ffn2': gain(ks[26], (L, D)),
        'ffn2_w_in': dense(ks[27], (L, D, 2 * D_FF), D),
        'ffn2_w_out': dense(ks[28], (L, D_FF, D), D_FF),
        'norm_final': gain(ks[29], (D,)),
    }

def second_block(x, norm_ffn1, ffn1_w_in, ffn1_w_out, norm_mix, w_in, w_out, pool_w, pool_b,
              pool_scale, hgrn_lb_logits, hgrn_norm, rwkv_mu, rwkv_w0, rwkv_w2, rwkv_a0, rwkv_a2,
              rwkv_g2, rwkv_k_k, rwkv_k_a, rwkv_r_k, rwkv_ln_w, rwkv_ln_b, gla_w2, gla_b, gla_norm,
              norm_ffn2, ffn2_w_in, ffn2_w_out, norm_final):
    sm = jax.nn.softmax(hgrn_lb_logits.astype(jnp.float32), axis=0)
    lower_bounds = jnp.cumsum(sm, axis=0) - sm[0]
    for l in range(DEPTH_2):
        x = x + 0.5 * swiglu_ffn(rms_norm_2(x, norm_ffn1[l]), ffn1_w_in[l], ffn1_w_out[l])
        x = x + token_mixer(rms_norm_2(x, norm_mix[l]), w_in[l], w_out[l], pool_w[l], pool_b[l],
                            pool_scale[l], lower_bounds[l], hgrn_norm[l], rwkv_mu[l], rwkv_w0[l],
                            rwkv_w2[l], rwkv_a0[l], rwkv_a2[l], rwkv_g2[l], rwkv_k_k[l], rwkv_k_a[l],
                            rwkv_r_k[l], rwkv_ln_w[l], rwkv_ln_b[l], gla_w2[l], gla_b[l], gla_norm[l])
        x = x + 0.5 * swiglu_ffn(rms_norm_2(x, norm_ffn2[l]), ffn2_w_in[l], ffn2_w_out[l])
    return rms_norm_2(x, norm_final)


def setup_inputs(seed=0):
    out = dict(first_inputs(seed))
    for name, value in second_inputs(seed + 1).items():
        if name != "x":
            out[name + "_2"] = value
    return out


def reference(
    x, positions, norm_gain, w_in, w_out, rel_bias, final_gain, norm_ffn1_2, ffn1_w_in_2,
    ffn1_w_out_2, norm_mix_2, w_in_2, w_out_2, pool_w_2, pool_b_2, pool_scale_2,
    hgrn_lb_logits_2, hgrn_norm_2, rwkv_mu_2, rwkv_w0_2, rwkv_w2_2, rwkv_a0_2, rwkv_a2_2,
    rwkv_g2_2, rwkv_k_k_2, rwkv_k_a_2, rwkv_r_k_2, rwkv_ln_w_2, rwkv_ln_b_2, gla_w2_2, gla_b_2,
    gla_norm_2, norm_ffn2_2, ffn2_w_in_2, ffn2_w_out_2, norm_final_2,
):
    x = first_block(
        x, positions, norm_gain, w_in, w_out, rel_bias, final_gain,
    )
    return second_block(
        x, norm_ffn1_2, ffn1_w_in_2, ffn1_w_out_2, norm_mix_2, w_in_2, w_out_2, pool_w_2,
        pool_b_2, pool_scale_2, hgrn_lb_logits_2, hgrn_norm_2, rwkv_mu_2, rwkv_w0_2, rwkv_w2_2,
        rwkv_a0_2, rwkv_a2_2, rwkv_g2_2, rwkv_k_k_2, rwkv_k_a_2, rwkv_r_k_2, rwkv_ln_w_2,
        rwkv_ln_b_2, gla_w2_2, gla_b_2, gla_norm_2, norm_ffn2_2, ffn2_w_in_2, ffn2_w_out_2,
        norm_final_2,
    )


_drawn_inputs = setup_inputs


def setup_inputs(seed=0):
    import zlib

    import numpy as np

    out = dict(_drawn_inputs(seed))
    spreads = {}
    factors = {'rel_bias': 6.771,
     'pool_b_2': 8.0,
     'rwkv_w2_2': 2.879,
     'rwkv_k_k_2': 15.825,
     'rwkv_ln_w_2': 2.683,
     'rwkv_ln_b_2': 29.314}
    for name, (base, spread) in spreads.items():
        noise = np.random.default_rng([zlib.crc32(name.encode()), seed]).standard_normal(out[name].shape)
        drawn = base * np.exp(spread * noise) if base else spread * noise
        out[name] = __import__('jax').numpy.asarray(drawn.astype(out[name].dtype))
    for name, factor in factors.items():
        out[name] = (out[name] * factor).astype(out[name].dtype)
    return out
```

```python
import math
from contextlib import ExitStack

import concourse.bass as bass
import numpy as np
from concourse import mybir

F32 = mybir.dt.float32
I32 = mybir.dt.int32
ALU = mybir.AluOpType
ACT = mybir.ActivationFunctionType
AX_X = mybir.AxisListType.X

P = 128
SEQ = 512
D = 1024
KT = D // P
TT = SEQ // P
CHUNK = 64
CLIP = 256
ATT_HEADS, ATT_DIM = 8, 64
RET_HEADS, RET_DIM = 4, 128
EPS = 1e-6
GN_EPS = 64e-5
NEG_INF = -1e30
D_FF = 2816
FT = D_FF // P
G = 256
UNIT = 1024
RING = 8
BANKS = 8
LEVELS = (64, 32, 16, 8, 4, 2, 1)
HALF_E = math.exp(-0.5)
ROUND = 12582912.0

COLS = {}
for _name, _n in (("gain0", 8), ("gain1", 8), ("final_gain", 8), ("norm_ffn1", 8), ("norm_mix", 8),
                  ("norm_ffn2", 8), ("norm_final", 8), ("pool_b", 2), ("pool_scale", 2),
                  ("rwkv_mu", 8), ("rwkv_w0", 2), ("rwkv_a0", 2), ("rwkv_k_k", 2), ("rwkv_k_a", 2),
                  ("rwkv_r_k", 2), ("gla_b", 2), ("lb_logits", 2)):
    COLS[_name] = (sum(n for _, n in COLS.values()), _n)
N_COLS = sum(n for _, n in COLS.values())

SHARED = {"ident": (0, 128), "inv_freq": (128, 64)}
N_SHARED = 192
MIXER = {"same_head": (0, 128), "before": (128, 128), "upto": (256, 128), "pairs": (384, 7 * 128),
         "pairs_ts": (384 + 896, 128), "restart": (1408, 512), "inv_count": (1920, 1024)}
N_MIXER = 1920


class Queue:

    def __init__(self, sem, chained=False):
        self.sem, self.count, self.steps, self.waited = sem, 0, [], {}
        self.chained = chained

    def wait(self, *tokens):
        for token in tokens:
            if token is None:
                continue
            sem, value = token
            if value > self.waited.get(sem, 0):
                self.waited[sem] = value
                self.steps.append(lambda eng, s=sem, v=value: eng.wait_ge(s, v))

    def do(self, emit, *tokens):
        self.wait(*tokens)
        if self.chained:
            self.wait(self.now())
        self.count += 1
        self.steps.append(lambda eng: emit(eng).then_inc(self.sem, 1))
        return (self.sem, self.count)

    def quiet(self, emit, *tokens):
        self.wait(*tokens)
        self.steps.append(emit)

    def dma(self, emit, sem, value, *tokens):
        self.wait(*tokens)
        self.steps.append(lambda eng: emit(eng).then_inc(sem, 16))
        return (sem, value)

    def now(self):
        return (self.sem, self.count) if self.count else None

    def run(self, eng):
        for step in self.steps:
            step(eng)


def build(nc, t):
    with ExitStack() as ctx:
        def sbuf(name, shape, dt=F32):
            return ctx.enter_context(nc.sbuf_tensor(f"sb_{name}", shape, dt))

        def sem(name):
            return ctx.enter_context(nc.semaphore(name))

        pe, dve, act, pool, sp = (Queue(sem(f"done_{n}"), n in ("dve", "act", "pool")) for n in ("pe", "dve", "act", "pool", "sp"))

        x = sbuf("x", [P, KT, SEQ])
        xg = sbuf("xg", [P, KT, SEQ])
        yT = sbuf("yT", [P, KT, SEQ])
        ring = sbuf("ring", [P, RING, UNIT])
        cols = sbuf("cols", [P, N_COLS])
        shared = sbuf("shared", [P, N_SHARED])
        ones = sbuf("ones", [P, P])
        mean_ones = sbuf("mean_ones", [P, P])
        square = sbuf("square", [P, 2, SEQ])
        inv_rms = sbuf("inv_rms", [P, SEQ])
        inv_rms_t = sbuf("inv_rms_t", [P, TT])
        small = sbuf("small", [P, 256])
        arena_cols = 28416
        arena = sbuf("arena", [P, arena_cols])
        banks = [ctx.enter_context(nc.psum_tensor(f"bank{i}", [P, 512], F32)) for i in range(BANKS)]

        def col(name, i, rows=slice(0, P)):
            at = COLS[name][0] + i
            return cols[rows, at:at + 1]

        ident = shared[:, 0:128]

        bank_free = [[] for _ in range(BANKS)]
        turn = [0]
        held = set()

        def take():
            while True:
                i = turn[0] % BANKS
                turn[0] += 1
                if i not in held:
                    return i

        def psum_group(i, out, pairs, *tokens):
            pe.wait(*bank_free[i])
            pe.wait(*tokens)
            for n, (lhsT, rhs) in enumerate(pairs):
                first, last = n == 0, n == len(pairs) - 1
                emit = (lambda e, o=out, l=lhsT, r=rhs, f=first, z=last:
                        e.matmul(o, l, r, start=f, stop=z))
                if last:
                    return pe.do(emit)
                pe.quiet(emit)

        def transposes(i, blocks, *tokens):
            pe.wait(*bank_free[i])
            pe.wait(*tokens)
            for n, (out, in_) in enumerate(blocks):
                emit = lambda e, o=out, a=in_: e.transpose(o, a, ident)
                if n == len(blocks) - 1:
                    return pe.do(emit)
                pe.quiet(emit)

        slot_sem = [sem(f"weights_{i}") for i in range(RING)]
        slot_free = [None] * RING
        units = [0]

        def weights(dram):
            i, n = units[0] % RING, units[0] // RING + 1
            units[0] += 1
            width = dram.shape[-1]
            dst = ring[:, i, 0:width]
            token = sp.dma(lambda e: e.dma_start(dst, dram), slot_sem[i], 16 * n, slot_free[i])
            return i, dst, token

        def feature_major(units_of, k_tiles, rhs, *tokens, m=P):
            i, k = take(), 0
            pe.wait(*bank_free[i])
            pe.wait(*tokens)
            for dram in units_of:
                slot, w, loaded = weights(dram)
                pe.wait(loaded)
                n_here = w.shape[-1] // m
                for j in range(n_here):
                    emit = (lambda e, o=banks[i][0:m, :], l=w[:, j * m:(j + 1) * m], r=rhs(k),
                            f=(k == 0), z=(k == k_tiles - 1): e.matmul(o, l, r, start=f, stop=z))
                    k += 1
                    if j == n_here - 1:
                        slot_free[slot] = pe.do(emit)
                    else:
                        pe.quiet(emit)
            return i, slot_free[slot]

        def token_major(units_of, *tokens):
            out = [take() for _ in range(TT)]
            for i in out:
                pe.wait(*bank_free[i])
            pe.wait(*tokens)
            done, k = None, 0
            for dram in units_of:
                slot, w, loaded = weights(dram)
                pe.wait(loaded)
                for j in range(2):
                    for tile, i in enumerate(out):
                        emit = (lambda e, o=banks[i][:, :], l=xg[:, k, tile * P:(tile + 1) * P],
                                r=w[:, j * 512:(j + 1) * 512], f=(k == 0), z=(k == KT - 1):
                                e.matmul(o, l, r, start=f, stop=z))
                        done = pe.do(emit) if j == 1 and tile == TT - 1 else pe.quiet(emit)
                    k += 1
                slot_free[slot] = done
            return out, done

        arena_at = [0]

        def phase():
            arena_at[0] = 0
            ends = [q.now() for q in (pe, dve, act, pool)]
            for q in (dve, act, pool):
                q.wait(*ends)

        def room(*shape):
            n = int(np.prod(shape))
            at = arena_at[0]
            arena_at[0] += n
            assert arena_at[0] <= arena_cols, (arena_at[0], arena_cols)
            ap = arena[:, at:at + n]
            if len(shape) == 2:
                return ap.rearrange("p (a b) -> p a b", b=shape[1])
            if len(shape) == 3:
                return ap.rearrange("p (a b c) -> p a b c", b=shape[1], c=shape[2])
            return ap

        def copy_act(out, in_, *tokens, func=ACT.Identity, scale=1.0, bias=0.0, accum=None):
            return act.do(lambda e: e.activation(out, in_, func, bias=bias, scale=scale,
                                                 accum_out=accum), *tokens)

        def tt(q, out, a, b, op, *tokens):
            return q.do(lambda e: e.tensor_tensor(out, a, b, op), *tokens)

        def ts(q, out, a, s1, s2, op0, op1, *tokens):
            return q.do(lambda e: e.tensor_scalar(out, a, s1, s2, op0, op1), *tokens)

        def stt(out, a, s, b, op0, op1, *tokens):
            return dve.do(lambda e: e.scalar_tensor_tensor(out=out, in0=a, scalar=s, in1=b, op0=op0,
                                                           op1=op1), *tokens)

        def recip(out, in_, *tokens):
            return dve.do(lambda e: e.reciprocal(out, in_), *tokens)

        fixed_sem = sem("fixed_loads")
        x_sem = [sem(f"x_load_{i}") for i in range(2)]
        for i in range(2):
            src, half = t["xT"][:, 4 * i:4 * i + 4, :], x[:, 4 * i:4 * i + 4, :]
            act.dma(lambda e, s=src, h=half: e.dma_start(h, s), x_sem[i], 16)
        x_loaded = [(x_sem[i], 16) for i in range(2)]
        positions = sbuf("positions", [P, TT], I32)
        fixed = [(cols, t["cols"]), (shared, t["shared"]), (positions, t["positions"])]
        for out, src in fixed:
            pool.dma(lambda e, o=out, s=src: e.dma_start(o[:, :], s), fixed_sem, 0)
        fixed_done = (fixed_sem, 16 * len(fixed))
        ones_set = dve.do(lambda e: e.memset(ones[:, :], 1.0))
        mean_set = dve.do(lambda e: e.memset(mean_ones[:, :], 1.0 / D))
        for q in (pe, dve, act, pool):
            q.wait(fixed_done)
        pe.wait(ones_set, mean_set)

        square_free = [None, None]
        norm_bank = [None]

        def start_norm():
            norm_bank[0] = take()
            held.add(norm_bank[0])

        def square_in(f, *tokens):
            return copy_act(square[:, f % 2, :], x[:, f, :], *tokens, square_free[f % 2],
                            func=ACT.Square)

        def add_square(f, squared):
            b = norm_bank[0]
            if f == 0:
                pe.wait(*bank_free[b])
            square_free[f % 2] = pe.do(
                lambda e: e.matmul(banks[b][:, :], mean_ones[:, :], square[:, f % 2, :],
                                   start=(f == 0), stop=(f == KT - 1)), squared)

        rms_free = [None]

        def finish_norm(token_side):
            b = norm_bank[0]
            root = copy_act(inv_rms[:, :], banks[b][:, :], square_free[(KT - 1) % 2], dve.now(),
                            rms_free[0], func=ACT.Sqrt, bias=EPS)
            bank_free[b] = [root]
            held.discard(b)
            done = recip(inv_rms[:, :], inv_rms[:, :], root)
            if not token_side:
                return done, None
            i = take()
            pe.wait(*bank_free[i])
            for tile in range(TT):
                turned = pe.do(lambda e, tile=tile: e.matmul(
                    banks[i][:, tile:tile + 1], inv_rms[0:1, tile * P:(tile + 1) * P], ones[0:1, 0:1],
                    start=True, stop=True), done)
            side = copy_act(inv_rms_t[:, :], banks[i][:, 0:TT], turned, act.now())
            bank_free[i] = [side]
            return done, side

        def gained(f, gain, *tokens):
            return copy_act(xg[:, f, :], x[:, f, :], *tokens, scale=col(gain, f))

        def first_norm(gain):
            start_norm()
            xg_done = None
            for f in range(KT):
                squared = square_in(f, x_loaded[f // 4])
                xg_done = gained(f, gain)
                add_square(f, squared)
            return xg_done

        def apply_norm(gain, write, rms_done):
            for f in range(KT):
                write(f, stt(x[:, f, :], x[:, f, :], col(gain, f), inv_rms[:, :], ALU.mult, ALU.mult,
                             rms_done))

        def output_product(unit_of, rhs, k_tiles, factor, next_gain, *tokens):
            pending = None
            start_norm()
            xg_done = None
            for f in range(KT):
                i, done = feature_major(unit_of(f), k_tiles, rhs, *tokens)
                if pending:
                    add_square(*pending)
                added = stt(x[:, f, :], banks[i][:, :], factor, x[:, f, :], ALU.mult, ALU.add, done)
                bank_free[i] = [added]
                pending = (f, square_in(f, added))
                if next_gain:
                    xg_done = gained(f, next_gain, added, pe_used_xg[0])
            add_square(*pending)
            return xg_done

        pe_used_xg = [None]

        cos2 = sbuf("cos2", [P, TT, P])
        sin2 = sbuf("sin2", [P, TT, P])
        pos_f = small[:, 0:TT]
        TWO_PI = 2 * math.pi
        part1 = 6.28125
        part2 = round((TWO_PI - part1) * 2 ** 21) / 2 ** 21
        part3 = TWO_PI - part1 - part2
        ready = dve.do(lambda e: e.tensor_copy(pos_f, positions[:, :]))
        angle = arena[:, 0:TT * 64].rearrange("p (a b) -> p a b", b=64)
        turns = arena[:, 256:512].rearrange("p (a b) -> p a b", b=64)
        for tile in range(TT):
            made = ts(dve, angle[:, tile, :], shared[:, 128:192], pos_f[:, tile:tile + 1], None,
                      ALU.mult, ALU.bypass, ready)
        made = ts(dve, turns, angle, 1.0 / TWO_PI, ROUND, ALU.mult, ALU.add, made)
        made = ts(dve, turns, turns, ROUND, None, ALU.subtract, ALU.bypass, made)
        for part in (part1, part2, part3):
            made = stt(angle, turns, -part, angle, ALU.mult, ALU.add, made)
        made = ts(dve, angle, angle, math.pi * (1 - 1e-7), -math.pi * (1 - 1e-7), ALU.min, ALU.max, made)
        sin_plus = copy_act(sin2[:, :, 64:128], angle, made, func=ACT.Sin)
        sin_minus = copy_act(sin2[:, :, 0:64], angle, func=ACT.Sin, scale=-1.0)
        absolute = copy_act(turns, angle, made, func=ACT.Abs)
        cos_a = copy_act(cos2[:, :, 0:64], turns, absolute, func=ACT.Sin, scale=-1.0, bias=math.pi / 2)
        rotary = copy_act(cos2[:, :, 64:128], turns, absolute, func=ACT.Sin, scale=-1.0,
                          bias=math.pi / 2)

        strip_sem, decay_sem = [sem(f"strips_{i}") for i in range(2)], sem("decays")
        xg_ready = first_norm("gain0")

        def layer(n, xg_ready, next_gain):
            phase()
            qT = room(4, SEQ)
            kT = room(4, SEQ)
            tok = {name: room(TT, 512) for name in ("av", "ag", "rq", "rk", "rv", "rg")}
            strips = room(4, SEQ)
            prob = room(2, SEQ)
            probT = room(2, SEQ)
            att = room(1280)
            rot = room(3, SEQ)
            decays = room(RET_HEADS, SEQ)
            decays_in = pool.dma(lambda e: e.dma_start(decays, t["decays"]), decay_sem, 16 * (n + 1))

            def load_strips(half, *tokens):
                loaded = pool.dma(lambda e: e.dma_start(strips, t["strips"][n, half]),
                                  strip_sem[half], 16 * (n + 1), *tokens)
                return pool.do(lambda e: e.memset(strips[0:64, :, 448:512], NEG_INF), loaded)

            strips_in = [load_strips(0), None]

            rms_done = side = None
            qk_done = None
            for f in range(8):
                i, done = feature_major([t["w_qk"][n, f]], KT, lambda k: xg[:, k, :], xg_ready)
                if f == 0:
                    rms_done, side = finish_norm(True)
                out = qT[:, f, :] if f < 4 else kT[:, f - 4, :]
                qk_done = stt(out, banks[i][:, :], ATT_DIM ** -0.5 if f < 4 else 1.0, inv_rms[:, :],
                              ALU.mult, ALU.mult, done, rms_done)
                bank_free[i] = [qk_done]

            landed = {}
            for g, name in enumerate(("rq", "rk", "av", "ag", "rv", "rg")):
                out, done = token_major([t["w_tok"][n, g, u] for u in range(4)])
                for tile, i in enumerate(out):
                    landed[name] = copy_act(tok[name][:, tile, :], banks[i][:, :], done, side,
                                            func=ACT.Silu if name in ("ag", "rg") else ACT.Identity,
                                            scale=inv_rms_t[:, tile:tile + 1])
                    bank_free[i] = [landed[name]]
            pe_used_xg[0] = pe.now()

            turned = {}
            rot_free = [None]
            for name in ("rq", "rk"):
                for tile in range(TT):
                    src = tok[name][:, tile, :].rearrange("p (h d) -> p h d", d=P)
                    a, b, r = (rot[:, s, :].rearrange("p (h d) -> p h d", d=P) for s in range(3))
                    c = cos2[:, tile, :].unsqueeze(1).to_broadcast([P, 4, P])
                    s_lo = sin2[:, tile, 0:64].unsqueeze(1).to_broadcast([P, 4, 64])
                    s_hi = sin2[:, tile, 64:128].unsqueeze(1).to_broadcast([P, 4, 64])
                    m0 = tt(dve, a, src, c, ALU.mult, landed[name], rotary)
                    tt(dve, b[:, :, 0:64], src[:, :, 64:128], s_lo, ALU.mult)
                    m1 = tt(dve, b[:, :, 64:128], src[:, :, 0:64], s_hi, ALU.mult)
                    m2 = tt(dve, r, a, b, ALU.add, m1, rot_free[0])
                    i = take()
                    rot_free[0] = transposes(
                        i, [(banks[i][:, h * P:(h + 1) * P], rot[:, 2, h * P:(h + 1) * P])
                            for h in range(4)], m2)
                    turned[name] = copy_act(tok[name][:, tile, :], banks[i][:, :], rot_free[0], m2)
                    bank_free[i] = [turned[name]]

            steps = [(h, q) for h in range(ATT_HEADS) for q in range(TT)]
            state = {}

            def scores(h, q):
                r = slice(64 * (h % 2), 64 * (h % 2) + 64)
                i = take()
                keys = (q + 1) * P
                done = psum_group(i, banks[i][:, 0:keys],
                                  [(qT[r, h // 2, q * P:(q + 1) * P], kT[r, h // 2, 0:keys])], qk_done)
                if (h, q) == (4, 0):
                    strips_in[1] = load_strips(1, state[(3, 3)]["biased"])
                s = state[(h, q)] = {}
                buf = (h * TT + q) % 2
                stat = 8 + 4 * ((h * TT + q) % 4)
                s["p"], s["stat"] = prob[:, buf, 0:keys], stat
                before = state.get(prev(h, q, 2))
                s["biased"] = dve.do(lambda e: e.tensor_tensor_reduce(
                    out=s["p"], in0=banks[i][:, 0:keys], in1=strips[:, h % 4, 512 - keys:512],
                    scale=1.0, scalar=-3e38, op0=ALU.add, op1=ALU.max,
                    accum_out=small[:, stat:stat + 1]), done, strips_in[h // 4],
                    before and before["turned"])
                bank_free[i] = [s["biased"]]
                minus = ts(dve, small[:, stat + 1:stat + 2], small[:, stat:stat + 1], -1.0, None,
                           ALU.mult, ALU.bypass, s["biased"])
                s["exp"] = copy_act(s["p"], s["p"], minus, func=ACT.Exp,
                                    bias=small[:, stat + 1:stat + 2], accum=small[:, stat + 2:stat + 3])

            def prev(h, q, n):
                k = h * TT + q - n
                return (k // TT, k % TT)

            def turn_probs(h, q):
                s = state[(h, q)]
                i = take()
                s["turned"] = transposes(i, [(banks[i][:, k * P:(k + 1) * P],
                                              s["p"][:, k * P:(k + 1) * P]) for k in range(q + 1)],
                                         s["exp"])
                before = state.get(prev(h, q, 2))
                s["buf"] = probT[:, (h * TT + q) % 2, :]
                s["probT"] = copy_act(s["buf"][:, 0:(q + 1) * P], banks[i][:, 0:(q + 1) * P],
                                      s["turned"], before and before["used"])
                bank_free[i] = [s["probT"]]
                s["inv"] = recip(small[:, s["stat"] + 3:s["stat"] + 4],
                                 small[:, s["stat"] + 2:s["stat"] + 3], s["exp"])

            def values(h, q):
                s = state[(h, q)]
                i = take()
                s["used"] = psum_group(i, banks[i][:, 0:ATT_DIM],
                                       [(s["buf"][:, k * P:(k + 1) * P],
                                         tok["av"][:, k, h * ATT_DIM:(h + 1) * ATT_DIM])
                                        for k in range(q + 1)], s["probT"], landed["av"])
                gate = tok["ag"][:, q, h * ATT_DIM:(h + 1) * ATT_DIM]
                s["out"] = stt(gate, banks[i][:, 0:ATT_DIM], small[:, s["stat"] + 3:s["stat"] + 4], gate,
                               ALU.mult, ALU.mult, s["used"], s["inv"], landed["ag"])
                bank_free[i] = [s["out"]]

            for n_step in range(len(steps) + 2):
                if n_step < len(steps):
                    scores(*steps[n_step])
                if 1 <= n_step <= len(steps):
                    turn_probs(*steps[n_step - 1])
                if n_step >= 2:
                    values(*steps[n_step - 2])
            att_out = state[steps[-1]]["out"]

            offs = [0, 512, 896, 1152]
            att_free = None
            for h in range(RET_HEADS):
                for j in range(TT):
                    width = (TT - j) * P
                    i = take()
                    kh = tok["rk"][:, j, h * P:(h + 1) * P]
                    qh = tok["rq"][:, j:TT, h * P:(h + 1) * P]
                    done = psum_group(i, banks[i][:, 0:width].rearrange("p (a b) -> p a b", b=P),
                                      [(kh, qh)], turned["rk"], turned["rq"])
                    weighted = tt(dve, att[:, offs[j]:offs[j] + width], banks[i][:, 0:width],
                                  decays[:, h, 0:width], ALU.mult, done, decays_in, att_free)
                    bank_free[i] = [weighted]
                i = take()
                held.add(i)
                for q in range(TT):
                    done = psum_group(i, banks[i][:, q * P:(q + 1) * P],
                                      [(att[:, offs[j] + (q - j) * P:offs[j] + (q - j + 1) * P],
                                        tok["rv"][:, j, h * P:(h + 1) * P]) for j in range(q + 1)],
                                      weighted, landed["rv"])
                att_free = done
                stat = 32 + 12 * h
                ss, root, inv = (small[:, stat + 4 * k:stat + 4 * k + 4] for k in range(3))
                for q in range(TT):
                    summed = copy_act(rot[:, 0, q * P:(q + 1) * P], banks[i][:, q * P:(q + 1) * P],
                                      done, rot_free[0], func=ACT.Square, accum=ss[:, q:q + 1])
                rooted = copy_act(root, ss, summed, func=ACT.Sqrt, scale=1.0 / RET_DIM, bias=EPS)
                inverted = recip(inv, root, rooted)
                for q in range(TT):
                    gate = tok["rg"][:, q, h * P:(h + 1) * P]
                    ret_out = stt(gate, banks[i][:, q * P:(q + 1) * P], inv[:, q:q + 1], gate, ALU.mult,
                                  ALU.mult, inverted, landed["rg"])
                bank_free[i] = [ret_out]
                held.discard(i)

            for half, (name, made) in enumerate((("ag", att_out), ("rg", ret_out))):
                for tile in range(TT):
                    i = take()
                    done = transposes(i, [(banks[i][:, f * P:(f + 1) * P],
                                           tok[name][:, tile, f * P:(f + 1) * P]) for f in range(4)], made)
                    y_done = copy_act(yT[:, 4 * half:4 * half + 4, tile * P:(tile + 1) * P],
                                      banks[i][:, :].rearrange("p (f c) -> p f c", c=P), done)
                    bank_free[i] = [y_done]
            rms_free[0] = dve.now()
            return output_product(lambda f: [t["w_out"][n, f]], lambda k: yT[:, k, :], KT, 1.0,
                                  next_gain, y_done)

        xg_ready = layer(0, xg_ready, "gain1")
        layer(1, xg_ready, None)

        rms_done, _ = finish_norm(False)
        made = {}
        apply_norm("final_gain", lambda f, token: made.__setitem__(f, token), rms_done)
        rms_free[0] = dve.now()

        def norm_of_stream(gain):
            start_norm()
            last = None
            for f in range(KT):
                squared = square_in(f, made[f])
                last = gained(f, gain, pe_used_xg[0])
                add_square(f, squared)
            return last

        xg_ready = norm_of_stream("norm_ffn1")

        def feed_forward(which, xg_ready, next_gain):
            phase()
            hidden = room(FT, SEQ)
            gate = room(2, SEQ)
            up = room(2, SEQ)
            rms_done = None
            for f in range(FT):
                b = f % 2
                ig, gate_done = feature_major([t["w_ffn_in"][which, 2 * f]], KT, lambda k: xg[:, k, :],
                                              xg_ready)
                if f == 0:
                    rms_done, _ = finish_norm(False)
                iu, up_done = feature_major([t["w_ffn_in"][which, 2 * f + 1]], KT,
                                            lambda k: xg[:, k, :])
                gated = tt(dve, gate[:, b, :], banks[ig][:, :], inv_rms[:, :], ALU.mult, gate_done,
                           rms_done)
                bank_free[ig] = [gated]
                silu = copy_act(gate[:, b, :], gate[:, b, :], gated, func=ACT.Silu)
                upped = tt(dve, up[:, b, :], banks[iu][:, :], inv_rms[:, :], ALU.mult, up_done)
                bank_free[iu] = [upped]
                h_done = tt(dve, hidden[:, f, :], gate[:, b, :], up[:, b, :], ALU.mult, silu, upped)
            pe_used_xg[0] = pe.now()
            rms_free[0] = dve.now()
            w = t["w_ffn_out"]
            return output_product(
                lambda f: [w[which, f][:, a:b] for a, b in ((0, 1024), (1024, 2048), (2048, D_FF))],
                lambda k: hidden[:, k, :], FT, 0.5, next_gain, h_done)

        def fence():
            ends = [q.now() for q in (pe, dve, act, pool)]
            for q in (dve, act, pool):
                q.wait(*ends)

        def over_tiles(ap, n=TT):
            return ap.unsqueeze(1).to_broadcast([P, n, ap.shape[-1]])

        def mixers(xg_ready):
            phase()
            mixer = room(N_MIXER)
            rows = room(4, G)
            lora = room(2, G)
            gla_w2 = room(G)
            pool_w = room(2, 64)
            mixer_sem = sem("mixer_loads")
            loads = [(mixer, t["mixer"]), (rows, t["rows"]), (lora, t["lora"]),
                     (gla_w2[0:16, :], t["gla_w2"]), (pool_w, t["pool_w"])]
            for out, src in loads:
                pool.dma(lambda e, o=out, s=src: e.dma_start(o, s), mixer_sem, 0)
            mixer_in = (mixer_sem, 16 * len(loads))
            for q in (pe, dve, act, pool):
                q.wait(mixer_in)

            def table(name):
                at, n = MIXER[name]
                return mixer[:, at:at + n]

            start = arena_at[0]
            same_head = table("same_head")
            norms = []

            def projected(unit, f, m=P):
                i, done = feature_major([unit], KT, lambda k: xg[:, k, :], xg_ready, m=m)
                if not norms:
                    norms.extend(finish_norm(True))
                return i, done

            pad = 16
            p_in, s2, s4 = room(2, SEQ + pad), room(2, SEQ + pad), room(2, SEQ + pad)
            s8, s16 = room(SEQ + pad), room(SEQ + pad)
            window, inv_count = room(2, SEQ), room(2, SEQ)
            count_in = pool.dma(lambda e: e.dma_start(inv_count, t["inv_count"]), sem("count_load"), 16)
            dve.do(lambda e: e.memset(p_in[:, :, 0:pad], 0.0))
            for f in range(2):
                i, done = projected(t["w_mix_f"][f], f)
                p_done = tt(dve, p_in[:, f, pad:], banks[i][:, :], inv_rms[:, :], ALU.mult, done, norms[0])
                bank_free[i] = [p_done]
            w = SEQ + pad
            tt(dve, s2[:, :, 1:w], p_in[:, :, 1:w], p_in[:, :, 0:w - 1], ALU.add)
            tt(dve, s4[:, :, 3:w], s2[:, :, 3:w], s2[:, :, 1:w - 2], ALU.add)
            tt(dve, s8[:, 7:w], s4[:, 1, 7:w], s4[:, 1, 3:w - 4], ALU.add)
            tt(dve, s16[:, 15:w], s8[:, 15:w], s8[:, 7:w - 8], ALU.add)
            for rows64, f, sums in ((slice(0, 64), 0, s2[:, 0]), (slice(64, 128), 0, s4[:, 0]),
                                    (slice(0, 64), 1, s8), (slice(64, 128), 1, s16)):
                tt(dve, window[rows64, f, :], sums[rows64, pad:], inv_count[rows64, f, :], ALU.mult,
                   count_in)
            pooled = tt(dve, window, window, p_in[:, :, pad:], ALU.subtract)
            for f in range(2):
                for r in (slice(0, 64), slice(64, 128)):
                    i = take()
                    done = psum_group(i, banks[i][r, :], [(pool_w[r, f, :], window[r, f, :])], pooled)
                    bank_free[i] = [ts(dve, yT[r, f, :], banks[i][r, :], col("pool_b", f, r),
                                       col("pool_scale", f, r), ALU.add, ALU.mult, done)]

            arena_at[0] = start
            fence()
            kkE, rE, bI, kI = (room(2, SEQ) for _ in range(4))
            tokA = room(TT, 512)
            tokB = room(TT, 512)
            g_tok = room(TT, G)
            eB = room(2, SEQ)
            inner = arena_at[0]
            mixed = room(8, SEQ)
            sigma, cum, eI, a_gate, kk, tmp = (room(2, SEQ) for _ in range(6))
            shifted = room(2, SEQ)
            keep = small[:, 100:108]
            kept = ts(dve, keep, cols[:, COLS["rwkv_mu"][0]:COLS["rwkv_mu"][0] + 8], -1.0, 1.0, ALU.mult,
                      ALU.add)
            for f in range(8):
                i, done = projected(t["w_mix_f"][2 + f], f)
                s = shifted[:, f % 2, :]
                scaled = tt(dve, s, banks[i][:, :], inv_rms[:, :], ALU.mult, done, act.now())
                bank_free[i] = [scaled]
                own = copy_act(mixed[:, f, :], s, scaled, kept, scale=keep[:, f:f + 1])
                mix = stt(mixed[:, f, 1:], s[:, 0:SEQ - 1], col("rwkv_mu", f), mixed[:, f, 1:], ALU.mult,
                          ALU.add, own)
            rr, rk, rv = mixed[:, 0:2, :], mixed[:, 2:4, :], mixed[:, 4:6, :]
            bent = copy_act(mixed[0:64, 6, :], mixed[0:64, 6, :], mix, func=ACT.Tanh)
            gate_in = copy_act(mixed[:, 7, :], mixed[:, 7, :], mix, func=ACT.Sigmoid)
            for f in range(2):
                for out, r, bias in ((sigma, slice(0, 64), "rwkv_w0"), (a_gate, slice(64, 128), "rwkv_a0")):
                    i = take()
                    done = psum_group(i, banks[i][:, :], [(lora[r, 0, f * P:(f + 1) * P], mixed[r, 6, :])],
                                      bent)
                    sig = copy_act(out[:, f, :], banks[i][:, :], done, func=ACT.Sigmoid, bias=col(bias, f))
                    bank_free[i] = [sig]
            for half in range(2):
                i = take()
                for j in range(2):
                    tile = 2 * half + j
                    done = psum_group(i, banks[i][:, j * G:(j + 1) * G],
                                      [(mixed[:, 7, tile * P:(tile + 1) * P], lora[:, 1, :])], gate_in)
                g_done = copy_act(g_tok[:, 2 * half:2 * half + 2, :],
                                  banks[i][:, :].rearrange("p (a b) -> p a b", b=G), done)
                bank_free[i] = [g_done]
            for f in range(2):
                scanned = dve.do(lambda e, f=f: e.tensor_tensor_scan(
                    cum[:, f, :], table("restart"), sigma[:, f, :], 0.0, ALU.mult, ALU.add), sig)
            before = tt(dve, tmp, cum, sigma, ALU.subtract)
            copy_act(eB, cum, scanned, func=ACT.Exp, scale=-HALF_E)
            copy_act(eI, cum, scanned, func=ACT.Exp, scale=HALF_E)
            exps = copy_act(tmp, tmp, before, func=ACT.Exp, scale=-HALF_E)
            for f in range(2):
                ts(dve, kk[:, f, :], rk[:, f, :], col("rwkv_k_k", f), None, ALU.mult, ALU.bypass)
            sq = tt(dve, kI, kk, kk, ALU.mult)
            for f in range(2):
                i = take()
                done = psum_group(i, banks[i][:, :], [(same_head, kI[:, f, :])], sq)
                floored = ts(dve, kI[:, f, :], banks[i][:, :], 1e-24, None, ALU.max, ALU.bypass, done)
                bank_free[i] = [floored]
            root = copy_act(kI, kI, floored, func=ACT.Sqrt)
            recip(kI, kI, root)
            tt(dve, kk, kk, kI, ALU.mult)
            tt(dve, kkE, kk, tmp, ALU.mult, exps)
            tt(dve, bI, kk, a_gate, ALU.mult)
            tt(dve, bI, bI, eI, ALU.mult)
            for f in range(2):
                ts(dve, tmp[:, f, :], a_gate[:, f, :], 1.0, col("rwkv_k_a", f), ALU.subtract, ALU.mult)
                stt(rk[:, f, :], tmp[:, f, :], 1.0, rk[:, f, :], ALU.add, ALU.mult)
                stt(sigma[:, f, :], rr[:, f, :], col("rwkv_r_k", f), rk[:, f, :], ALU.mult, ALU.mult)
            tt(dve, kI, rk, eI, ALU.mult)
            scaled = tt(dve, rE, rr, eB, ALU.mult)
            for tile in range(TT):
                c = slice(tile * P, (tile + 1) * P)
                for out, (a, b) in ((tokA, (kkE, kI)), (tokB, (bI, rv))):
                    i = take()
                    done = transposes(i, [(banks[i][:, n * P:(n + 1) * P], s[:, n % 2, c])
                                          for n, s in enumerate((a, a, b, b))], scaled)
                    tok_done = copy_act(out[:, tile, :], banks[i][:, :], done)
                    bank_free[i] = [tok_done]
            bonus = small[:, 112:128]
            i = take()
            for tile in range(TT):
                for f in range(2):
                    at = 4 * tile + 2 * f
                    done = psum_group(i, banks[i][:, at:at + 2],
                                      [(sigma[:, f, tile * P:(tile + 1) * P], same_head[:, 0:P:64])], scaled)
            bonus_done = copy_act(bonus, banks[i][:, 0:16], done)
            bank_free[i] = [bonus_done]

            fence()
            arena_at[0] = inner
            M_rk, M_rb, XT = (room(4, TT * P) for _ in range(3))
            AT, X, Pm, CT, A_ak = (room(2, TT * P) for _ in range(5))
            Gv = room(2, TT * 64)
            W1 = room(TT, G)
            W2T = room(TT, 2, P)
            tiles4 = lambda ap: ap.rearrange("p (a b) -> p a b", b=P)

            def gram(h, left, right):
                r, f = slice(64 * (h % 2), 64 * (h % 2) + 64), h // 2
                i = take()
                for tile in range(TT):
                    c = slice(tile * P, (tile + 1) * P)
                    done = psum_group(i, banks[i][:, c], [(left[r, f, c], right[r, f, c])], scaled)
                return i, done

            def masked(out, h, left, right, mask):
                i, done = gram(h, left, right)
                made = tt(dve, tiles4(out), tiles4(banks[i][:, :]), over_tiles(mask), ALU.mult, done)
                bank_free[i] = [made]
                return made

            def per_tile(left, right, *tokens, width=P, out=lambda b, tile: b[:, tile * P:(tile + 1) * P]):
                i = take()
                for tile in range(TT):
                    done = psum_group(i, out(banks[i], tile), [(left(tile), right(tile))], *tokens)
                return i, done

            def tile_of(ap):
                return lambda tile: ap[:, tile * P:(tile + 1) * P]

            def pairs(m):
                n = LEVELS.index(m)
                return table("pairs")[:, n * P:(n + 1) * P]

            for pair in (0, 2):
                made = {}
                for s in range(2):
                    h = pair + s
                    masked(X[:, s, :], h, kkE, bI, table("pairs_ts"))
                    stt(tiles4(X[:, s, :]), tiles4(X[:, s, :]), -1.0, over_tiles(ident), ALU.mult, ALU.add)
                    masked(AT[:, s, :], h, bI, kkE, table("before"))
                    tt(dve, tiles4(XT[:, h, :]), tiles4(AT[:, s, :]), over_tiles(pairs(1)), ALU.mult)
                    made[s] = stt(tiles4(XT[:, h, :]), tiles4(XT[:, h, :]), -1.0, over_tiles(ident),
                                  ALU.mult, ALU.add)
                    masked(A_ak[:, s, :], h, kI, kkE, table("before"))
                    masked(M_rk[:, h, :], h, kI, rE, table("upto"))
                    m_done = masked(M_rb[:, h, :], h, bI, rE, table("upto"))
                for m in (2, 4, 8, 16, 32):
                    for s in range(2):
                        h = pair + s
                        below = tt(pool, tiles4(CT[:, s, :]), tiles4(AT[:, s, :]), over_tiles(pairs(m)),
                                   ALU.mult, made[s], pe.now())
                        i, done = per_tile(tile_of(CT[:, s, :]), tile_of(X[:, s, :]), below, made[s])
                        p_done = copy_act(Pm[:, s, :], banks[i][:, :], done)
                        bank_free[i] = [p_done]
                        if m < 32:
                            i, done = per_tile(tile_of(XT[:, h, :]), tile_of(Pm[:, s, :]), p_done)
                            bank_free[i] = [tt(dve, X[:, s, :], X[:, s, :], banks[i][:, :], ALU.subtract,
                                               done)]
                        i, done = per_tile(tile_of(Pm[:, s, :]), tile_of(XT[:, h, :]), p_done)
                        made[s] = tt(dve, XT[:, h, :], XT[:, h, :], banks[i][:, :], ALU.subtract, done)
                        bank_free[i] = [made[s]]
                for s in range(2):
                    h = pair + s
                    v_cols = slice(G + h * 64, G + (h + 1) * 64)
                    cols64 = lambda b, tile: b[:, tile * 64:(tile + 1) * 64]
                    i, done = per_tile(tile_of(A_ak[:, s, :]), lambda tile: tokB[:, tile, v_cols], m_done,
                                       tok_done, out=cols64)
                    g_made = copy_act(Gv[:, s, :], banks[i][:, 0:TT * 64], done)
                    bank_free[i] = [g_made]
                    i, done = per_tile(tile_of(XT[:, h, :]),
                                       lambda tile: Gv[:, s, tile * 64:(tile + 1) * 64], g_made, made[s],
                                       out=cols64)
                    w1_done = copy_act(W1[:, :, h * 64:(h + 1) * 64],
                                       banks[i][:, 0:TT * 64].rearrange("p (a b) -> p a b", b=64), done,
                                       scale=-1.0)
                    bank_free[i] = [w1_done]
                    r = slice(64 * s, 64 * s + 64)
                    i, done = per_tile(lambda tile: tokA[:, tile, h * 64:(h + 1) * 64], tile_of(XT[:, h, :]),
                                       out=lambda b, tile: b[r, tile * P:(tile + 1) * P])
                    w2_done = copy_act(W2T[r, :, h // 2, :], tiles4(banks[i][r, :]), done)
                    bank_free[i] = [w2_done]

            fence()
            U = kkE.rearrange("p a b -> p (a b)").rearrange("p (a b) -> p a b", b=G)
            out_r = bI.rearrange("p a b -> p (a b)").rearrange("p (a b) -> p a b", b=G)
            free_k = kI.rearrange("p a b -> p (a b)")
            S, S1, fade = (free_k[:, n * 256:(n + 1) * 256].rearrange("p (a b) -> p a b", b=P)
                           for n in range(3))
            s_done = dve.do(lambda e: e.memset(S, 0.0))
            n_chunks = SEQ // CHUNK
            o_bank = None
            for c in range(n_chunks):
                tile, r = c // 2, slice(64 * (c % 2), 64 * (c % 2) + 64)
                for f in range(2):
                    faded = copy_act(fade[:, f, :], same_head, s_done, scale=eB[:, f, 64 * c + 63:64 * c + 64])
                i = take()
                for f in range(2):
                    done = psum_group(i, banks[i][r, f * P:(f + 1) * P],
                                      [(W2T[:, tile, f, 64 * (c % 2):64 * (c % 2) + 64], S[:, f, :])],
                                      s_done, w2_done)
                u_done = stt(U[r, tile, :], banks[i][r, 0:G], -1.0, W1[r, tile, :], ALU.mult, ALU.add, done,
                             w1_done)
                bank_free[i] = [u_done]
                if c % 2 == 0:
                    o_bank = take()
                    held.add(o_bank)
                    pe.wait(*bank_free[o_bank])
                for f in range(2):
                    pe.quiet(lambda e, o=banks[o_bank][r, f * P:(f + 1) * P],
                             l=rE[:, f, 64 * c:64 * c + 64], s=S[:, f, :], first=(f == 0):
                             e.matmul(o, l, s, start=first, stop=False, skip_group_check=True))
                if c < n_chunks - 1:
                    i = take()
                    for f in range(2):
                        lo, hi = slice(f * P, (f + 1) * P), slice(G + f * P, G + (f + 1) * P)
                        done = psum_group(i, banks[i][:, lo],
                                          [(tokA[r, tile, hi], tokB[r, tile, hi]),
                                           (tokB[r, tile, lo], U[r, tile, lo])], u_done)
                    tt(dve, S1, banks[i][:, 0:G].rearrange("p (a b) -> p a b", b=P), S, ALU.add, done)
                    s_done = tt(dve, S, S1, fade, ALU.mult, faded)
                    bank_free[i] = [s_done]
                if c % 2 == 1:
                    pe.wait(u_done)
                    for h in range(4):
                        v_cols, o_cols = slice(G + h * 64, G + (h + 1) * 64), slice(h * 64, (h + 1) * 64)
                        m_cols = slice(tile * P, (tile + 1) * P)
                        pe.quiet(lambda e, o=banks[o_bank][:, o_cols], l=M_rk[:, h, m_cols],
                                 v=tokB[:, tile, v_cols]:
                                 e.matmul(o, l, v, start=False, stop=False, skip_group_check=True))
                        done = pe.do(lambda e, o=banks[o_bank][:, o_cols], l=M_rb[:, h, m_cols],
                                     v=U[:, tile, o_cols]:
                                     e.matmul(o, l, v, start=False, stop=True, skip_group_check=True))
                    o_done = copy_act(out_r[:, tile, :], banks[o_bank][:, 0:G], done)
                    bank_free[o_bank] = [o_done]
                    held.discard(o_bank)

            heads = lambda ap: ap.rearrange("p t (h d) -> p (t h) d", d=64)
            per_head = lambda ap: ap.unsqueeze(2).to_broadcast([P, 16, 64])
            mean, var = small[:, 128:144], small[:, 144:160]
            o16, u16 = heads(out_r), heads(U)
            dve.do(lambda e: e.tensor_reduce(mean, o16, AX_X, ALU.add), o_done)
            ts(dve, mean, mean, 1.0 / 64, None, ALU.mult, ALU.bypass)
            tt(dve, o16, o16, per_head(mean), ALU.subtract)
            tt(dve, u16, o16, o16, ALU.mult)
            summed = dve.do(lambda e: e.tensor_reduce(var, u16, AX_X, ALU.add))
            root = copy_act(var, var, summed, func=ACT.Sqrt, scale=1.0 / 64, bias=GN_EPS)
            recip(var, var, root)
            tt(dve, o16, o16, per_head(var), ALU.mult)
            tt(dve, out_r, out_r, over_tiles(rows[:, 1, :]), ALU.mult)
            tt(dve, out_r, out_r, over_tiles(rows[:, 2, :]), ALU.add)
            for tile in range(TT):
                tt(dve, U[:, tile, :].rearrange("p (h d) -> p h d", d=64),
                   tokB[:, tile, G:].rearrange("p (h d) -> p h d", d=64),
                   bonus[:, 4 * tile:4 * tile + 4].unsqueeze(2).to_broadcast([P, 4, 64]), ALU.mult, bonus_done)
            tt(dve, out_r, out_r, U, ALU.add)
            y_r = tt(dve, out_r, out_r, g_tok, ALU.mult, g_done)

            def to_yT(source, f, y_tile, *tokens):
                i = take()
                done = transposes(i, [(banks[i][:, tile * P:(tile + 1) * P],
                                       source[:, tile, f * P:(f + 1) * P]) for tile in range(TT)], *tokens)
                bank_free[i] = [copy_act(yT[:, y_tile, :], banks[i][:, :], done)]
                return bank_free[i][0]

            for f in range(2):
                to_yT(out_r, f, 4 + f, y_r)

            fence()
            arena_at[0] = start
            q4, k4, c4 = room(4, SEQ), room(4, SEQ), room(4, SEQ)
            E2 = [room(4, SEQ), room(4, SEQ)]
            near = room(8, TT * P)
            far = room(8, 768)
            hv, gv = room(TT, 512), room(TT, 512)
            lb, e_lb, keep_lb = small[:, 160:162], small[:, 162:164], small[:, 164:166]
            logits = cols[:, COLS["lb_logits"][0]:COLS["lb_logits"][0] + 2]
            centred = tt(dve, e_lb, logits, logits, ALU.subtract)
            raised = copy_act(e_lb, e_lb, centred, func=ACT.Exp)
            recip(lb, e_lb, raised)
            tt(dve, e_lb, e_lb, lb, ALU.mult)
            tt(dve, lb, e_lb, e_lb, ALU.subtract)
            ts(dve, keep_lb, lb, -1.0, 1.0, ALU.mult, ALU.add)

            E, L = E2
            for f in range(2):
                i, done = projected(t["w_mix_f"][10 + f], f)
                got = tt(dve, q4[:, f, :], banks[i][:, :], inv_rms[:, :], ALU.mult, done)
                bank_free[i] = [got]
                bent = copy_act(q4[:, f, :], q4[:, f, :], got, func=ACT.Silu)
                ts(dve, q4[:, f, :], q4[:, f, :], 0.125, None, ALU.mult, ALU.bypass, bent)
                i, done = projected(t["w_mix_f"][12 + f], f)
                got = tt(dve, k4[:, f, :], banks[i][:, :], inv_rms[:, :], ALU.mult, done)
                bank_free[i] = [got]
                sig = copy_act(c4[:, f, :], k4[:, f, :], got, func=ACT.Sigmoid)
                ts(dve, c4[:, f, :], c4[:, f, :], keep_lb[:, f:f + 1], lb[:, f:f + 1], ALU.mult, ALU.add, sig)
                ts(dve, k4[:, f, :], c4[:, f, :], -1.0, 1.0, ALU.mult, ALU.add)
                ts(dve, E[:, f, :], c4[:, f, :], 2.0 ** -60, None, ALU.max, ALU.bypass)
                ts(dve, c4[:, f, :], c4[:, f, :], 1e-30, 2.0 ** 60, ALU.max, ALU.mult)
                got = ts(dve, c4[:, f, :], c4[:, f, :], 1.0, None, ALU.min, ALU.bypass)
                copy_act(E[:, f, :], E[:, f, :], got, func=ACT.Ln)
                logs = copy_act(c4[:, f, :], c4[:, f, :], func=ACT.Ln)
                tt(dve, c4[:, f, :], c4[:, f, :], E[:, f, :], ALU.add, logs)
            for f in range(2):
                i, done = projected(t["w_mix_f"][14 + f], f)
                bank_free[i] = [stt(q4[:, 2 + f, :], banks[i][:, :], 0.125, inv_rms[:, :], ALU.mult,
                                    ALU.mult, done)]
                i, done = projected(t["w_mix_f"][16 + f], f)
                bank_free[i] = [tt(dve, k4[:, 2 + f, :], banks[i][:, :], inv_rms[:, :], ALU.mult, done)]
            i, done = projected(t["w_mix_ga"], 0, m=16)
            ga = L[0:16, 0, :]
            ga_done = tt(dve, ga, banks[i][0:16, :], inv_rms[0:16, :], ALU.mult, done)
            bank_free[i] = [ga_done]
            for f in range(2):
                i = take()
                done = psum_group(i, banks[i][:, :], [(gla_w2[0:16, f * P:(f + 1) * P], ga)], ga_done)
                low = ts(dve, c4[:, 2 + f, :], banks[i][:, :], col("gla_b", f), 0.0, ALU.add, ALU.min, done)
                size = copy_act(E[:, 2 + f, :], banks[i][:, :], low, func=ACT.Abs, bias=col("gla_b", f))
                bank_free[i] = [size]
                copy_act(E[:, 2 + f, :], E[:, 2 + f, :], func=ACT.Exp, scale=-1.0)
                logs = copy_act(E[:, 2 + f, :], E[:, 2 + f, :], func=ACT.Ln, bias=1.0)
                tt(dve, c4[:, 2 + f, :], c4[:, 2 + f, :], E[:, 2 + f, :], ALU.subtract, logs)
                ts(dve, c4[:, 2 + f, :], c4[:, 2 + f, :], 1.0 / 16, None, ALU.mult, ALU.bypass)
            for g, (out, func) in enumerate(((hv, ACT.Sigmoid), (gv, ACT.Silu))):
                got, done = token_major([t["w_mix_tok"][g, u] for u in range(4)])
                for tile, i in enumerate(got):
                    s = inv_rms_t[:, tile:tile + 1]
                    copy_act(out[:, tile, 0:G], banks[i][:, 0:G], done, norms[1], scale=s)
                    v_done = copy_act(out[:, tile, G:], banks[i][:, G:], func=func, scale=s)
                    bank_free[i] = [v_done]
            pe_used_xg[0] = pe.now()
            rms_free[0] = dve.now()
            for f in range(4):
                c_done = dve.do(lambda e, f=f: e.tensor_tensor_scan(
                    c4[:, f, :], table("restart"), c4[:, f, :], 0.0, ALU.mult, ALU.add))

            def head_tile(h):
                return slice(64 * (h % 2), 64 * (h % 2) + 64), h // 2

            for h in range(8):
                r, g = head_tile(h)
                i = take()
                for tile in range(TT):
                    c = slice(tile * P, (tile + 1) * P)
                    done = psum_group(i, banks[i][:, c], [(k4[r, g, c], q4[r, g, c])], c_done)
                bank_free[i] = [tt(dve, tiles4(near[:, h, :]), tiles4(banks[i][:, :]), over_tiles(ident),
                                   ALU.mult, done)]
            flat = lambda ap: ap.rearrange("p a b -> p (a b)")
            e_free = [None, None]
            for n, m in enumerate((32, 16, 8, 4, 2, 1, 64, 128, 256)):
                e = E2[n % 2]
                blocks = lambda ap: flat(ap).rearrange("p (n c) -> p n c", c=2 * m)
                cb, eb, qb, kb = blocks(c4), blocks(e), blocks(q4), blocks(k4)
                nb = 2 * SEQ // m
                if m > 64:
                    half = flat(c4).rearrange("p (n c) -> p n c", c=m)
                    tt(dve, half[:, :, m // 2:m], half[:, :, m // 2:m],
                       half[:, :, m // 2 - 1:m // 2].to_broadcast([P, 2 * nb, m // 2]), ALU.add, act.now())
                border = cb[:, :, m - 1:m].to_broadcast([P, nb, m])
                tt(dve, eb[:, :, 0:m], border, cb[:, :, 0:m], ALU.subtract, e_free[n % 2])
                if m < 64:
                    made = tt(dve, eb[:, :, m:], cb[:, :, m:], border, ALU.subtract)
                    made = copy_act(flat(e), flat(e), made, func=ACT.Exp)
                else:
                    copy_act(eb[:, :, m:], cb[:, :, m:], dve.now(), func=ACT.Exp)
                    made = copy_act(eb[:, :, 0:m], eb[:, :, 0:m], func=ACT.Exp)
                left = tt(pool, eb[:, :, 0:m], eb[:, :, 0:m], kb[:, :, 0:m], ALU.mult, made)
                right = tt(dve, eb[:, :, m:], eb[:, :, m:], qb[:, :, m:], ALU.mult, made)
                for h in range(8):
                    r, g = head_tile(h)
                    i = take()
                    if m <= 64:
                        for tile in range(TT):
                            c = slice(tile * P, (tile + 1) * P)
                            done = psum_group(i, banks[i][:, c], [(e[r, g, c], e[r, g, c])], left, right)
                        mask = pairs(m).bitcast(I32).unsqueeze(1).to_broadcast([P, TT, P])
                        bank_free[i] = [dve.do(lambda eng, h=h, i=i, mask=mask: eng.copy_predicated(
                            tiles4(near[:, h, :]), mask, tiles4(banks[i][:, :])), done)]
                    elif m == 128:
                        for n_far, key in enumerate((0, 2)):
                            done = psum_group(i, banks[i][:, n_far * P:(n_far + 1) * P],
                                              [(e[r, g, key * P:(key + 1) * P],
                                                e[r, g, (key + 1) * P:(key + 2) * P])], left, right)
                        bank_free[i] = [copy_act(far[:, h, 0:256], banks[i][:, 0:256], done)]
                    else:
                        for key in range(2):
                            done = psum_group(i, banks[i][:, key * 256:(key + 1) * 256],
                                              [(e[r, g, key * P:(key + 1) * P], e[r, g, 256:512])],
                                              left, right)
                        bank_free[i] = [copy_act(far[:, h, 256:768], banks[i][:, :], done)]
                e_free[n % 2] = done
            scores_done = (dve.now(), act.now())

            fence()
            o4 = q4
            for tile in range(TT):
                i = take()
                for h in range(8):
                    val = hv if h < 4 else gv
                    v_cols = slice((h % 4) * 64, (h % 4 + 1) * 64)
                    products = [(near[:, h, tile * P:(tile + 1) * P], val[:, tile, v_cols])]
                    if tile % 2:
                        n_far = tile // 2
                        products.append((far[:, h, n_far * P:(n_far + 1) * P], val[:, tile - 1, v_cols]))
                    if tile >= 2:
                        for key in range(2):
                            at = 256 + key * 256 + (tile - 2) * P
                            products.append((far[:, h, at:at + P], val[:, key, v_cols]))
                    done = psum_group(i, banks[i][:, h * 64:(h + 1) * 64], products, *scores_done, v_done)
                o_done = copy_act(o4[:, tile, :], banks[i][:, :], done)
                bank_free[i] = [o_done]
            h_out, g_out = o4[:, :, 0:G], o4[:, :, G:]
            sq4 = E2[0]
            ms_h, ms_g = small[:, 128:132], small[:, 132:148]
            tt(dve, sq4, o4, o4, ALU.mult, o_done)
            dve.do(lambda e: e.tensor_reduce(ms_h, sq4[:, :, 0:G], AX_X, ALU.add))
            for tile in range(TT):
                reduced = dve.do(lambda e, tile=tile: e.tensor_reduce(
                    ms_g[:, 4 * tile:4 * tile + 4], sq4[:, tile, G:].rearrange("p (h d) -> p h d", d=64),
                    AX_X, ALU.add))
            copy_act(ms_h, ms_h, reduced, func=ACT.Sqrt, scale=1.0 / G, bias=EPS)
            root = copy_act(ms_g, ms_g, func=ACT.Sqrt, scale=1.0 / 64, bias=EPS)
            recip(small[:, 128:148], small[:, 128:148], root)
            tt(dve, h_out, h_out, ms_h.unsqueeze(2).to_broadcast([P, TT, G]), ALU.mult)
            for tile in range(TT):
                part = g_out[:, tile, :].rearrange("p (h d) -> p h d", d=64)
                tt(dve, part, part, ms_g[:, 4 * tile:4 * tile + 4].unsqueeze(2).to_broadcast([P, 4, 64]),
                   ALU.mult)
            tt(dve, h_out, h_out, over_tiles(rows[:, 0, :]), ALU.mult)
            tt(dve, g_out, g_out, over_tiles(rows[:, 3, :]), ALU.mult)
            tt(dve, h_out, h_out, hv[:, :, G:], ALU.mult)
            y_o = tt(dve, g_out, g_out, gv[:, :, G:], ALU.mult)
            for f, y_tile in enumerate((2, 3, 6, 7)):
                y_done = to_yT(o4, f, y_tile, y_o)
            return output_product(lambda f: [t["w_mix_out"][f]], lambda k: yT[:, k, :], KT, 1.0,
                                  "norm_ffn2", y_done, dve.now())

        xg_ready = feed_forward(0, xg_ready, "norm_mix")
        xg_ready = mixers(xg_ready)
        feed_forward(1, xg_ready, None)

        rms_done, _ = finish_norm(False)
        out_sem = sem("out_stored")
        sent = [0]

        def send(f, token):
            sent[0] += 1
            sp.dma(lambda e: e.dma_start(t["outT"][:, f, :], x[:, f, :]), out_sem, 0, token)

        apply_norm("norm_final", send, rms_done)
        sp.wait((out_sem, 16 * sent[0]))

        block = ctx.enter_context(nc.Block())
        block.tensor(pe.run)
        block.vector(dve.run)
        block.scalar(act.run)
        block.gpsimd(pool.run)
        block.sync(sp.run)


def constants():
    f32 = np.float32
    shared = np.zeros((P, N_SHARED), f32)
    shared[:, 0:128] = np.eye(P)
    lin = np.linspace(0.0, 1.0, RET_DIM // 2, dtype=f32)
    shared[:, 128:192] = (f32(1.0) / np.power(f32(10000.0), lin)).astype(f32)
    j, i = np.arange(P)[:, None], np.arange(SEQ)[None, :]
    decays = np.zeros((P, RET_HEADS, SEQ), f32)
    for h in range(RET_HEADS):
        log_g = np.log1p(-(2.0 ** (-5.0 - h)))
        decays[:, h] = np.where(i // CHUNK >= j // CHUNK, RET_DIM ** -0.5 * np.exp(np.abs(i - j) * log_g), 0)
    r, c = np.arange(P)[:, None], np.arange(P)[None, :]
    mixer = np.zeros((P, N_MIXER + 1024), f32)

    def put(name, a):
        at, n = MIXER[name]
        mixer[:, at:at + n] = a.reshape(a.shape[0], n)

    put("same_head", (r // 64 == c // 64).astype(f32))
    put("before", ((r // 64 == c // 64) & (r < c)).astype(f32))
    put("upto", ((r // 64 == c // 64) & (r <= c)).astype(f32))
    pair = lambda m, s, t: ((s // (2 * m) == t // (2 * m)) & (s // m % 2 == 0) & (t // m % 2 == 1))
    put("pairs", np.stack([pair(m, r, c) for m in LEVELS], 1).astype(f32))
    put("pairs_ts", pair(1, c, r).astype(f32))
    tokens = np.arange(SEQ)
    put("restart", np.broadcast_to((tokens % CHUNK != 0).astype(f32), (P, SEQ)))
    windows = np.array([[2, 8], [4, 16]])[np.arange(P) // 64]
    count = np.minimum(tokens[None, None, :] + 1, windows[:, :, None])
    put("inv_count", (1.0 / count).astype(f32))
    return shared, decays, mixer


def layouts(inputs):
    a = {k: np.asarray(v) for k, v in inputs.items()}

    def tiles(w, m=P):
        k, n = w.shape
        return w.reshape(k // P, P, n // m, m).transpose(2, 1, 0, 3).reshape(n // m, P, -1)

    def groups(w):
        k, n = w.shape
        return w.reshape(k // 256, 2, P, n // 512, 512).transpose(3, 0, 2, 1, 4).reshape(
            n // 512, k // 256, P, 1024)

    out = {"xT": a["x"][0].T.reshape(KT, P, SEQ).transpose(1, 0, 2),
           "positions": a["positions"].astype(np.int32).reshape(TT, P).T}
    w_in = a["w_in"]
    out["w_qk"] = np.stack([tiles(w[:, 0:1024]) for w in w_in])
    order = (4, 5, 2, 3, 6, 7)
    out["w_tok"] = np.stack([np.concatenate([groups(w[:, 512 * g:512 * g + 512]) for g in order])
                             for w in w_in])
    out["w_out"] = np.stack([tiles(w) for w in a["w_out"]])
    r = a["rel_bias"]
    distance = np.arange(P)[:, None] + (SEQ - P) - np.arange(SEQ)[None, :]
    strips = r[:, :, np.clip(distance, -CLIP, CLIP) + CLIP]
    out["strips"] = strips.reshape(2, 2, 4, P, SEQ).transpose(0, 1, 3, 2, 4)
    ffn = [(a["ffn1_w_in_2"][0], a["ffn1_w_out_2"][0]), (a["ffn2_w_in_2"][0], a["ffn2_w_out_2"][0])]
    out["w_ffn_in"] = np.stack([np.stack([tiles(w[:, :D_FF]), tiles(w[:, D_FF:])], 1)
                                .reshape(2 * FT, P, UNIT) for w, _ in ffn])
    out["w_ffn_out"] = np.stack([tiles(w) for _, w in ffn])
    named = {"gain0": a["norm_gain"][0], "gain1": a["norm_gain"][1], "final_gain": a["final_gain"],
             "norm_ffn1": a["norm_ffn1_2"], "norm_mix": a["norm_mix_2"], "norm_ffn2": a["norm_ffn2_2"],
             "norm_final": a["norm_final_2"], "pool_b": a["pool_b_2"], "pool_scale": a["pool_scale_2"],
             "rwkv_mu": a["rwkv_mu_2"], "rwkv_w0": a["rwkv_w0_2"], "rwkv_a0": a["rwkv_a0_2"],
             "rwkv_k_k": a["rwkv_k_k_2"], "rwkv_k_a": a["rwkv_k_a_2"], "rwkv_r_k": a["rwkv_r_k_2"],
             "gla_b": a["gla_b_2"], "lb_logits": a["hgrn_lb_logits_2"]}
    out["cols"] = np.concatenate([named[k].reshape(n, P).T for k, (_, n) in COLS.items()], axis=1)
    out["shared"], out["decays"], out["mixer"] = constants()
    w = a["w_in_2"][0]
    feature_cols = ((0, 256), (1280, 2304), (256, 512), (512, 768), (2304, 2560), (2560, 2816))
    out["w_mix_f"] = np.concatenate([tiles(w[:, lo:hi]) for lo, hi in feature_cols])
    out["w_mix_ga"] = tiles(w[:, 3328:], 16)[0]
    out["w_mix_tok"] = np.concatenate([groups(w[:, 768:1280]), groups(w[:, 2816:3328])])
    out["w_mix_out"] = tiles(a["w_out_2"][0])
    out["rows"] = np.stack([np.broadcast_to(a[k][0], (P, G)) for k in
                            ("hgrn_norm_2", "rwkv_ln_w_2", "rwkv_ln_b_2", "gla_norm_2")], axis=1)
    out["lora"] = np.stack([np.concatenate([a["rwkv_w2_2"][0], a["rwkv_a2_2"][0]]), a["rwkv_g2_2"][0]], 1)
    out["gla_w2"] = a["gla_w2_2"][0]
    out["pool_w"] = a["pool_w_2"][0].reshape(2, P, 64).transpose(1, 0, 2)
    out["inv_count"] = out["mixer"][:, N_MIXER:].reshape(P, 2, SEQ)
    out["mixer"] = out["mixer"][:, :N_MIXER]
    return {k: np.ascontiguousarray(v) for k, v in out.items()}


def kernel(**inputs):
    import concourse.bacc as bacc
    from concourse.bass_utils import run_bass_kernel_spmd

    nc = bacc.Bacc("TRN2", target_bir_lowering=False, num_devices=1)
    arrays = layouts(inputs)
    t = {k: nc.dram_tensor(k, v.shape, mybir.dt.from_np(v.dtype), kind="ExternalInput").ap()
         for k, v in arrays.items()}
    t["outT"] = nc.dram_tensor("outT", (P, KT, SEQ), F32, kind="ExternalOutput").ap()
    build(nc, t)
    got = run_bass_kernel_spmd(nc, [arrays], core_ids=[0]).results[0]["outT"]
    return got.transpose(2, 1, 0).reshape(1, SEQ, D)
```

```python
import math
from contextlib import ExitStack

import concourse.bass as bass
import numpy as np
from concourse import mybir

F32 = mybir.dt.float32
F32R = mybir.dt.float32r
I32 = mybir.dt.int32
ALU = mybir.AluOpType
ACT = mybir.ActivationFunctionType
AX_X = mybir.AxisListType.X

P = 128
SEQ = 512
D = 1024
KT = D // P
TT = SEQ // P
CHUNK = 64
CLIP = 256
ATT_HEADS, ATT_DIM = 8, 64
RET_HEADS, RET_DIM = 4, 128
EPS = 1e-6
GN_EPS = 64e-5
NEG_INF = -1e30
D_FF = 2816
FT = D_FF // P
G = 256
UNIT = 1024
RAW = 4
SPLIT = 3
BANKS = 8
LEVELS = (64, 32, 16, 8, 4, 2, 1)
HALF_E = math.exp(-0.5)
ROUND = 12582912.0

COLS = {}
for _name, _n in (("gain0", 8), ("gain1", 8), ("final_gain", 8), ("norm_ffn1", 8), ("norm_mix", 8),
                  ("norm_ffn2", 8), ("norm_final", 8), ("pool_b", 2), ("pool_scale", 2),
                  ("rwkv_mu", 8), ("rwkv_w0", 2), ("rwkv_a0", 2), ("rwkv_k_k", 2), ("rwkv_k_a", 2),
                  ("rwkv_r_k", 2), ("gla_b", 2), ("lb_logits", 2)):
    COLS[_name] = (sum(n for _, n in COLS.values()), _n)
N_COLS = sum(n for _, n in COLS.values())

SHARED = {"ident": (0, 128), "inv_freq": (128, 64)}
N_SHARED = 192
MIXER = {"same_head": (0, 128), "before": (128, 128), "upto": (256, 128), "pairs": (384, 7 * 128),
         "pairs_ts": (384 + 896, 128), "restart": (1408, 512), "inv_count": (1920, 1024)}
N_MIXER = 1920


class Queue:

    def __init__(self, sem, chained=False):
        self.sem, self.count, self.steps, self.waited = sem, 0, [], {}
        self.chained = chained

    def wait(self, *tokens):
        for token in tokens:
            if token is None:
                continue
            sem, value = token
            if value > self.waited.get(sem, 0):
                self.waited[sem] = value
                self.steps.append(lambda eng, s=sem, v=value: eng.wait_ge(s, v))

    def do(self, emit, *tokens):
        self.wait(*tokens)
        if self.chained:
            self.wait(self.now())
        self.count += 1
        self.steps.append(lambda eng: emit(eng).then_inc(self.sem, 1))
        return (self.sem, self.count)

    def quiet(self, emit, *tokens):
        self.wait(*tokens)
        self.steps.append(emit)

    def dma(self, emit, sem, value, *tokens):
        self.wait(*tokens)
        self.steps.append(lambda eng: emit(eng).then_inc(sem, 16))
        return (sem, value)

    def now(self):
        return (self.sem, self.count) if self.count else None

    def run(self, eng):
        for step in self.steps:
            step(eng)


def unit_order(t):
    order = []
    for n in range(2):
        order += [t["w_qk"][n, f] for f in range(8)]
        order += [t["w_tok"][n, g, u] for g in range(6) for u in range(4)]
        order += [t["w_out"][n, f] for f in range(KT)]

    def feed_forward(which):
        units = [t["w_ffn_in"][which, f] for f in range(2 * FT)]
        return units + [t["w_ffn_out"][which, f][:, a:min(a + UNIT, D_FF)]
                        for f in range(KT) for a in range(0, D_FF, UNIT)]

    def mixer_tiles(*tiles):
        return [t["w_mix_f"][f] for f in tiles]

    def mixer_group(g):
        return [t["w_mix_tok"][g, u] for u in range(4)]

    order += feed_forward(0)
    order += mixer_tiles(0, 1)
    order += mixer_tiles(10, 12, 11, 13) + mixer_group(0)
    order += mixer_tiles(14, 16, 15, 17) + [t["w_mix_ga"]]
    values, projections = mixer_group(1), mixer_tiles(*range(2, 10))
    order += values[0:2] + projections[0:1] + values[2:4] + projections[1:]
    order += [t["w_mix_out"][f] for f in range(KT)]
    return order + feed_forward(1)


def build(nc, t):
    with ExitStack() as ctx:
        def sbuf(name, shape, dt=F32):
            return ctx.enter_context(nc.sbuf_tensor(f"sb_{name}", shape, dt))

        def sem(name):
            return ctx.enter_context(nc.semaphore(name))

        pe, dve, act, pool, sp = (Queue(sem(f"done_{n}"), n in ("dve", "act", "pool")) for n in ("pe", "dve", "act", "pool", "sp"))

        class Region:

            def __init__(self, at, end):
                self.at, self.end = -(-at // 32) * 32, end

            def room(self, name, *shape, dt=F32):
                names[name] = names.get(name, 0) + 1
                size = -(-int(np.prod(shape)) * 4 // 32) * 32
                assert self.at + size <= self.end, (name, self.at + size, self.end)
                h = nc.alloc_sbuf_tensor_at(f"sb_{name}_{names[name]}", [P, *shape], dt, offset=self.at)
                self.at += size
                return h[(slice(None),) * (1 + len(shape))]

        names = {}
        stay = Region(nc.sbuf_base, nc.sbuf_usable_end // 32 * 32)
        x = stay.room("x", KT, SEQ)
        raw = stay.room("raw", RAW, UNIT)
        w_high = stay.room("w_high", SPLIT, UNIT, dt=F32R)
        w_low = stay.room("w_low", SPLIT, UNIT, dt=F32R)
        cols = stay.room("cols", N_COLS)
        shared = stay.room("shared", N_SHARED)
        ones = stay.room("ones", P)
        square = stay.room("square", 2, SEQ)
        inv_rms = stay.room("inv_rms", SEQ)
        inv_rms_t = stay.room("inv_rms_t", TT)
        small = stay.room("small", 256)
        positions = stay.room("positions", TT, dt=I32)
        cos2, sin2 = stay.room("cos2", TT, P), stay.room("sin2", TT, P)
        xg_at = stay.at
        xg = Region(xg_at, stay.end)
        xg_high, xg_low = xg.room("xg_high", KT, SEQ, dt=F32R), xg.room("xg_low", KT, SEQ, dt=F32R)
        phase_at = xg.at
        banks = [ctx.enter_context(nc.psum_tensor(f"bank{i}", [P, 512], F32)) for i in range(BANKS)]

        def col(name, i, rows=slice(0, P)):
            at = COLS[name][0] + i
            return cols[rows, at:at + 1]

        ident = shared[:, 0:128]

        bank_free = [[] for _ in range(BANKS)]
        turn = [0]
        held = set()

        def take():
            while True:
                i = turn[0] % BANKS
                turn[0] += 1
                if i not in held:
                    return i

        def psum_group(i, out, pairs, *tokens):
            pe.wait(*bank_free[i])
            pe.wait(*tokens)
            for n, (lhsT, rhs) in enumerate(pairs):
                first, last = n == 0, n == len(pairs) - 1
                emit = (lambda e, o=out, l=lhsT, r=rhs, f=first, z=last:
                        e.matmul(o, l, r, start=f, stop=z))
                if last:
                    return pe.do(emit)
                pe.quiet(emit)

        def transposes(i, blocks, *tokens):
            pe.wait(*bank_free[i])
            pe.wait(*tokens)
            for n, (out, in_) in enumerate(blocks):
                emit = lambda e, o=out, a=in_: e.transpose(o, a, ident)
                if n == len(blocks) - 1:
                    return pe.do(emit)
                pe.quiet(emit)

        raw_sem = [sem(f"weights_{i}") for i in range(RAW)]
        raw_free = [None] * RAW
        split_free = [None] * SPLIT
        order = unit_order(t)
        loaded, parts, used = [], [], [0]

        def load_unit():
            n = len(loaded)
            dram, slot = order[n], n % RAW
            dst = raw[:, slot, 0:dram.shape[-1]]
            loaded.append((dst, sp.dma(lambda e: e.dma_start(dst, dram), raw_sem[slot],
                                       16 * (n // RAW + 1), raw_free[slot])))

        def split_unit():
            n = len(parts)
            src, token = loaded[n]
            width, slot = src.shape[-1], n % SPLIT
            high, low = w_high[:, slot, 0:width], w_low[:, slot, 0:width]
            rounded = copy_act(high, src, token, split_free[slot])
            raw_free[n % RAW] = tt(dve, low, src, high.bitcast(F32), ALU.subtract, rounded)
            parts.append((high, low, raw_free[n % RAW]))
            if len(loaded) < len(order):
                load_unit()

        def next_unit():
            n = used[0]
            used[0] += 1
            while len(parts) < min(n + SPLIT, len(order)):
                split_unit()
            return n % SPLIT, parts[n]

        def three_passes(out, w, v, first, last):
            for n, (a, b) in enumerate(((w[0], v[0]), (w[0], v[1]), (w[1], v[0]))):
                yield (lambda e, a=a, b=b, f=(first and n == 0), z=(last and n == 2):
                       e.matmul(out, a, b, start=f, stop=z))

        def run_products(slot, emits):
            for emit in emits[:-1]:
                pe.quiet(emit)
            split_free[slot] = pe.do(emits[-1])
            return split_free[slot]

        def feature_major(n_units, k_tiles, rhs, *tokens):
            i, k = take(), 0
            pe.wait(*bank_free[i])
            pe.wait(*tokens)
            for _ in range(n_units):
                slot, (high, low, ready) = next_unit()
                pe.wait(ready)
                emits = []
                for j in range(high.shape[-1] // P):
                    c = slice(j * P, (j + 1) * P)
                    emits += three_passes(banks[i][:, :], (high[:, c], low[:, c]), rhs(k), k == 0,
                                          k == k_tiles - 1)
                    k += 1
                done = run_products(slot, emits)
            return i, done

        def token_major(*tokens):
            out = [take() for _ in range(TT)]
            held.update(out)
            for i in out:
                pe.wait(*bank_free[i])
            pe.wait(*tokens)
            for u in range(KT // 2):
                slot, (high, low, ready) = next_unit()
                pe.wait(ready)
                emits = []
                for j in range(2):
                    k, c = 2 * u + j, slice(j * 512, (j + 1) * 512)
                    for tile, i in enumerate(out):
                        r = slice(tile * P, (tile + 1) * P)
                        emits += three_passes(banks[i][:, :], (xg_high[:, k, r], xg_low[:, k, r]),
                                              (high[:, c], low[:, c]), k == 0, k == KT - 1)
                done = run_products(slot, emits)
                if u < KT // 2 - 1:
                    yield
            held.difference_update(out)
            token_major_result[:] = [out, done]

        token_major_result = []

        def whole_group(*tokens):
            for _ in token_major(*tokens):
                pass
            return token_major_result

        def xg_tile(k):
            return xg_high[:, k, :], xg_low[:, k, :]

        def fence():
            ends = [q.now() for q in (pe, dve, act, pool)]
            for q in (dve, act, pool):
                q.wait(*ends)

        def phase():
            fence()
            return Region(phase_at, stay.end)

        def copy_act(out, in_, *tokens, func=ACT.Identity, scale=1.0, bias=0.0, accum=None):
            return act.do(lambda e: e.activation(out, in_, func, bias=bias, scale=scale,
                                                 accum_out=accum), *tokens)

        def tt(q, out, a, b, op, *tokens):
            return q.do(lambda e: e.tensor_tensor(out, a, b, op), *tokens)

        def ts(q, out, a, s1, s2, op0, op1, *tokens):
            return q.do(lambda e: e.tensor_scalar(out, a, s1, s2, op0, op1), *tokens)

        def stt(out, a, s, b, op0, op1, *tokens):
            return dve.do(lambda e: e.scalar_tensor_tensor(out=out, in0=a, scalar=s, in1=b, op0=op0,
                                                           op1=op1), *tokens)

        def recip(out, in_, *tokens):
            return dve.do(lambda e: e.reciprocal(out, in_), *tokens)

        def split_from_bank(high, low, i, *tokens):
            src = banks[i][:, :]
            if len(high.shape) == 3:
                src = src.rearrange("p (f c) -> p f c", c=P)
            rounded = copy_act(high, src, *tokens)
            bank_free[i] = [tt(dve, low, src, high.bitcast(F32), ALU.subtract, rounded)]
            return bank_free[i][0]

        fixed_sem = sem("fixed_loads")
        x_sem = [sem(f"x_load_{i}") for i in range(2)]
        for i in range(2):
            src, half = t["xT"][:, 4 * i:4 * i + 4, :], x[:, 4 * i:4 * i + 4, :]
            act.dma(lambda e, s=src, h=half: e.dma_start(h, s), x_sem[i], 16)
        x_loaded = [(x_sem[i], 16) for i in range(2)]
        fixed = [(cols, t["cols"]), (shared, t["shared"]), (positions, t["positions"])]
        for out, src in fixed:
            pool.dma(lambda e, o=out, s=src: e.dma_start(o, s), fixed_sem, 0)
        fixed_done = (fixed_sem, 16 * len(fixed))
        ones_set = dve.do(lambda e: e.memset(ones[:, :], 1.0))
        for _ in range(RAW):
            load_unit()
        for q in (pe, dve, act, pool):
            q.wait(fixed_done)
        pe.wait(ones_set)

        square_free = [None, None]
        norm_bank = [None]

        def start_norm():
            norm_bank[0] = take()
            held.add(norm_bank[0])

        def square_in(f, *tokens):
            return copy_act(square[:, f % 2, :], x[:, f, :], *tokens, *square_free,
                            func=ACT.Square)

        def add_square(f, squared):
            b = norm_bank[0]
            if f == 0:
                pe.wait(*bank_free[b])
            pe.wait(squared)
            for tile in range(TT):
                emit = (lambda e, tile=tile: e.matmul(
                    banks[b][:, tile:tile + 1], square[:, f % 2, tile * P:(tile + 1) * P],
                    ones[:, 0:1], start=(f == 0 and tile == 0), stop=(f == KT - 1),
                    skip_group_check=True))
                if tile == TT - 1:
                    square_free[f % 2] = pe.do(emit)
                else:
                    pe.quiet(emit)

        def finish_norm():
            b = norm_bank[0]
            root = copy_act(inv_rms_t, banks[b][:, 0:TT], square_free[(KT - 1) % 2], dve.now(),
                            func=ACT.Sqrt, scale=1.0 / D, bias=EPS)
            bank_free[b] = [root]
            held.discard(b)
            side = recip(inv_rms_t, inv_rms_t, root)
            diagonal = square[:, 0, :].rearrange("p (a b) -> p a b", b=P)
            spread = tt(dve, diagonal, ident.unsqueeze(1).to_broadcast([P, TT, P]),
                        inv_rms_t.unsqueeze(2).to_broadcast([P, TT, P]), ALU.mult, *square_free)
            i = take()
            square_free[0] = psum_group(i, banks[i][:, :], [(ones, square[:, 0, :])], spread)
            done = copy_act(inv_rms, banks[i][:, :], square_free[0])
            bank_free[i] = [done]
            return done, side

        def gained(f, gain, *tokens):
            high = copy_act(xg_high[:, f, :], x[:, f, :], *tokens, scale=col(gain, f))
            return stt(xg_low[:, f, :], x[:, f, :], col(gain, f), xg_high[:, f, :].bitcast(F32), ALU.mult,
                       ALU.subtract, high)

        def first_norm(gain):
            start_norm()
            xg_done = None
            for f in range(KT):
                squared = square_in(f, x_loaded[f // 4])
                xg_done = gained(f, gain)
                add_square(f, squared)
            return xg_done

        def apply_norm(gain, write, rms_done):
            for f in range(KT):
                write(f, stt(x[:, f, :], x[:, f, :], col(gain, f), inv_rms, ALU.mult, ALU.mult,
                             rms_done))

        def output_product(n_units, rhs, k_tiles, factor, next_gain, *tokens):
            pending = None
            start_norm()
            xg_done = None
            for f in range(KT):
                i, done = feature_major(n_units, k_tiles, rhs, *tokens)
                if pending:
                    add_square(*pending)
                added = stt(x[:, f, :], banks[i][:, :], factor, x[:, f, :], ALU.mult, ALU.add, done)
                bank_free[i] = [added]
                pending = (f, square_in(f, added))
                if next_gain:
                    xg_done = gained(f, next_gain, added, pe_used_xg[0])
            add_square(*pending)
            return xg_done

        pe_used_xg = [None]

        pos_f = small[:, 0:TT]
        TWO_PI = 2 * math.pi
        part1 = 6.28125
        part2 = round((TWO_PI - part1) * 2 ** 21) / 2 ** 21
        part3 = TWO_PI - part1 - part2
        ready = dve.do(lambda e: e.tensor_copy(pos_f, positions[:, :]))
        first = phase()
        angle, turns = first.room("angle", TT, 64), first.room("turns", TT, 64)
        for tile in range(TT):
            made = ts(dve, angle[:, tile, :], shared[:, 128:192], pos_f[:, tile:tile + 1], None,
                      ALU.mult, ALU.bypass, ready)
        made = ts(dve, turns, angle, 1.0 / TWO_PI, ROUND, ALU.mult, ALU.add, made)
        made = ts(dve, turns, turns, ROUND, None, ALU.subtract, ALU.bypass, made)
        for part in (part1, part2, part3):
            made = stt(angle, turns, -part, angle, ALU.mult, ALU.add, made)
        made = ts(dve, angle, angle, math.pi * (1 - 1e-7), -math.pi * (1 - 1e-7), ALU.min, ALU.max, made)
        sin_plus = copy_act(sin2[:, :, 64:128], angle, made, func=ACT.Sin)
        sin_minus = copy_act(sin2[:, :, 0:64], angle, func=ACT.Sin, scale=-1.0)
        absolute = copy_act(turns, angle, made, func=ACT.Abs)
        cos_a = copy_act(cos2[:, :, 0:64], turns, absolute, func=ACT.Sin, scale=-1.0, bias=math.pi / 2)
        rotary = copy_act(cos2[:, :, 64:128], turns, absolute, func=ACT.Sin, scale=-1.0,
                          bias=math.pi / 2)

        strip_sem, decay_sem = [sem(f"strips_{i}") for i in range(2)], sem("decays")
        xg_ready = first_norm("gain0")

        def layer(n, xg_ready, next_gain):
            region = phase()
            tok = {name: region.room(name, TT, 512) for name in ("av", "ag", "rq", "rk", "rv", "rg")}
            att2 = region.room("att", 2, 1280)
            rot = region.room("rot", 3, SEQ)
            decays = region.room("decays", RET_HEADS, SEQ)
            y_at = region.at
            qT = region.room("qT", 4, SEQ)
            kT = region.room("kT", 4, SEQ)
            strips = region.room("strips", 4, SEQ)
            prob = region.room("prob", 2, SEQ)
            probT = region.room("probT", 2, SEQ)
            decays_in = pool.dma(lambda e: e.dma_start(decays, t["decays"]), decay_sem, 16 * (n + 1))

            def load_strips(half, *tokens):
                loaded = pool.dma(lambda e: e.dma_start(strips, t["strips"][n, half]),
                                  strip_sem[half], 16 * (n + 1), *tokens)
                return pool.do(lambda e: e.memset(strips[0:64, :, 448:512], NEG_INF), loaded)

            strips_in = [load_strips(0), None]

            rms_done = side = None
            qk_done = None
            for f in range(8):
                i, done = feature_major(1, KT, xg_tile, xg_ready)
                if f == 0:
                    rms_done, side = finish_norm()
                out = qT[:, f, :] if f < 4 else kT[:, f - 4, :]
                qk_done = stt(out, banks[i][:, :], ATT_DIM ** -0.5 if f < 4 else 1.0, inv_rms,
                              ALU.mult, ALU.mult, done, rms_done)
                bank_free[i] = [qk_done]

            landed = {}

            def group_steps(names):
                for name in names:
                    yield from token_major()
                    out, done = token_major_result
                    for tile, i in enumerate(out):
                        landed[name] = copy_act(tok[name][:, tile, :], banks[i][:, :], done, side,
                                                func=ACT.Silu if name in ("ag", "rg") else ACT.Identity,
                                                scale=inv_rms_t[:, tile:tile + 1])
                        bank_free[i] = [landed[name]]
                    pe_used_xg[0] = pe.now()
                    yield

            for _ in group_steps(("rq", "rk", "av", "ag")):
                pass
            filler = group_steps(("rv", "rg"))

            turned = {}
            rot_free = [None]
            for name in ("rq", "rk"):
                for tile in range(TT):
                    src = tok[name][:, tile, :].rearrange("p (h d) -> p h d", d=P)
                    a, b, r = (rot[:, s, :].rearrange("p (h d) -> p h d", d=P) for s in range(3))
                    c = cos2[:, tile, :].unsqueeze(1).to_broadcast([P, 4, P])
                    s_lo = sin2[:, tile, 0:64].unsqueeze(1).to_broadcast([P, 4, 64])
                    s_hi = sin2[:, tile, 64:128].unsqueeze(1).to_broadcast([P, 4, 64])
                    m0 = tt(dve, a, src, c, ALU.mult, landed[name], rotary)
                    tt(dve, b[:, :, 0:64], src[:, :, 64:128], s_lo, ALU.mult)
                    m1 = tt(dve, b[:, :, 64:128], src[:, :, 0:64], s_hi, ALU.mult)
                    m2 = tt(dve, r, a, b, ALU.add, m1, rot_free[0])
                    i = take()
                    rot_free[0] = transposes(
                        i, [(banks[i][:, h * P:(h + 1) * P], rot[:, 2, h * P:(h + 1) * P])
                            for h in range(4)], m2)
                    turned[name] = copy_act(tok[name][:, tile, :], banks[i][:, :], rot_free[0], m2)
                    bank_free[i] = [turned[name]]

            steps = [(h, q) for h in range(ATT_HEADS) for q in range(TT)]
            state = {}

            def scores(h, q):
                r = slice(64 * (h % 2), 64 * (h % 2) + 64)
                i = take()
                keys = (q + 1) * P
                done = psum_group(i, banks[i][:, 0:keys],
                                  [(qT[r, h // 2, q * P:(q + 1) * P], kT[r, h // 2, 0:keys])], qk_done)
                if (h, q) == (4, 0):
                    strips_in[1] = load_strips(1, state[(3, 3)]["biased"])
                s = state[(h, q)] = {}
                buf = (h * TT + q) % 2
                stat = 8 + 4 * ((h * TT + q) % 4)
                s["p"], s["stat"] = prob[:, buf, 0:keys], stat
                before = state.get(prev(h, q, 2))
                s["biased"] = dve.do(lambda e: e.tensor_tensor_reduce(
                    out=s["p"], in0=banks[i][:, 0:keys], in1=strips[:, h % 4, 512 - keys:512],
                    scale=1.0, scalar=-3e38, op0=ALU.add, op1=ALU.max,
                    accum_out=small[:, stat:stat + 1]), done, strips_in[h // 4],
                    before and before["turned"])
                bank_free[i] = [s["biased"]]
                minus = ts(dve, small[:, stat + 1:stat + 2], small[:, stat:stat + 1], -1.0, None,
                           ALU.mult, ALU.bypass, s["biased"])
                s["exp"] = copy_act(s["p"], s["p"], minus, func=ACT.Exp,
                                    bias=small[:, stat + 1:stat + 2], accum=small[:, stat + 2:stat + 3])

            def prev(h, q, n):
                k = h * TT + q - n
                return (k // TT, k % TT)

            def turn_probs(h, q):
                s = state[(h, q)]
                i = take()
                s["turned"] = transposes(i, [(banks[i][:, k * P:(k + 1) * P],
                                              s["p"][:, k * P:(k + 1) * P]) for k in range(q + 1)],
                                         s["exp"])
                before = state.get(prev(h, q, 2))
                s["buf"] = probT[:, (h * TT + q) % 2, :]
                s["probT"] = copy_act(s["buf"][:, 0:(q + 1) * P], banks[i][:, 0:(q + 1) * P],
                                      s["turned"], before and before["used"])
                bank_free[i] = [s["probT"]]
                s["inv"] = recip(small[:, s["stat"] + 3:s["stat"] + 4],
                                 small[:, s["stat"] + 2:s["stat"] + 3], s["exp"])

            def values(h, q):
                s = state[(h, q)]
                i = take()
                s["used"] = psum_group(i, banks[i][:, 0:ATT_DIM],
                                       [(s["buf"][:, k * P:(k + 1) * P],
                                         tok["av"][:, k, h * ATT_DIM:(h + 1) * ATT_DIM])
                                        for k in range(q + 1)], s["probT"], landed["av"])
                gate = tok["ag"][:, q, h * ATT_DIM:(h + 1) * ATT_DIM]
                s["out"] = stt(gate, banks[i][:, 0:ATT_DIM], small[:, s["stat"] + 3:s["stat"] + 4], gate,
                               ALU.mult, ALU.mult, s["used"], s["inv"], landed["ag"])
                bank_free[i] = [s["out"]]

            for n_step in range(len(steps) + 2):
                if n_step % 4 == 1:
                    next(filler, None)
                if n_step < len(steps):
                    scores(*steps[n_step])
                if 1 <= n_step <= len(steps):
                    turn_probs(*steps[n_step - 1])
                if n_step >= 2:
                    values(*steps[n_step - 2])
            for _ in filler:
                pass
            att_out = state[steps[-1]]["out"]

            offs = [0, 512, 896, 1152]
            att_free, weighted = [None, None], {}
            ret_out = None

            def ret_scores(h):
                att = att2[:, h % 2, :]
                for j in range(TT):
                    width = (TT - j) * P
                    i = take()
                    kh = tok["rk"][:, j, h * P:(h + 1) * P]
                    qh = tok["rq"][:, j:TT, h * P:(h + 1) * P]
                    done = psum_group(i, banks[i][:, 0:width].rearrange("p (a b) -> p a b", b=P),
                                      [(kh, qh)], turned["rk"], turned["rq"])
                    weighted[h] = tt(dve, att[:, offs[j]:offs[j] + width], banks[i][:, 0:width],
                                     decays[:, h, 0:width], ALU.mult, done, decays_in, att_free[h % 2])
                    bank_free[i] = [weighted[h]]

            def ret_values(h):
                att = att2[:, h % 2, :]
                i = take()
                held.add(i)
                for q in range(TT):
                    done = psum_group(i, banks[i][:, q * P:(q + 1) * P],
                                      [(att[:, offs[j] + (q - j) * P:offs[j] + (q - j + 1) * P],
                                        tok["rv"][:, j, h * P:(h + 1) * P]) for j in range(q + 1)],
                                      weighted[h], landed["rv"])
                att_free[h % 2] = done
                stat = 32 + 12 * h
                ss, root, inv = (small[:, stat + 4 * k:stat + 4 * k + 4] for k in range(3))
                for q in range(TT):
                    summed = copy_act(rot[:, 0, q * P:(q + 1) * P], banks[i][:, q * P:(q + 1) * P],
                                      done, rot_free[0], func=ACT.Square, accum=ss[:, q:q + 1])
                rooted = copy_act(root, ss, summed, func=ACT.Sqrt, scale=1.0 / RET_DIM, bias=EPS)
                inverted = recip(inv, root, rooted)
                for q in range(TT):
                    gate = tok["rg"][:, q, h * P:(h + 1) * P]
                    out = stt(gate, banks[i][:, q * P:(q + 1) * P], inv[:, q:q + 1], gate, ALU.mult,
                              ALU.mult, inverted, landed["rg"])
                bank_free[i] = [out]
                held.discard(i)
                return out

            for h in range(RET_HEADS + 1):
                if h < RET_HEADS:
                    ret_scores(h)
                if h:
                    ret_out = ret_values(h - 1)

            fence()
            over = Region(y_at, stay.end)
            y_high, y_low = (over.room(part, KT, SEQ, dt=F32R) for part in ("y_high", "y_low"))
            for half, (name, made) in enumerate((("ag", att_out), ("rg", ret_out))):
                for tile in range(TT):
                    i = take()
                    done = transposes(i, [(banks[i][:, f * P:(f + 1) * P],
                                           tok[name][:, tile, f * P:(f + 1) * P]) for f in range(4)], made)
                    part = (slice(None), slice(4 * half, 4 * half + 4), slice(tile * P, (tile + 1) * P))
                    y_done = split_from_bank(y_high[part], y_low[part], i, done)
            return output_product(1, lambda k: (y_high[:, k, :], y_low[:, k, :]), KT, 1.0, next_gain,
                                  y_done)

        xg_ready = layer(0, xg_ready, "gain1")
        layer(1, xg_ready, None)

        rms_done, _ = finish_norm()
        made = {}
        apply_norm("final_gain", lambda f, token: made.__setitem__(f, token), rms_done)

        def norm_of_stream(gain):
            start_norm()
            last = None
            for f in range(KT):
                squared = square_in(f, made[f])
                last = gained(f, gain, pe_used_xg[0])
                add_square(f, squared)
            return last

        xg_ready = norm_of_stream("norm_ffn1")

        def feed_forward(which, xg_ready, next_gain):
            region = phase()
            h_high, h_low = (region.room(part, FT, SEQ, dt=F32R) for part in ("h_high", "h_low"))
            gate = region.room("gate", 2, SEQ)
            up = region.room("up", 2, SEQ)
            rms_done = None
            for f in range(FT):
                b = f % 2
                ig, gate_done = feature_major(1, KT, xg_tile, xg_ready)
                if f == 0:
                    rms_done, _ = finish_norm()
                iu, up_done = feature_major(1, KT, xg_tile)
                gated = tt(dve, gate[:, b, :], banks[ig][:, :], inv_rms, ALU.mult, gate_done, rms_done)
                bank_free[ig] = [gated]
                silu = copy_act(gate[:, b, :], gate[:, b, :], gated, func=ACT.Silu)
                upped = tt(dve, up[:, b, :], banks[iu][:, :], inv_rms, ALU.mult, up_done)
                bank_free[iu] = [upped]
                product = tt(dve, up[:, b, :], gate[:, b, :], up[:, b, :], ALU.mult, silu, upped)
                rounded = copy_act(h_high[:, f, :], up[:, b, :], product)
                h_done = tt(dve, h_low[:, f, :], up[:, b, :], h_high[:, f, :].bitcast(F32), ALU.subtract,
                            rounded)
            pe_used_xg[0] = pe.now()
            return output_product(3, lambda k: (h_high[:, k, :], h_low[:, k, :]), FT, 0.5, next_gain,
                                  h_done)

        def over_tiles(ap, n=TT):
            return ap.unsqueeze(1).to_broadcast([P, n, ap.shape[-1]])

        def mixers(xg_ready):
            region = phase()
            mixer = region.room("mixer", N_MIXER)
            rows = region.room("rows", 4, G)
            lora = region.room("lora", 2, G)
            gla_w2 = region.room("gla_w2", G)
            pool_w = region.room("pool_w", 2, 64)
            y_pool = region.room("y_pool", 2, SEQ)
            ga_sb = region.room("ga", SEQ)
            y_tok = {name: region.room(f"y_{name}", TT, G) for name in ("hgrn", "rwkv", "gla")}
            mixer_sem = sem("mixer_loads")
            loads = [(mixer, t["mixer"]), (rows, t["rows"]), (lora, t["lora"]),
                     (gla_w2[0:16, :], t["gla_w2"]), (pool_w, t["pool_w"])]
            for out, src in loads:
                pool.dma(lambda e, o=out, s=src: e.dma_start(o, s), mixer_sem, 0)
            mixer_in = (mixer_sem, 16 * len(loads))
            for q in (pe, dve, act, pool):
                q.wait(mixer_in)

            def table(name):
                at, n = MIXER[name]
                return mixer[:, at:at + n]

            start = region.at
            same_head = table("same_head")
            norms = []

            def projected():
                i, done = feature_major(1, KT, xg_tile, xg_ready)
                if not norms:
                    norms.extend(finish_norm())
                return i, done

            pad = 16
            p_in, s2, s4 = (region.room(n, 2, SEQ + pad) for n in ("p_in", "s2", "s4"))
            s8, s16 = (region.room(n, SEQ + pad) for n in ("s8", "s16"))
            window, inv_count = (region.room(n, 2, SEQ) for n in ("window", "inv_count"))
            count_in = pool.dma(lambda e: e.dma_start(inv_count, t["inv_count"]), sem("count_load"), 16)
            dve.do(lambda e: e.memset(p_in[:, :, 0:pad], 0.0))
            for f in range(2):
                i, done = projected()
                p_done = tt(dve, p_in[:, f, pad:], banks[i][:, :], inv_rms, ALU.mult, done, norms[0])
                bank_free[i] = [p_done]
            w = SEQ + pad
            tt(dve, s2[:, :, 1:w], p_in[:, :, 1:w], p_in[:, :, 0:w - 1], ALU.add)
            tt(dve, s4[:, :, 3:w], s2[:, :, 3:w], s2[:, :, 1:w - 2], ALU.add)
            tt(dve, s8[:, 7:w], s4[:, 1, 7:w], s4[:, 1, 3:w - 4], ALU.add)
            tt(dve, s16[:, 15:w], s8[:, 15:w], s8[:, 7:w - 8], ALU.add)
            for rows64, f, sums in ((slice(0, 64), 0, s2[:, 0]), (slice(64, 128), 0, s4[:, 0]),
                                    (slice(0, 64), 1, s8), (slice(64, 128), 1, s16)):
                tt(dve, window[rows64, f, :], sums[rows64, pad:], inv_count[rows64, f, :], ALU.mult,
                   count_in)
            pooled = tt(dve, window, window, p_in[:, :, pad:], ALU.subtract)
            for f in range(2):
                for r in (slice(0, 64), slice(64, 128)):
                    i = take()
                    done = psum_group(i, banks[i][r, :], [(pool_w[r, f, :], window[r, f, :])], pooled)
                    bank_free[i] = [ts(dve, y_pool[r, f, :], banks[i][r, :], col("pool_b", f, r),
                                       col("pool_scale", f, r), ALU.add, ALU.mult, done)]

            def to_token(y, f, y_tile, *tokens):
                i = take()
                done = transposes(i, [(banks[i][:, tile * P:(tile + 1) * P],
                                       y[:, tile, f * P:(f + 1) * P]) for tile in range(TT)], *tokens)
                return split_from_bank(y_high[:, y_tile, :], y_low[:, y_tile, :], i, done)

            def head_tile(h):
                return slice(64 * (h % 2), 64 * (h % 2) + 64), h // 2

            tiles4 = lambda ap: ap.rearrange("p (a b) -> p a b", b=P)
            flat = lambda ap: ap.rearrange("p a b -> p (a b)")

            def halves(ap, m, right, dims="p (n c) -> p n c"):
                v = ap.rearrange(dims, c=2 * m) if "t" not in dims else ap.rearrange(dims, t=TT, c=2 * m)
                at = slice(m, 2 * m) if right else slice(0, m)
                return v[:, :, at] if len(v.shape) == 3 else v[:, :, :, at]

            def pairs(m):
                n = LEVELS.index(m)
                return table("pairs")[:, n * P:(n + 1) * P]

            def pair_mask(m):
                v = halves(pairs(m), m, True)
                return v.unsqueeze(1).to_broadcast([P, TT, v.shape[1], m])

            region = Region(start, stay.end)
            first_at = region.at
            operands = {}
            for name in ("hgrn", "gla"):
                q2, k2, c2 = (region.room(f"{n}_{name}", 2, SEQ) for n in "qkc")
                operands[name] = (q2, k2, c2, region.room(f"v_{name}", TT, 512))
                if name == "hgrn":
                    second_at = region.at
            E2 = [region.room("E", 2, SEQ) for _ in range(2)]
            near = region.room("near", 4, TT * P)
            far = region.room("far", 4, 768)
            v_done, projected_at = {}, {}

            def linear_attention(name, y, fill):
                q2, k2, c2, v2 = operands[name]
                for f in range(2):
                    c_done = dve.do(lambda e, f=f: e.tensor_tensor_scan(
                        c2[:, f, :], table("restart"), c2[:, f, :], 0.0, ALU.mult, ALU.add))
                for h in range(4):
                    r, g = head_tile(h)
                    i = take()
                    for tile in range(TT):
                        c = slice(tile * P, (tile + 1) * P)
                        done = psum_group(i, banks[i][:, c], [(k2[r, g, c], q2[r, g, c])], c_done)
                    bank_free[i] = [tt(dve, tiles4(near[:, h, :]), tiles4(banks[i][:, :]), over_tiles(ident),
                                       ALU.mult, done)]
                levels = (32, 16, 8, 4, 2, 1, 64, 128, 256)
                e_free, factors = [None, None], {}

                def factor(n):
                    m, e = levels[n], E2[n % 2]
                    cl, cr, el, er = (halves(flat(ap), m, side) for ap in (c2, e) for side in (False, True))
                    ql, kl = halves(flat(q2), m, True), halves(flat(k2), m, False)
                    nb = SEQ // m
                    if m > 64:
                        right = halves(flat(c2), m // 2, True)
                        last = halves(flat(c2), m // 2, False)[:, :, m // 2 - 1:m // 2]
                        tt(dve, right, right, last.to_broadcast([P, 2 * nb, m // 2]), ALU.add, act.now())
                    border = cl[:, :, m - 1:m].to_broadcast([P, nb, m])
                    made = tt(dve, el, border, cl, ALU.subtract, e_free[n % 2])
                    if m < 64:
                        made = tt(dve, er, cr, border, ALU.subtract)
                        made = copy_act(flat(e), flat(e), made, func=ACT.Exp)
                    else:
                        copy_act(er, cr, made, func=ACT.Exp)
                        made = copy_act(el, el, func=ACT.Exp)
                    left = tt(pool, el, el, kl, ALU.mult, made)
                    right = tt(dve, er, er, ql, ALU.mult, made)
                    factors[n] = (left, right)

                def scores(n):
                    m, e = levels[n], E2[n % 2]
                    for h in range(4):
                        r, g = head_tile(h)
                        i = take()
                        if m <= 64:
                            for tile in range(TT):
                                et = e[r, g, tile * P:(tile + 1) * P]
                                out = banks[i][:, tile * 64:(tile + 1) * 64]
                                done = psum_group(i, out.rearrange("p (n c) -> p n c", c=m),
                                                  [(et, halves(et, m, True))], *factors[n])
                            data = banks[i][:, 0:256].rearrange("p (t n c) -> p t n c", t=TT, c=m)
                            out = halves(near[:, h, :], m, True, "p (t n c) -> p t n c")
                            bank_free[i] = [dve.do(lambda e, o=out, d=data, m=m: e.copy_predicated(
                                o, pair_mask(m).bitcast(I32), d), done)]
                        elif m == 128:
                            for n_far, key in enumerate((0, 2)):
                                done = psum_group(i, banks[i][:, n_far * P:(n_far + 1) * P],
                                                  [(e[r, g, key * P:(key + 1) * P],
                                                    e[r, g, (key + 1) * P:(key + 2) * P])], *factors[n])
                            bank_free[i] = [copy_act(far[:, h, 0:256], banks[i][:, 0:256], done)]
                        else:
                            for key in range(2):
                                done = psum_group(i, banks[i][:, key * 256:(key + 1) * 256],
                                                  [(e[r, g, key * P:(key + 1) * P], e[r, g, 256:512])],
                                                  *factors[n])
                            bank_free[i] = [copy_act(far[:, h, 256:768], banks[i][:, :], done)]
                    e_free[n % 2] = done

                factor(0)
                for n in range(len(levels)):
                    if n + 1 < len(levels):
                        factor(n + 1)
                    fill(n)
                    scores(n)

                scores_done = (dve.now(), act.now())
                for half in range(2):
                    i = take()
                    for tile in (2 * half, 2 * half + 1):
                        for h in range(4):
                            v_cols = slice(h * 64, (h + 1) * 64)
                            products = [(near[:, h, tile * P:(tile + 1) * P], v2[:, tile, v_cols])]
                            if tile % 2:
                                n_far = tile // 2
                                products.append((far[:, h, n_far * P:(n_far + 1) * P],
                                                 v2[:, tile - 1, v_cols]))
                            if tile >= 2:
                                for key in range(2):
                                    at = 256 + key * 256 + (tile - 2) * P
                                    products.append((far[:, h, at:at + P], v2[:, key, v_cols]))
                            at = (tile % 2) * G + h * 64
                            done = psum_group(i, banks[i][:, at:at + 64], products, *scores_done,
                                              v_done[name])
                    o_done = copy_act(y[:, 2 * half:2 * half + 2, :],
                                      banks[i][:, :].rearrange("p (a b) -> p a b", b=G), done)
                    bank_free[i] = [o_done]
                squares = E2[0].rearrange("p a b -> p (a b)").rearrange("p (a b) -> p a b", b=G)
                tt(dve, squares, y, y, ALU.mult, o_done, e_free[0])
                width = G if name == "hgrn" else 64
                n_norms = TT * G // width
                ms = small[:, 128:128 + n_norms]
                split = lambda ap: ap.rearrange("p t (h d) -> p (t h) d", d=width)
                reduced = dve.do(lambda e: e.tensor_reduce(ms, split(squares), AX_X, ALU.add))
                root = copy_act(ms, ms, reduced, func=ACT.Sqrt, scale=1.0 / width, bias=EPS)
                recip(ms, ms, root)
                tt(dve, split(y), split(y), ms.unsqueeze(2).to_broadcast([P, n_norms, width]), ALU.mult)
                tt(dve, y, y, over_tiles(rows[:, 0 if name == "hgrn" else 3, :]), ALU.mult)
                return tt(dve, y, y, v2[:, :, G:], ALU.mult)

            def value_steps(name, func):
                yield from token_major()
                out, done = token_major_result
                v2 = operands[name][3]
                for tile, i in enumerate(out):
                    s = inv_rms_t[:, tile:tile + 1]
                    copy_act(v2[:, tile, 0:G], banks[i][:, 0:G], done, norms[1], scale=s)
                    v_done[name] = copy_act(v2[:, tile, G:], banks[i][:, G:], func=func, scale=s)
                    bank_free[i] = [v_done[name]]
                yield

            lb, e_lb, keep_lb = small[:, 160:162], small[:, 162:164], small[:, 164:166]
            logits = cols[:, COLS["lb_logits"][0]:COLS["lb_logits"][0] + 2]
            centred = tt(dve, e_lb, logits, logits, ALU.subtract)
            raised = copy_act(e_lb, e_lb, centred, func=ACT.Exp)
            recip(lb, e_lb, raised)
            tt(dve, e_lb, e_lb, lb, ALU.mult)
            tt(dve, lb, e_lb, e_lb, ALU.subtract)
            ts(dve, keep_lb, lb, -1.0, 1.0, ALU.mult, ALU.add)

            fence()
            q2, k2, c2, _ = operands["hgrn"]
            low = E2[0]
            for f in range(2):
                i, done = projected()
                got = tt(dve, q2[:, f, :], banks[i][:, :], inv_rms, ALU.mult, done)
                bank_free[i] = [got]
                bent = copy_act(q2[:, f, :], q2[:, f, :], got, func=ACT.Silu)
                i, done = projected()
                got = tt(dve, k2[:, f, :], banks[i][:, :], inv_rms, ALU.mult, done)
                bank_free[i] = [got]
                sig = copy_act(c2[:, f, :], k2[:, f, :], got, func=ACT.Sigmoid)
                ts(dve, q2[:, f, :], q2[:, f, :], 0.125, None, ALU.mult, ALU.bypass, bent)
                ts(dve, c2[:, f, :], c2[:, f, :], keep_lb[:, f:f + 1], lb[:, f:f + 1], ALU.mult, ALU.add, sig)
                ts(dve, k2[:, f, :], c2[:, f, :], -1.0, 1.0, ALU.mult, ALU.add)
                ts(dve, low[:, f, :], c2[:, f, :], 2.0 ** -60, None, ALU.max, ALU.bypass)
                ts(dve, c2[:, f, :], c2[:, f, :], 1e-30, 2.0 ** 60, ALU.max, ALU.mult)
                got = ts(dve, c2[:, f, :], c2[:, f, :], 1.0, None, ALU.min, ALU.bypass)
            copy_act(flat(low), flat(low), got, func=ACT.Ln)
            logs = copy_act(flat(c2), flat(c2), func=ACT.Ln)
            tt(dve, c2, c2, low, ALU.add, logs)

            def gla_steps():
                q2, k2, c2, _ = operands["gla"]
                for f in range(2):
                    i, done = projected()
                    bank_free[i] = [stt(q2[:, f, :], banks[i][:, :], 0.125, inv_rms, ALU.mult, ALU.mult,
                                        done)]
                    yield
                    i, done = projected()
                    bank_free[i] = [tt(dve, k2[:, f, :], banks[i][:, :], inv_rms, ALU.mult, done)]
                    yield
                i, done = projected()
                ga = ga_sb[0:16, :]
                ga_done = tt(dve, ga, banks[i][0:16, :], inv_rms[0:16, :], ALU.mult, done)
                bank_free[i] = [ga_done]
                for f in range(2):
                    size = operands["gla"][3][:, f, :]
                    i = take()
                    done = psum_group(i, banks[i][:, :], [(gla_w2[0:16, f * P:(f + 1) * P], ga)], ga_done)
                    low = ts(dve, c2[:, f, :], banks[i][:, :], col("gla_b", f), 0.0, ALU.add, ALU.min, done)
                    sized = copy_act(size, banks[i][:, :], low, func=ACT.Abs, bias=col("gla_b", f))
                    bank_free[i] = [sized]
                    copy_act(size, size, func=ACT.Exp, scale=-1.0)
                    logs = copy_act(size, size, func=ACT.Ln, bias=1.0)
                    tt(dve, c2[:, f, :], c2[:, f, :], size, ALU.subtract, logs)
                    ts(dve, c2[:, f, :], c2[:, f, :], 1.0 / 16, None, ALU.mult, ALU.bypass)
                yield

            values_h, others = value_steps("hgrn", ACT.Sigmoid), gla_steps()

            def fill_hgrn(n):
                next(values_h if n < 4 else others)

            linear_attention("hgrn", y_tok["hgrn"], fill_hgrn)

            fence()
            region = Region(first_at, second_at)
            mixed = region.room("mixed", 8, SEQ)
            shifted = region.room("shifted", 2, SEQ)
            keep = small[:, 100:108]
            kept = ts(dve, keep, cols[:, COLS["rwkv_mu"][0]:COLS["rwkv_mu"][0] + 8], -1.0, 1.0, ALU.mult,
                      ALU.add)
            mix = [None]

            def rwkv_steps():
                for f in range(8):
                    i, done = projected()
                    s = shifted[:, f % 2, :]
                    scaled = tt(dve, s, banks[i][:, :], inv_rms, ALU.mult, done, act.now())
                    bank_free[i] = [scaled]
                    own = copy_act(mixed[:, f, :], s, scaled, kept, scale=keep[:, f:f + 1])
                    mix[0] = stt(mixed[:, f, 1:], s[:, 0:SEQ - 1], col("rwkv_mu", f), mixed[:, f, 1:],
                                 ALU.mult, ALU.add, own)
                    yield

            values_g, projections = value_steps("gla", ACT.Silu), rwkv_steps()

            def fill_gla(n):
                if n < 4:
                    next(values_g)
                    if n % 2:
                        next(projections)
                else:
                    next(projections)

            linear_attention("gla", y_tok["gla"], fill_gla)
            for _ in projections:
                pass
            pe_used_xg[0] = pe.now()

            fence()
            free_xg = Region(xg_at, phase_at)
            kkE, rE, bI, kI = (free_xg.room(n, 2, SEQ) for n in ("kkE", "rE", "bI", "kI"))
            tokA = free_xg.room("tokA", TT, 512)
            tokB = free_xg.room("tokB", TT, 512)
            kept_bytes = 2 * 4 * 2 * SEQ
            last = Region(stay.end - kept_bytes, stay.end)
            g_tok = last.room("g_tok", TT, G)
            eB = last.room("eB", 2, SEQ)
            region = Region(second_at, stay.end - kept_bytes)
            sigma, cum, eI, a_gate, kk, tmp = (region.room(n, 2, SEQ) for n in
                                               ("sigma", "cum", "eI", "a_gate", "kk", "tmp"))
            mix = mix[0]
            rr, rk, rv = mixed[:, 0:2, :], mixed[:, 2:4, :], mixed[:, 4:6, :]
            bent = copy_act(mixed[0:64, 6, :], mixed[0:64, 6, :], mix, func=ACT.Tanh)
            gate_in = copy_act(mixed[:, 7, :], mixed[:, 7, :], mix, func=ACT.Sigmoid)
            for f in range(2):
                for out, r, bias in ((sigma, slice(0, 64), "rwkv_w0"), (a_gate, slice(64, 128), "rwkv_a0")):
                    i = take()
                    done = psum_group(i, banks[i][:, :], [(lora[r, 0, f * P:(f + 1) * P], mixed[r, 6, :])],
                                      bent)
                    sig = copy_act(out[:, f, :], banks[i][:, :], done, func=ACT.Sigmoid, bias=col(bias, f))
                    bank_free[i] = [sig]
            for half in range(2):
                i = take()
                for j in range(2):
                    tile = 2 * half + j
                    done = psum_group(i, banks[i][:, j * G:(j + 1) * G],
                                      [(mixed[:, 7, tile * P:(tile + 1) * P], lora[:, 1, :])], gate_in)
                g_done = copy_act(g_tok[:, 2 * half:2 * half + 2, :],
                                  banks[i][:, :].rearrange("p (a b) -> p a b", b=G), done)
                bank_free[i] = [g_done]
            for f in range(2):
                scanned = dve.do(lambda e, f=f: e.tensor_tensor_scan(
                    cum[:, f, :], table("restart"), sigma[:, f, :], 0.0, ALU.mult, ALU.add), sig)
            before = tt(dve, tmp, cum, sigma, ALU.subtract)
            copy_act(eB, cum, scanned, func=ACT.Exp, scale=-HALF_E)
            copy_act(eI, cum, scanned, func=ACT.Exp, scale=HALF_E)
            exps = copy_act(tmp, tmp, before, func=ACT.Exp, scale=-HALF_E)
            for f in range(2):
                ts(dve, kk[:, f, :], rk[:, f, :], col("rwkv_k_k", f), None, ALU.mult, ALU.bypass)
            sq = tt(dve, kI, kk, kk, ALU.mult)
            for f in range(2):
                i = take()
                done = psum_group(i, banks[i][:, :], [(same_head, kI[:, f, :])], sq)
                floored = ts(dve, kI[:, f, :], banks[i][:, :], 1e-24, None, ALU.max, ALU.bypass, done)
                bank_free[i] = [floored]
            root = copy_act(kI, kI, floored, func=ACT.Sqrt)
            recip(kI, kI, root)
            tt(dve, kk, kk, kI, ALU.mult)
            tt(dve, kkE, kk, tmp, ALU.mult, exps)
            tt(dve, bI, kk, a_gate, ALU.mult)
            tt(dve, bI, bI, eI, ALU.mult)
            for f in range(2):
                ts(dve, tmp[:, f, :], a_gate[:, f, :], 1.0, col("rwkv_k_a", f), ALU.subtract, ALU.mult)
                stt(rk[:, f, :], tmp[:, f, :], 1.0, rk[:, f, :], ALU.add, ALU.mult)
                stt(sigma[:, f, :], rr[:, f, :], col("rwkv_r_k", f), rk[:, f, :], ALU.mult, ALU.mult)
            tt(dve, kI, rk, eI, ALU.mult)
            scaled = tt(dve, rE, rr, eB, ALU.mult)
            for tile in range(TT):
                c = slice(tile * P, (tile + 1) * P)
                for out, (a, b) in ((tokA, (kkE, kI)), (tokB, (bI, rv))):
                    i = take()
                    done = transposes(i, [(banks[i][:, n * P:(n + 1) * P], s[:, n % 2, c])
                                          for n, s in enumerate((a, a, b, b))], scaled)
                    tok_done = copy_act(out[:, tile, :], banks[i][:, :], done)
                    bank_free[i] = [tok_done]
            bonus = small[:, 112:128]
            i = take()
            for tile in range(TT):
                for f in range(2):
                    at = 4 * tile + 2 * f
                    done = psum_group(i, banks[i][:, at:at + 2],
                                      [(sigma[:, f, tile * P:(tile + 1) * P], same_head[:, 0:P:64])], scaled)
            bonus_done = copy_act(bonus, banks[i][:, 0:16], done)
            bank_free[i] = [bonus_done]

            fence()
            region = Region(first_at, stay.end - kept_bytes)
            M_rk, M_rb, XT = (region.room(n, 4, TT * P) for n in ("M_rk", "M_rb", "XT"))
            AT, X, Pm, CT, A_ak = (region.room(n, 2, TT * P) for n in ("AT", "X", "Pm", "CT", "A_ak"))
            Gv = region.room("Gv", 2, TT * 64)
            W1 = region.room("W1", TT, G)
            W2T = region.room("W2T", TT, 2, P)

            def gram(h, left, right):
                r, f = slice(64 * (h % 2), 64 * (h % 2) + 64), h // 2
                i = take()
                for tile in range(TT):
                    c = slice(tile * P, (tile + 1) * P)
                    done = psum_group(i, banks[i][:, c], [(left[r, f, c], right[r, f, c])], scaled)
                return i, done

            def masked(out, h, left, right, mask):
                i, done = gram(h, left, right)
                made = tt(dve, tiles4(out), tiles4(banks[i][:, :]), over_tiles(mask), ALU.mult, done)
                bank_free[i] = [made]
                return made

            def per_tile(left, right, *tokens, width=P, out=lambda b, tile: b[:, tile * P:(tile + 1) * P]):
                i = take()
                for tile in range(TT):
                    done = psum_group(i, out(banks[i], tile), [(left(tile), right(tile))], *tokens)
                return i, done

            def tile_of(ap):
                return lambda tile: ap[:, tile * P:(tile + 1) * P]

            for pair in (0, 2):
                made = {}
                for s in range(2):
                    h = pair + s
                    masked(X[:, s, :], h, kkE, bI, table("pairs_ts"))
                    stt(tiles4(X[:, s, :]), tiles4(X[:, s, :]), -1.0, over_tiles(ident), ALU.mult, ALU.add)
                    masked(AT[:, s, :], h, bI, kkE, table("before"))
                    tt(dve, tiles4(XT[:, h, :]), tiles4(AT[:, s, :]), over_tiles(pairs(1)), ALU.mult)
                    made[s] = stt(tiles4(XT[:, h, :]), tiles4(XT[:, h, :]), -1.0, over_tiles(ident),
                                  ALU.mult, ALU.add)
                    masked(A_ak[:, s, :], h, kI, kkE, table("before"))
                    masked(M_rk[:, h, :], h, kI, rE, table("upto"))
                    m_done = masked(M_rb[:, h, :], h, bI, rE, table("upto"))
                for m in (2, 4, 8, 16, 32):
                    for s in range(2):
                        h = pair + s
                        below = tt(pool, tiles4(CT[:, s, :]), tiles4(AT[:, s, :]), over_tiles(pairs(m)),
                                   ALU.mult, made[s], pe.now())
                        i, done = per_tile(tile_of(CT[:, s, :]), tile_of(X[:, s, :]), below, made[s])
                        p_done = copy_act(Pm[:, s, :], banks[i][:, :], done)
                        bank_free[i] = [p_done]
                        half_of = lambda ap, right, m=m: lambda tile: halves(tile_of(ap)(tile), m, right)
                        compact = lambda b, tile, m=m: b[:, tile * 64:(tile + 1) * 64].rearrange(
                            "p (n c) -> p n c", c=m)
                        def update(ap, right, i, done, m=m):
                            part = halves(ap, m, right)
                            bank_free[i] = [tt(dve, part, part, banks[i][:, 0:256].rearrange(
                                "p (n c) -> p n c", c=m), ALU.subtract, done)]
                            return bank_free[i][0]
                        if m < 32:
                            i, done = per_tile(tile_of(XT[:, h, :]), half_of(Pm[:, s, :], False), p_done,
                                               out=compact)
                            update(X[:, s, :], False, i, done)
                        i, done = per_tile(tile_of(Pm[:, s, :]), half_of(XT[:, h, :], True), p_done,
                                           out=compact)
                        made[s] = update(XT[:, h, :], True, i, done)
                for s in range(2):
                    h = pair + s
                    v_cols = slice(G + h * 64, G + (h + 1) * 64)
                    cols64 = lambda b, tile: b[:, tile * 64:(tile + 1) * 64]
                    i, done = per_tile(tile_of(A_ak[:, s, :]), lambda tile: tokB[:, tile, v_cols], m_done,
                                       tok_done, out=cols64)
                    g_made = copy_act(Gv[:, s, :], banks[i][:, 0:TT * 64], done)
                    bank_free[i] = [g_made]
                    i, done = per_tile(tile_of(XT[:, h, :]),
                                       lambda tile: Gv[:, s, tile * 64:(tile + 1) * 64], g_made, made[s],
                                       out=cols64)
                    w1_done = copy_act(W1[:, :, h * 64:(h + 1) * 64],
                                       banks[i][:, 0:TT * 64].rearrange("p (a b) -> p a b", b=64), done,
                                       scale=-1.0)
                    bank_free[i] = [w1_done]
                    r = slice(64 * s, 64 * s + 64)
                    i, done = per_tile(lambda tile: tokA[:, tile, h * 64:(h + 1) * 64], tile_of(XT[:, h, :]),
                                       out=lambda b, tile: b[r, tile * P:(tile + 1) * P])
                    w2_done = copy_act(W2T[r, :, h // 2, :], tiles4(banks[i][r, :]), done)
                    bank_free[i] = [w2_done]

            fence()
            U = kkE.rearrange("p a b -> p (a b)").rearrange("p (a b) -> p a b", b=G)
            out_r = y_tok["rwkv"]
            free_k = kI.rearrange("p a b -> p (a b)")
            S, S1, fade = (free_k[:, n * 256:(n + 1) * 256].rearrange("p (a b) -> p a b", b=P)
                           for n in range(3))
            s_done = dve.do(lambda e: e.memset(S, 0.0))
            n_chunks = SEQ // CHUNK
            o_bank = None
            for c in range(n_chunks):
                tile, r = c // 2, slice(64 * (c % 2), 64 * (c % 2) + 64)
                for f in range(2):
                    faded = copy_act(fade[:, f, :], same_head, s_done, scale=eB[:, f, 64 * c + 63:64 * c + 64])
                i = take()
                for f in range(2):
                    done = psum_group(i, banks[i][r, f * P:(f + 1) * P],
                                      [(W2T[:, tile, f, 64 * (c % 2):64 * (c % 2) + 64], S[:, f, :])],
                                      s_done, w2_done)
                u_done = stt(U[r, tile, :], banks[i][r, 0:G], -1.0, W1[r, tile, :], ALU.mult, ALU.add, done,
                             w1_done)
                bank_free[i] = [u_done]
                if c % 2 == 0:
                    o_bank = take()
                    held.add(o_bank)
                    pe.wait(*bank_free[o_bank])
                for f in range(2):
                    pe.quiet(lambda e, o=banks[o_bank][r, f * P:(f + 1) * P],
                             l=rE[:, f, 64 * c:64 * c + 64], s=S[:, f, :], first=(f == 0):
                             e.matmul(o, l, s, start=first, stop=False, skip_group_check=True))
                if c < n_chunks - 1:
                    i = take()
                    for f in range(2):
                        lo, hi = slice(f * P, (f + 1) * P), slice(G + f * P, G + (f + 1) * P)
                        done = psum_group(i, banks[i][:, lo],
                                          [(tokA[r, tile, hi], tokB[r, tile, hi]),
                                           (tokB[r, tile, lo], U[r, tile, lo])], u_done)
                    tt(dve, S1, banks[i][:, 0:G].rearrange("p (a b) -> p a b", b=P), S, ALU.add, done)
                    s_done = tt(dve, S, S1, fade, ALU.mult, faded)
                    bank_free[i] = [s_done]
                if c % 2 == 1:
                    pe.wait(u_done)
                    for h in range(4):
                        v_cols, o_cols = slice(G + h * 64, G + (h + 1) * 64), slice(h * 64, (h + 1) * 64)
                        m_cols = slice(tile * P, (tile + 1) * P)
                        pe.quiet(lambda e, o=banks[o_bank][:, o_cols], l=M_rk[:, h, m_cols],
                                 v=tokB[:, tile, v_cols]:
                                 e.matmul(o, l, v, start=False, stop=False, skip_group_check=True))
                        done = pe.do(lambda e, o=banks[o_bank][:, o_cols], l=M_rb[:, h, m_cols],
                                     v=U[:, tile, o_cols]:
                                     e.matmul(o, l, v, start=False, stop=True, skip_group_check=True))
                    o_done = copy_act(out_r[:, tile, :], banks[o_bank][:, 0:G], done)
                    bank_free[o_bank] = [o_done]
                    held.discard(o_bank)

            heads = lambda ap: ap.rearrange("p t (h d) -> p (t h) d", d=64)
            per_head = lambda ap: ap.unsqueeze(2).to_broadcast([P, 16, 64])
            mean, var = small[:, 128:144], small[:, 144:160]
            o16, u16 = heads(out_r), heads(U)
            dve.do(lambda e: e.tensor_reduce(mean, o16, AX_X, ALU.add), o_done)
            ts(dve, mean, mean, 1.0 / 64, None, ALU.mult, ALU.bypass)
            tt(dve, o16, o16, per_head(mean), ALU.subtract)
            tt(dve, u16, o16, o16, ALU.mult)
            summed = dve.do(lambda e: e.tensor_reduce(var, u16, AX_X, ALU.add))
            root = copy_act(var, var, summed, func=ACT.Sqrt, scale=1.0 / 64, bias=GN_EPS)
            recip(var, var, root)
            tt(dve, o16, o16, per_head(var), ALU.mult)
            tt(dve, out_r, out_r, over_tiles(rows[:, 1, :]), ALU.mult)
            tt(dve, out_r, out_r, over_tiles(rows[:, 2, :]), ALU.add)
            for tile in range(TT):
                tt(dve, U[:, tile, :].rearrange("p (h d) -> p h d", d=64),
                   tokB[:, tile, G:].rearrange("p (h d) -> p h d", d=64),
                   bonus[:, 4 * tile:4 * tile + 4].unsqueeze(2).to_broadcast([P, 4, 64]), ALU.mult, bonus_done)
            tt(dve, out_r, out_r, U, ALU.add)
            y_r = tt(dve, out_r, out_r, g_tok, ALU.mult, g_done)

            fence()
            region = Region(first_at, stay.end)
            y_high, y_low = (region.room(part, KT, SEQ, dt=F32R) for part in ("y_high", "y_low"))
            for f in range(2):
                rounded = copy_act(y_high[:, f, :], y_pool[:, f, :])
                tt(dve, y_low[:, f, :], y_pool[:, f, :], y_high[:, f, :].bitcast(F32), ALU.subtract, rounded)
            for name, y_tile in (("hgrn", 2), ("rwkv", 4), ("gla", 6)):
                for f in range(2):
                    y_done = to_token(y_tok[name], f, y_tile + f, y_r)
            return output_product(1, lambda k: (y_high[:, k, :], y_low[:, k, :]), KT, 1.0, "norm_ffn2",
                                  y_done)

        xg_ready = feed_forward(0, xg_ready, "norm_mix")
        xg_ready = mixers(xg_ready)
        feed_forward(1, xg_ready, None)

        rms_done, _ = finish_norm()
        out_sem = sem("out_stored")
        sent = [0]

        def send(f, token):
            sent[0] += 1
            sp.dma(lambda e: e.dma_start(t["outT"][:, f, :], x[:, f, :]), out_sem, 0, token)

        apply_norm("norm_final", send, rms_done)
        sp.wait((out_sem, 16 * sent[0]))

        block = ctx.enter_context(nc.Block())
        block.tensor(pe.run)
        block.vector(dve.run)
        block.scalar(act.run)
        block.gpsimd(pool.run)
        block.sync(sp.run)


def constants():
    f32 = np.float32
    shared = np.zeros((P, N_SHARED), f32)
    shared[:, 0:128] = np.eye(P)
    lin = np.linspace(0.0, 1.0, RET_DIM // 2, dtype=f32)
    shared[:, 128:192] = (f32(1.0) / np.power(f32(10000.0), lin)).astype(f32)
    j, i = np.arange(P)[:, None], np.arange(SEQ)[None, :]
    decays = np.zeros((P, RET_HEADS, SEQ), f32)
    for h in range(RET_HEADS):
        log_g = np.log1p(-(2.0 ** (-5.0 - h)))
        decays[:, h] = np.where(i // CHUNK >= j // CHUNK, RET_DIM ** -0.5 * np.exp(np.abs(i - j) * log_g), 0)
    r, c = np.arange(P)[:, None], np.arange(P)[None, :]
    mixer = np.zeros((P, N_MIXER + 1024), f32)

    def put(name, a):
        at, n = MIXER[name]
        mixer[:, at:at + n] = a.reshape(a.shape[0], n)

    put("same_head", (r // 64 == c // 64).astype(f32))
    put("before", ((r // 64 == c // 64) & (r < c)).astype(f32))
    put("upto", ((r // 64 == c // 64) & (r <= c)).astype(f32))
    pair = lambda m, s, t: ((s // (2 * m) == t // (2 * m)) & (s // m % 2 == 0) & (t // m % 2 == 1))
    put("pairs", np.stack([pair(m, r, c) for m in LEVELS], 1).astype(f32))
    put("pairs_ts", pair(1, c, r).astype(f32))
    tokens = np.arange(SEQ)
    put("restart", np.broadcast_to((tokens % CHUNK != 0).astype(f32), (P, SEQ)))
    windows = np.array([[2, 8], [4, 16]])[np.arange(P) // 64]
    count = np.minimum(tokens[None, None, :] + 1, windows[:, :, None])
    put("inv_count", (1.0 / count).astype(f32))
    return shared, decays, mixer


def layouts(inputs):
    a = {k: np.asarray(v) for k, v in inputs.items()}

    def tiles(w, m=P):
        k, n = w.shape
        return w.reshape(k // P, P, n // m, m).transpose(2, 1, 0, 3).reshape(n // m, P, -1)

    def groups(w):
        k, n = w.shape
        return w.reshape(k // 256, 2, P, n // 512, 512).transpose(3, 0, 2, 1, 4).reshape(
            n // 512, k // 256, P, 1024)

    out = {"xT": a["x"][0].T.reshape(KT, P, SEQ).transpose(1, 0, 2),
           "positions": a["positions"].astype(np.int32).reshape(TT, P).T}
    w_in = a["w_in"]
    out["w_qk"] = np.stack([tiles(w[:, 0:1024]) for w in w_in])
    order = (4, 5, 2, 3, 6, 7)
    out["w_tok"] = np.stack([np.concatenate([groups(w[:, 512 * g:512 * g + 512]) for g in order])
                             for w in w_in])
    out["w_out"] = np.stack([tiles(w) for w in a["w_out"]])
    r = a["rel_bias"]
    distance = np.arange(P)[:, None] + (SEQ - P) - np.arange(SEQ)[None, :]
    strips = r[:, :, np.clip(distance, -CLIP, CLIP) + CLIP]
    out["strips"] = strips.reshape(2, 2, 4, P, SEQ).transpose(0, 1, 3, 2, 4)
    ffn = [(a["ffn1_w_in_2"][0], a["ffn1_w_out_2"][0]), (a["ffn2_w_in_2"][0], a["ffn2_w_out_2"][0])]
    out["w_ffn_in"] = np.stack([np.stack([tiles(w[:, :D_FF]), tiles(w[:, D_FF:])], 1)
                                .reshape(2 * FT, P, UNIT) for w, _ in ffn])
    out["w_ffn_out"] = np.stack([tiles(w) for _, w in ffn])
    named = {"gain0": a["norm_gain"][0], "gain1": a["norm_gain"][1], "final_gain": a["final_gain"],
             "norm_ffn1": a["norm_ffn1_2"], "norm_mix": a["norm_mix_2"], "norm_ffn2": a["norm_ffn2_2"],
             "norm_final": a["norm_final_2"], "pool_b": a["pool_b_2"], "pool_scale": a["pool_scale_2"],
             "rwkv_mu": a["rwkv_mu_2"], "rwkv_w0": a["rwkv_w0_2"], "rwkv_a0": a["rwkv_a0_2"],
             "rwkv_k_k": a["rwkv_k_k_2"], "rwkv_k_a": a["rwkv_k_a_2"], "rwkv_r_k": a["rwkv_r_k_2"],
             "gla_b": a["gla_b_2"], "lb_logits": a["hgrn_lb_logits_2"]}
    out["cols"] = np.concatenate([named[k].reshape(n, P).T for k, (_, n) in COLS.items()], axis=1)
    out["shared"], out["decays"], out["mixer"] = constants()
    w = a["w_in_2"][0]
    feature_cols = ((0, 256), (1280, 2304), (256, 512), (512, 768), (2304, 2560), (2560, 2816))
    out["w_mix_f"] = np.concatenate([tiles(w[:, lo:hi]) for lo, hi in feature_cols])
    out["w_mix_ga"] = tiles(np.pad(w[:, 3328:], ((0, 0), (0, P - 16))))[0]
    out["w_mix_tok"] = np.concatenate([groups(w[:, 768:1280]), groups(w[:, 2816:3328])])
    out["w_mix_out"] = tiles(a["w_out_2"][0])
    out["rows"] = np.stack([np.broadcast_to(a[k][0], (P, G)) for k in
                            ("hgrn_norm_2", "rwkv_ln_w_2", "rwkv_ln_b_2", "gla_norm_2")], axis=1)
    out["lora"] = np.stack([np.concatenate([a["rwkv_w2_2"][0], a["rwkv_a2_2"][0]]), a["rwkv_g2_2"][0]], 1)
    out["gla_w2"] = a["gla_w2_2"][0]
    out["pool_w"] = a["pool_w_2"][0].reshape(2, P, 64).transpose(1, 0, 2)
    out["inv_count"] = out["mixer"][:, N_MIXER:].reshape(P, 2, SEQ)
    out["mixer"] = out["mixer"][:, :N_MIXER]
    return {k: np.ascontiguousarray(v) for k, v in out.items()}


def kernel(**inputs):
    import concourse.bacc as bacc
    from concourse.bass_utils import run_bass_kernel_spmd

    nc = bacc.Bacc("TRN2", target_bir_lowering=False, num_devices=1)
    arrays = layouts(inputs)
    t = {k: nc.dram_tensor(k, v.shape, mybir.dt.from_np(v.dtype), kind="ExternalInput").ap()
         for k, v in arrays.items()}
    t["outT"] = nc.dram_tensor("outT", (P, KT, SEQ), F32, kind="ExternalOutput").ap()
    build(nc, t)
    got = run_bass_kernel_spmd(nc, [arrays], core_ids=[0]).results[0]["outT"]
    return got.transpose(2, 1, 0).reshape(1, SEQ, D)
```

```python
import math
from contextlib import ExitStack

import concourse.bass as bass
import numpy as np
from concourse import mybir

F32 = mybir.dt.float32
F32R = mybir.dt.float32r
I32 = mybir.dt.int32
ALU = mybir.AluOpType
ACT = mybir.ActivationFunctionType
AX_X = mybir.AxisListType.X

P = 128
SEQ = 512
D = 1024
KT = D // P
TT = SEQ // P
CHUNK = 64
CLIP = 256
ATT_HEADS, ATT_DIM = 8, 64
RET_HEADS, RET_DIM = 4, 128
EPS = 1e-6
GN_EPS = 64e-5
NEG_INF = -1e30
D_FF = 2816
FT = D_FF // P
G = 256
UNIT = 1024
RAW = 4
SPLIT = 3
BANKS = 8
LEVELS = (64, 32, 16, 8, 4, 2, 1)
HALF_E = math.exp(-0.5)
ROUND = 12582912.0

COLS = {}
for _name, _n in (("gain0", 8), ("gain1", 8), ("final_gain", 8), ("norm_ffn1", 8), ("norm_mix", 8),
                  ("norm_ffn2", 8), ("norm_final", 8), ("pool_b", 2), ("pool_scale", 2),
                  ("rwkv_mu", 8), ("rwkv_w0", 2), ("rwkv_a0", 2), ("rwkv_k_k", 2), ("rwkv_k_a", 2),
                  ("rwkv_r_k", 2), ("gla_b", 2), ("lb_logits", 2)):
    COLS[_name] = (sum(n for _, n in COLS.values()), _n)
N_COLS = sum(n for _, n in COLS.values())

N_SHARED = 192
MIXER = {"same_head": (0, 128), "before": (128, 128), "upto": (256, 128), "pairs": (384, 7 * 128),
         "pairs_ts": (384 + 896, 128), "restart": (1408, 512)}
N_MIXER = 1920


class Queue:

    def __init__(self, sem, chained=False):
        self.sem, self.count, self.steps, self.waited = sem, 0, [], {}
        self.chained = chained

    def wait(self, *tokens):
        for token in tokens:
            if token is None:
                continue
            sem, value = token
            if value > self.waited.get(sem, 0):
                self.waited[sem] = value
                self.steps.append(lambda eng, s=sem, v=value: eng.wait_ge(s, v))

    def do(self, emit, *tokens):
        self.wait(*tokens)
        if self.chained:
            self.wait(self.now())
        self.count += 1
        self.steps.append(lambda eng: emit(eng).then_inc(self.sem, 1))
        return (self.sem, self.count)

    def quiet(self, emit, *tokens):
        self.wait(*tokens)
        self.steps.append(emit)

    def dma(self, emit, sem, value, *tokens):
        self.wait(*tokens)
        self.steps.append(lambda eng: emit(eng).then_inc(sem, 16))
        return (sem, value)

    def now(self):
        return (self.sem, self.count) if self.count else None

    def run(self, eng):
        for step in self.steps:
            step(eng)


def unit_order(t):
    order = []
    for n in range(2):
        order += [t["w_qk"][n, f] for f in range(8)]
        order += [t["w_tok"][n, g, u] for g in range(6) for u in range(4)]
        order += [t["w_out"][n, f] for f in range(KT)]

    def feed_forward(which):
        units = [t["w_ffn_in"][which, f] for f in range(2 * FT)]
        return units + [t["w_ffn_out"][which, f][:, a:min(a + UNIT, D_FF)]
                        for f in range(KT) for a in range(0, D_FF, UNIT)]

    def mixer_tiles(*tiles):
        return [t["w_mix_f"][f] for f in tiles]

    def mixer_group(g):
        return [t["w_mix_tok"][g, u] for u in range(4)]

    order += feed_forward(0)
    order += mixer_tiles(0, 1)
    order += mixer_tiles(10, 12, 11, 13) + mixer_group(0)
    order += mixer_tiles(14, 16, 15, 17) + [t["w_mix_ga"]]
    values, projections = mixer_group(1), mixer_tiles(*range(2, 10))
    order += values[0:2] + projections[0:1]
    order += [values[2], projections[1], values[3]] + projections[2:]
    order += [t["w_mix_out"][f] for f in range(KT)] + [t["w_mix_out_rwkv"][u] for u in range(2)]
    return order + feed_forward(1)


def build(nc, t):
    with ExitStack() as ctx:
        def sem(name):
            return ctx.enter_context(nc.semaphore(name))

        pe, sp = (Queue(sem(f"done_{n}")) for n in ("pe", "sp"))
        dve, act, pool = (Queue(sem(f"done_{n}"), chained=True) for n in ("dve", "act", "pool"))

        class Region:

            def __init__(self, at, end):
                self.at, self.end = -(-at // 32) * 32, end

            def room(self, name, *shape, dt=F32):
                names[name] = names.get(name, 0) + 1
                size = -(-int(np.prod(shape)) * 4 // 32) * 32
                assert self.at + size <= self.end, (name, self.at + size, self.end)
                h = nc.alloc_sbuf_tensor_at(f"sb_{name}_{names[name]}", [P, *shape], dt, offset=self.at)
                self.at += size
                return h[(slice(None),) * (1 + len(shape))]

        names = {}
        stay = Region(nc.sbuf_base, nc.sbuf_usable_end // 32 * 32)
        x = stay.room("x", KT, SEQ)
        raw = stay.room("raw", RAW, UNIT)
        w_high = stay.room("w_high", SPLIT, UNIT, dt=F32R)
        w_low = stay.room("w_low", SPLIT, UNIT, dt=F32R)
        cols = stay.room("cols", N_COLS)
        shared = stay.room("shared", N_SHARED)
        ones = stay.room("ones", P)
        square = stay.room("square", 2, SEQ)
        square_sum = stay.room("square_sum", SEQ)
        inv_rms = stay.room("inv_rms", SEQ)
        inv_rms_t = stay.room("inv_rms_t", TT)
        small = stay.room("small", 256)
        positions = stay.room("positions", TT, dt=I32)
        rotary_at = stay.at
        cos2, sin2 = stay.room("cos2", TT, P), stay.room("sin2", TT, P)
        xg_at = stay.at
        xg = Region(xg_at, stay.end)
        xg_high, xg_low = xg.room("xg_high", KT, SEQ, dt=F32R), xg.room("xg_low", KT, SEQ, dt=F32R)
        phase_at = xg.at
        banks = [ctx.enter_context(nc.psum_tensor(f"bank{i}", [P, 512], F32)) for i in range(BANKS)]

        def col(name, i, rows=slice(0, P)):
            at = COLS[name][0] + i
            return cols[rows, at:at + 1]

        ident = shared[:, 0:128]

        bank_free = [[] for _ in range(BANKS)]
        turn = [0]
        held = set()

        def take():
            while True:
                i = turn[0] % BANKS
                turn[0] += 1
                if i not in held:
                    return i

        def psum_group(i, out, pairs, *tokens):
            pe.wait(*bank_free[i])
            pe.wait(*tokens)
            for n, (lhsT, rhs) in enumerate(pairs):
                first, last = n == 0, n == len(pairs) - 1
                emit = (lambda e, o=out, l=lhsT, r=rhs, f=first, z=last:
                        e.matmul(o, l, r, start=f, stop=z))
                if last:
                    return pe.do(emit)
                pe.quiet(emit)

        def transposes(i, blocks, *tokens):
            pe.wait(*bank_free[i])
            pe.wait(*tokens)
            for n, (out, in_) in enumerate(blocks):
                emit = lambda e, o=out, a=in_: e.transpose(o, a, ident)
                if n == len(blocks) - 1:
                    return pe.do(emit)
                pe.quiet(emit)

        raw_sem = [sem(f"weights_{i}") for i in range(RAW)]
        raw_free = [None] * RAW
        split_free = [None] * SPLIT
        order = unit_order(t)
        loaded, parts, used = [], [], [0]

        def load_unit():
            n = len(loaded)
            dram, slot = order[n], n % RAW
            dst = raw[:, slot, 0:dram.shape[-1]]
            loaded.append((dst, sp.dma(lambda e: e.dma_start(dst, dram), raw_sem[slot],
                                       16 * (n // RAW + 1), raw_free[slot])))

        def split_unit():
            n = len(parts)
            src, token = loaded[n]
            width, slot = src.shape[-1], n % SPLIT
            high, low = w_high[:, slot, 0:width], w_low[:, slot, 0:width]
            rounded = copy_act(high, src, token, split_free[slot])
            raw_free[n % RAW] = tt(dve, low, src, high.bitcast(F32), ALU.subtract, rounded)
            parts.append((high, low, raw_free[n % RAW]))
            if len(loaded) < len(order):
                load_unit()

        def split_ahead():
            while len(parts) < min(used[0] + SPLIT, len(order)):
                split_unit()

        def next_unit():
            split_ahead()
            used[0] += 1
            return (used[0] - 1) % SPLIT, parts[used[0] - 1]

        def three_passes(out, w, v, first, last):
            for n, (a, b) in enumerate(((w[0], v[0]), (w[0], v[1]), (w[1], v[0]))):
                yield (lambda e, a=a, b=b, f=(first and n == 0), z=(last and n == 2):
                       e.matmul(out, a, b, start=f, stop=z))

        def run_products(slot, emits):
            for emit in emits[:-1]:
                pe.quiet(emit)
            split_free[slot] = pe.do(emits[-1])
            return split_free[slot]

        def feature_major(n_units, k_tiles, rhs, halfway=None):
            i, k = take(), 0
            held.add(i)
            pe.wait(*bank_free[i])
            for _ in range(n_units):
                slot, (high, low, ready) = next_unit()
                pe.wait(ready)
                n_tiles = high.shape[-1] // P
                for j in range(n_tiles):
                    if halfway and k == k_tiles // 2:
                        halfway()
                    c = slice(j * P, (j + 1) * P)
                    *v, made = rhs(k)
                    pe.wait(made)
                    passes = list(three_passes(banks[i][:, :], (high[:, c], low[:, c]), v, k == 0,
                                               k == k_tiles - 1))
                    k += 1
                    if j < n_tiles - 1:
                        for emit in passes:
                            pe.quiet(emit)
                done = run_products(slot, passes)
            held.discard(i)
            return i, done

        def token_major(pieces):
            out = [take() for _ in range(TT)]
            held.update(out)
            for i in out:
                pe.wait(*bank_free[i])
            pe.wait(xg_made[-1])
            for u in range(KT // 2):
                slot, (high, low, ready) = next_unit()
                pe.wait(ready)
                emits = []
                for j in range(2):
                    k, c = 2 * u + j, slice(j * 512, (j + 1) * 512)
                    for tile, i in enumerate(out):
                        r = slice(tile * P, (tile + 1) * P)
                        emits += three_passes(banks[i][:, :], (xg_high[:, k, r], xg_low[:, k, r]),
                                              (high[:, c], low[:, c]), k == 0, k == KT - 1)
                n = len(emits) // pieces
                for piece in range(pieces - 1):
                    for emit in emits[piece * n:(piece + 1) * n]:
                        pe.quiet(emit)
                    yield
                done = run_products(slot, emits[(pieces - 1) * n:])
                if u < KT // 2 - 1:
                    yield
            token_major_result[:] = [out, done]

        token_major_result = []
        xg_made = [None] * KT

        def xg_tile(k):
            return xg_high[:, k, :], xg_low[:, k, :], xg_made[k]

        def fence():
            ends = [q.now() for q in (pe, dve, act, pool)]
            for q in (dve, act, pool):
                q.wait(*ends)

        def phase():
            fence()
            return Region(phase_at, stay.end)

        def copy_act(out, in_, *tokens, func=ACT.Identity, scale=1.0, bias=0.0, accum=None):
            return act.do(lambda e: e.activation(out, in_, func, bias=bias, scale=scale,
                                                 accum_out=accum), *tokens)

        def tt(q, out, a, b, op, *tokens):
            return q.do(lambda e: e.tensor_tensor(out, a, b, op), *tokens)

        def ts(q, out, a, s1, s2, op0, op1, *tokens):
            return q.do(lambda e: e.tensor_scalar(out, a, s1, s2, op0, op1), *tokens)

        def stt(out, a, s, b, op0, op1, *tokens):
            return dve.do(lambda e: e.scalar_tensor_tensor(out=out, in0=a, scalar=s, in1=b, op0=op0,
                                                           op1=op1), *tokens)

        def recip(out, in_, *tokens):
            return dve.do(lambda e: e.reciprocal(out, in_), *tokens)

        def split_from_bank(high, low, i, *tokens):
            src = banks[i][:, :]
            if len(high.shape) == 3:
                src = src.rearrange("p (f c) -> p f c", c=P)
            rounded = copy_act(high, src, *tokens)
            bank_free[i] = [tt(dve, low, src, high.bitcast(F32), ALU.subtract, rounded)]
            return bank_free[i][0]

        cols_sem, fixed_sem = sem("cols_load"), sem("fixed_loads")
        cols_in = sp.dma(lambda e: e.dma_start(cols, t["cols"]), cols_sem, 16)
        load_unit()
        x_loaded = []
        for f in range(KT):
            x_sem = sem(f"x_load_{f}")
            x_loaded.append(act.dma(lambda e, f=f: e.dma_start(x[:, f, :], t["xT"][:, f, :]), x_sem, 16))
        for out, src in ((shared, t["shared"]), (positions, t["positions"])):
            pool.dma(lambda e, o=out, s=src: e.dma_start(o, s), fixed_sem, 0)
        fixed_in = (fixed_sem, 32)
        load_unit()
        sp.wait(x_loaded[KT // 2])
        for _ in range(RAW - 2):
            load_unit()
        ones_set = dve.do(lambda e: e.memset(ones[:, :], 1.0))
        for q in (dve, act):
            q.wait(cols_in)
        pe.wait(ones_set)

        square_free = [None, None]
        summed = [None, None]

        def square_in(f, *tokens, adder=pool):
            if f == 0:
                summed[0] = copy_act(square_sum, x[:, f, :], *tokens, summed[1], func=ACT.Square)
            else:
                squared = copy_act(square[:, f % 2, :], x[:, f, :], *tokens, square_free[f % 2],
                                   func=ACT.Square)
                square_free[f % 2] = summed[0] = tt(adder, square_sum, square_sum, square[:, f % 2, :],
                                                    ALU.add, squared, summed[0])

        def finish_norm():
            b = take()
            for tile in range(TT):
                summed[1] = psum_group(b, banks[b][:, tile:tile + 1],
                                       [(square_sum[:, tile * P:(tile + 1) * P], ones[:, 0:1])], summed[0])
            root = copy_act(inv_rms_t, banks[b][:, 0:TT], summed[1], dve.now(), func=ACT.Sqrt,
                            scale=1.0 / D, bias=EPS)
            bank_free[b] = [root]
            side = recip(inv_rms_t, inv_rms_t, root)
            diagonal = square[:, 0, :].rearrange("p (a b) -> p a b", b=P)
            spread = tt(dve, diagonal, ident.unsqueeze(1).to_broadcast([P, TT, P]),
                        inv_rms_t.unsqueeze(2).to_broadcast([P, TT, P]), ALU.mult, *square_free)
            i = take()
            square_free[0] = psum_group(i, banks[i][:, :], [(ones, square[:, 0, :])], spread)
            done = copy_act(inv_rms, banks[i][:, :], square_free[0])
            bank_free[i] = [done]
            return done, side

        def gained(f, gain, *tokens):
            high = copy_act(xg_high[:, f, :], x[:, f, :], *tokens, scale=col(gain, f))
            xg_made[f] = stt(xg_low[:, f, :], x[:, f, :], col(gain, f), xg_high[:, f, :].bitcast(F32),
                             ALU.mult, ALU.subtract, high)

        def norm_of_stream(gain, ready):
            for f in range(KT):
                gained(f, gain, ready(f), pe_used_xg[0])
            sum_squares()

        def sum_squares():
            split_ahead()
            for f in range(KT):
                square_in(f, adder=dve)

        def normalise(gain, follow, rms_done):
            before = None
            for f in range(KT):
                made = stt(x[:, f, :], x[:, f, :], col(gain, f), inv_rms, ALU.mult, ALU.mult, rms_done)
                if before:
                    follow(*before)
                before = (f, made)
            follow(*before)

        def output_product(n_units, rhs, k_tiles, factor, next_gain, halfway=None):
            for f in range(KT):
                i, done = feature_major(n_units, k_tiles, rhs, None if f else halfway)
                added = stt(x[:, f, :], banks[i][:, :], factor, x[:, f, :], ALU.mult, ALU.add, done)
                bank_free[i] = [added]
                if next_gain:
                    gained(f, next_gain, added, pe_used_xg[0])
                square_in(f, added)

        pe_used_xg = [None]

        strip_sem, decay_sem = [sem(f"strip_{i}") for i in range(4)], sem("decays")
        split_unit()
        norm_of_stream("gain0", lambda f: x_loaded[f])
        for q in (pe, dve, act, pool):
            q.wait(fixed_in)

        def rotary_tables(region):
            pos_f = small[:, 0:TT]
            TWO_PI = 2 * math.pi
            part1 = 6.28125
            part2 = round((TWO_PI - part1) * 2 ** 21) / 2 ** 21
            part3 = TWO_PI - part1 - part2
            ready = dve.do(lambda e: e.tensor_copy(pos_f, positions[:, :]))
            angle, turns = region.room("angle", TT, 64), region.room("turns", TT, 64)
            for tile in range(TT):
                made = ts(dve, angle[:, tile, :], shared[:, 128:192], pos_f[:, tile:tile + 1], None,
                          ALU.mult, ALU.bypass, ready)
            made = ts(dve, turns, angle, 1.0 / TWO_PI, ROUND, ALU.mult, ALU.add, made)
            made = ts(dve, turns, turns, ROUND, None, ALU.subtract, ALU.bypass, made)
            for part in (part1, part2, part3):
                made = stt(angle, turns, -part, angle, ALU.mult, ALU.add, made)
            made = ts(dve, angle, angle, math.pi * (1 - 1e-7), -math.pi * (1 - 1e-7), ALU.min, ALU.max, made)
            copy_act(sin2[:, :, 64:128], angle, made, func=ACT.Sin)
            copy_act(sin2[:, :, 0:64], angle, func=ACT.Sin, scale=-1.0)
            absolute = copy_act(turns, angle, made, func=ACT.Abs)
            copy_act(cos2[:, :, 0:64], turns, absolute, func=ACT.Sin, scale=-1.0, bias=math.pi / 2)
            return copy_act(cos2[:, :, 64:128], turns, absolute, func=ACT.Sin, scale=-1.0,
                            bias=math.pi / 2)

        rotary = []

        def layer(n, next_gain):
            region = phase()
            tok = {name: region.room(name, TT, 512) for name in ("av", "ag", "rq", "rk", "rv", "rg")}
            att_at = region.at
            att2 = region.room("att", 2, 1280)
            prob = Region(att_at, region.at).room("prob", 4, SEQ)
            rot = region.room("rot", 3, SEQ)
            decays = region.room("decays", RET_HEADS, SEQ)
            y_at = region.at
            qT = region.room("qT", 4, SEQ)
            kT = region.room("kT", 4, SEQ)
            strips = region.room("strips", 4, SEQ)
            probT = region.room("probT", 2, SEQ)
            decays_in = pool.dma(lambda e: e.dma_start(decays, t["decays"]), decay_sem, 16 * (n + 1))

            def load_strip(h, *tokens):
                loaded = pool.dma(lambda e: e.dma_start(strips[:, h % 4, :], t["strips"][n, h]),
                                  strip_sem[h % 4], 16 * (2 * n + h // 4 + 1), *tokens)
                strips_in[h] = pool.do(lambda e: e.memset(strips[0:64, h % 4, 448:512], NEG_INF), loaded)

            strips_in = {}
            for h in range(4):
                load_strip(h)

            products = [feature_major(1, KT, xg_tile) for _ in range(3)]
            rms_done, side = finish_norm()
            for f in range(8):
                i, done = products[f] if f < 3 else feature_major(1, KT, xg_tile)
                out = qT[:, f, :] if f < 4 else kT[:, f - 4, :]
                qk_done = stt(out, banks[i][:, :], ATT_DIM ** -0.5 if f < 4 else 1.0, inv_rms,
                              ALU.mult, ALU.mult, done, rms_done)
                bank_free[i] = [qk_done]

            landed = {}

            def group_steps(names, pieces):
                for name in names:
                    yield from token_major(pieces)
                    group_banks, done = token_major_result
                    for tile, i in enumerate(group_banks):
                        scale = inv_rms_t[:, tile:tile + 1]
                        if name in ("rv", "rg") or name != "ag" and tile % 2:
                            out = ts(dve, tok[name][:, tile, :], banks[i][:, :], scale, None, ALU.mult,
                                     ALU.bypass, done)
                        else:
                            out = copy_act(tok[name][:, tile, :], banks[i][:, :], done, side, scale=scale,
                                           func=ACT.Silu if name == "ag" else ACT.Identity)
                        landed[name] = landed.get(name, [])[-1:] + [out]
                        bank_free[i] = [out]
                        held.discard(i)
                    pe_used_xg[0] = done
                    yield

            turned, rot_free = {}, [None, None]

            def rotate(name, tile):
                src = tok[name][:, tile, :].rearrange("p (h d) -> p h d", d=P)
                a, b, r = (rot[:, s, :].rearrange("p (h d) -> p h d", d=P) for s in range(3))
                c = cos2[:, tile, :].unsqueeze(1).to_broadcast([P, 4, P])
                s_lo = sin2[:, tile, 0:64].unsqueeze(1).to_broadcast([P, 4, 64])
                s_hi = sin2[:, tile, 64:128].unsqueeze(1).to_broadcast([P, 4, 64])
                tt(dve, a, src, c, ALU.mult, *landed[name], rotary[0])
                tt(dve, b[:, :, 0:64], src[:, :, 64:128], s_lo, ALU.mult)
                tt(dve, b[:, :, 64:128], src[:, :, 0:64], s_hi, ALU.mult)
                return tt(dve, r, a, b, ALU.add, rot_free[0])

            def turn_rotated(name, tile, rotated):
                i = take()
                rot_free[0] = transposes(
                    i, [(banks[i][:, h * P:(h + 1) * P], rot[:, 2, h * P:(h + 1) * P])
                        for h in range(4)], rotated)
                turned[name] = copy_act(tok[name][:, tile, :], banks[i][:, :], rot_free[0])
                bank_free[i] = [turned[name]]

            if n == 0:
                rotary.append(rotary_tables(Region(att_at, stay.end)))
            for _ in group_steps(("rq",), 1):
                pass
            for name, before in (("rk", "rq"), ("av", "rk")):
                steps = group_steps((name,), 1)
                for tile in range(TT):
                    rotated = rotate(before, tile)
                    next(steps)
                    turn_rotated(before, tile, rotated)
                for _ in steps:
                    pass
            for _ in group_steps(("ag",), 1):
                pass
            filler = group_steps(("rv", "rg"), 4)

            steps = [(h, q) for h in range(ATT_HEADS) for q in range(TT)]
            state = {}

            def scores(h, q):
                r = slice(64 * (h % 2), 64 * (h % 2) + 64)
                i = take()
                keys = (q + 1) * P
                done = psum_group(i, banks[i][:, 0:keys],
                                  [(qT[r, h // 2, q * P:(q + 1) * P], kT[r, h // 2, 0:keys])], qk_done)
                if q == 0 and 1 <= h <= 4:
                    load_strip(h + 3, state[(h - 1, TT - 1)]["biased"])
                s = state[(h, q)] = {}
                buf = (h * TT + q) % 4
                stat = 8 + 4 * ((h * TT + q) % 4)
                s["p"], s["stat"] = prob[:, buf, 0:keys], stat
                before = state.get(prev(h, q, 4))
                s["biased"] = dve.do(lambda e: e.tensor_tensor_reduce(
                    out=s["p"], in0=banks[i][:, 0:keys], in1=strips[:, h % 4, 512 - keys:512],
                    scale=1.0, scalar=-3e38, op0=ALU.add, op1=ALU.max,
                    accum_out=small[:, stat:stat + 1]), done, strips_in[h],
                    before and before["turned"])
                bank_free[i] = [s["biased"]]
                minus = ts(dve, small[:, stat + 1:stat + 2], small[:, stat:stat + 1], -1.0, None,
                           ALU.mult, ALU.bypass, s["biased"])
                s["exp"] = copy_act(s["p"], s["p"], minus, func=ACT.Exp,
                                    bias=small[:, stat + 1:stat + 2], accum=small[:, stat + 2:stat + 3])

            def prev(h, q, n):
                k = h * TT + q - n
                return (k // TT, k % TT)

            def turn_probs(h, q):
                s = state[(h, q)]
                i = take()
                s["turned"] = transposes(i, [(banks[i][:, k * P:(k + 1) * P],
                                              s["p"][:, k * P:(k + 1) * P]) for k in range(q + 1)],
                                         s["exp"])
                before = state.get(prev(h, q, 2))
                s["buf"] = probT[:, (h * TT + q) % 2, :]
                s["probT"] = copy_act(s["buf"][:, 0:(q + 1) * P], banks[i][:, 0:(q + 1) * P],
                                      s["turned"], before and before["used"])
                bank_free[i] = [s["probT"]]
                s["inv"] = recip(small[:, s["stat"] + 3:s["stat"] + 4],
                                 small[:, s["stat"] + 2:s["stat"] + 3], s["exp"])

            def values(h, q):
                s = state[(h, q)]
                i = take()
                s["used"] = psum_group(i, banks[i][:, 0:ATT_DIM],
                                       [(s["buf"][:, k * P:(k + 1) * P],
                                         tok["av"][:, k, h * ATT_DIM:(h + 1) * ATT_DIM])
                                        for k in range(q + 1)], s["probT"], *landed["av"])
                gate = tok["ag"][:, q, h * ATT_DIM:(h + 1) * ATT_DIM]
                s["out"] = stt(gate, banks[i][:, 0:ATT_DIM], small[:, s["stat"] + 3:s["stat"] + 4], gate,
                               ALU.mult, ALU.mult, s["used"], s["inv"], *landed["ag"])
                bank_free[i] = [s["out"]]

            for n_step in range(len(steps) + 3):
                if n_step < len(steps):
                    scores(*steps[n_step])
                if n_step:
                    next(filler, None)
                if n_step >= 3:
                    values(*steps[n_step - 3])
                if 2 <= n_step < len(steps) + 2:
                    turn_probs(*steps[n_step - 2])
            for _ in filler:
                pass
            att_out = state[steps[-1]]["out"]

            offs = [0, 512, 896, 1152]
            att_free, weighted = [None, None], {}
            ret_out = None

            def ret_scores(h):
                att = att2[:, h % 2, :]
                for j in range(TT):
                    width = (TT - j) * P
                    i = take()
                    kh = tok["rk"][:, j, h * P:(h + 1) * P]
                    qh = tok["rq"][:, j:TT, h * P:(h + 1) * P]
                    done = psum_group(i, banks[i][:, 0:width].rearrange("p (a b) -> p a b", b=P),
                                      [(kh, qh)], turned["rk"], turned["rq"])
                    weighted[h] = tt(dve, att[:, offs[j]:offs[j] + width], banks[i][:, 0:width],
                                     decays[:, h, 0:width], ALU.mult, done, decays_in, att_free[h % 2])
                    bank_free[i] = [weighted[h]]

            def ret_values(h):
                att = att2[:, h % 2, :]
                i = take()
                held.add(i)
                for q in range(TT):
                    done = psum_group(i, banks[i][:, q * P:(q + 1) * P],
                                      [(att[:, offs[j] + (q - j) * P:offs[j] + (q - j + 1) * P],
                                        tok["rv"][:, j, h * P:(h + 1) * P]) for j in range(q + 1)],
                                      weighted[h], *landed["rv"])
                att_free[h % 2] = done
                stat = 32 + 12 * h
                ss, root, inv = (small[:, stat + 4 * k:stat + 4 * k + 4] for k in range(3))
                for q in range(TT):
                    summed = copy_act(rot[:, 0, q * P:(q + 1) * P], banks[i][:, q * P:(q + 1) * P],
                                      done, rot_free[0], func=ACT.Square, accum=ss[:, q:q + 1])
                rooted = copy_act(root, ss, summed, func=ACT.Sqrt, scale=1.0 / RET_DIM, bias=EPS)
                inverted = recip(inv, root, rooted)
                for q in range(TT):
                    normed = copy_act(rot[:, 1, q * P:(q + 1) * P], banks[i][:, q * P:(q + 1) * P], inverted,
                                      rot_free[1], scale=inv[:, q:q + 1])
                bank_free[i] = [normed]
                held.discard(i)
                gate = tok["rg"][:, :, h * P:(h + 1) * P]
                rot_free[1] = tt(pool, gate, gate, rot[:, 1, :].rearrange("p (a b) -> p a b", b=P),
                                 ALU.mult, normed, gated)
                return rot_free[1]

            over = Region(y_at, stay.end)
            y_high, y_low = (over.room(part, KT, SEQ, dt=F32R) for part in ("y_high", "y_low"))

            def turn_output(half, name, tile, made):
                i = take()
                done = transposes(i, [(banks[i][:, f * P:(f + 1) * P],
                                       tok[name][:, tile, f * P:(f + 1) * P]) for f in range(4)], made)
                part = (slice(None), slice(4 * half, 4 * half + 4), slice(tile * P, (tile + 1) * P))
                return split_from_bank(y_high[part], y_low[part], i, done)

            gated = copy_act(tok["rg"].rearrange("p a b -> p (a b)"), tok["rg"].rearrange("p a b -> p (a b)"),
                             *landed["rg"], func=ACT.Silu)
            for h in range(RET_HEADS + 1):
                if h < RET_HEADS:
                    ret_scores(h)
                    att_turned = turn_output(0, "ag", h, att_out)
                if h:
                    ret_out = ret_values(h - 1)
            y_made = [att_turned] * 4

            def turn_retention():
                for tile in range(TT):
                    turned = turn_output(1, "rg", tile, ret_out)
                y_made.extend([turned] * 4)

            output_product(1, lambda k: (y_high[:, k, :], y_low[:, k, :], y_made[k]), KT, 1.0, next_gain,
                           turn_retention)

        layer(0, "gain1")
        layer(1, None)

        rms_done, _ = finish_norm()
        normalise("final_gain", lambda f, token: gained(f, "norm_ffn1", token, pe_used_xg[0]), rms_done)
        sum_squares()

        def feed_forward(which, next_gain):
            region = phase()
            h_high, h_low = (region.room(part, FT, SEQ, dt=F32R) for part in ("h_high", "h_low"))
            gate = region.room("gate", 2, SEQ)
            up = region.room("up", 2, SEQ)
            h_made = []
            early = [feature_major(1, KT, xg_tile) for _ in range(3)]
            rms_done, _ = finish_norm()
            for f in range(FT):
                b = f % 2
                ig, gate_done = early.pop(0) if early else feature_major(1, KT, xg_tile)
                iu, up_done = early.pop(0) if early else feature_major(1, KT, xg_tile)
                gated = tt(dve, gate[:, b, :], banks[ig][:, :], inv_rms, ALU.mult, gate_done, rms_done)
                bank_free[ig] = [gated]
                silu = copy_act(gate[:, b, :], gate[:, b, :], gated, func=ACT.Silu)
                upped = tt(dve, up[:, b, :], banks[iu][:, :], inv_rms, ALU.mult, up_done)
                bank_free[iu] = [upped]
                product = tt(dve, up[:, b, :], gate[:, b, :], up[:, b, :], ALU.mult, silu, upped)
                rounded = copy_act(h_high[:, f, :], up[:, b, :], product)
                h_made.append(tt(dve, h_low[:, f, :], up[:, b, :], h_high[:, f, :].bitcast(F32),
                                 ALU.subtract, rounded))
            pe_used_xg[0] = pe.now()
            output_product(3, lambda k: (h_high[:, k, :], h_low[:, k, :], h_made[k]), FT, 0.5, next_gain)

        def over_tiles(ap, n=TT):
            return ap.unsqueeze(1).to_broadcast([P, n, ap.shape[-1]])

        def mixers():
            region = phase()
            mixer = region.room("mixer", N_MIXER)
            rows = region.room("rows", 4, G)
            lora = region.room("lora", 2, G)
            gla_w2 = region.room("gla_w2", G)
            pool_w = region.room("pool_w", 2, 64)
            y_pool = region.room("y_pool", 2, SEQ)
            ga_sb = region.room("ga", SEQ)
            y_tok = {name: region.room(f"y_{name}", TT, G) for name in ("hgrn", "rwkv", "gla")}
            mixer_sem = sem("mixer_loads")
            loads = [(mixer, t["mixer"]), (rows, t["rows"]), (lora, t["lora"]),
                     (gla_w2[0:16, :], t["gla_w2"]), (pool_w, t["pool_w"])]
            for out, src in loads:
                pool.dma(lambda e, o=out, s=src: e.dma_start(o, s), mixer_sem, 0)
            mixer_in = (mixer_sem, 16 * len(loads))

            def table(name):
                at, n = MIXER[name]
                return mixer[:, at:at + n]

            first_at = region.at
            operands = {}
            for name in ("hgrn", "gla"):
                q2, k2, c2 = (region.room(f"{n}_{name}", 2, SEQ) for n in "qkc")
                operands[name] = (q2, k2, c2, region.room(f"v_{name}", TT, 512))
                if name == "hgrn":
                    second_at = region.at
            E2 = [region.room("E", 2, SEQ) for _ in range(2)]
            near_at = region.at
            near = region.room("near", 4, TT * P)
            far = region.room("far", 4, 768)
            same_head = table("same_head")
            early = [feature_major(1, KT, xg_tile) for _ in range(2)]
            norms = finish_norm()

            def projected():
                return early.pop(0) if early else feature_major(1, KT, xg_tile)

            region = Region(near_at, stay.end)
            pad = 16
            p_in, s2, s4 = (region.room(n, 2, SEQ + pad) for n in ("p_in", "s2", "s4"))
            s8, s16 = (region.room(n, SEQ + pad) for n in ("s8", "s16"))
            window = region.room("window", 2, SEQ)
            inv_count = Region(rotary_at, xg_at).room("inv_count", 2, SEQ)
            count_in = pool.dma(lambda e: e.dma_start(inv_count, t["inv_count"]), sem("count_load"), 16)
            dve.do(lambda e: e.memset(p_in[:, :, 0:pad], 0.0))
            for f in range(2):
                i, done = projected()
                p_done = tt(dve, p_in[:, f, pad:], banks[i][:, :], inv_rms, ALU.mult, done, norms[0])
                bank_free[i] = [p_done]
            w = SEQ + pad
            tt(pool, s2[:, :, 1:w], p_in[:, :, 1:w], p_in[:, :, 0:w - 1], ALU.add, p_done)
            tt(pool, s4[:, :, 3:w], s2[:, :, 3:w], s2[:, :, 1:w - 2], ALU.add)
            tt(pool, s8[:, 7:w], s4[:, 1, 7:w], s4[:, 1, 3:w - 4], ALU.add)
            tt(pool, s16[:, 15:w], s8[:, 15:w], s8[:, 7:w - 8], ALU.add)
            for rows64, f, sums in ((slice(0, 64), 0, s2[:, 0]), (slice(64, 128), 0, s4[:, 0]),
                                    (slice(0, 64), 1, s8), (slice(64, 128), 1, s16)):
                tt(pool, window[rows64, f, :], sums[rows64, pad:], inv_count[rows64, f, :], ALU.mult,
                   count_in)
            pooled = tt(pool, window, window, p_in[:, :, pad:], ALU.subtract)

            def pool_outputs():
                for f in range(2):
                    for r in (slice(0, 64), slice(64, 128)):
                        i = take()
                        done = psum_group(i, banks[i][r, :], [(pool_w[r, f, :], window[r, f, :])], pooled)
                        bank_free[i] = [ts(dve, y_pool[r, f, :], banks[i][r, :], col("pool_b", f, r),
                                           col("pool_scale", f, r), ALU.add, ALU.mult, done)]

            def to_token(y, f, y_tile, *tokens):
                i = take()
                done = transposes(i, [(banks[i][:, tile * P:(tile + 1) * P],
                                       y[:, tile, f * P:(f + 1) * P]) for tile in range(TT)], *tokens)
                return split_from_bank(y_high[:, y_tile, :], y_low[:, y_tile, :], i, done)

            def head_tile(h):
                return slice(64 * (h % 2), 64 * (h % 2) + 64), h // 2

            tiles4 = lambda ap: ap.rearrange("p (a b) -> p a b", b=P)
            flat = lambda ap: ap.rearrange("p a b -> p (a b)")

            def halves(ap, m, right, dims="p (n c) -> p n c"):
                v = ap.rearrange(dims, c=2 * m) if "t" not in dims else ap.rearrange(dims, t=TT, c=2 * m)
                at = slice(m, 2 * m) if right else slice(0, m)
                return v[:, :, at] if len(v.shape) == 3 else v[:, :, :, at]

            def pairs(m):
                n = LEVELS.index(m)
                return table("pairs")[:, n * P:(n + 1) * P]

            def pair_mask(m):
                v = halves(pairs(m), m, True)
                return v.unsqueeze(1).to_broadcast([P, TT, v.shape[1], m])

            v_done = {}

            def linear_attention(name, y, fill):
                q2, k2, c2, v2 = operands[name]
                for f in range(2):
                    c_done = dve.do(lambda e, f=f: e.tensor_tensor_scan(
                        c2[:, f, :], table("restart"), c2[:, f, :], 0.0, ALU.mult, ALU.add))
                fill(0)
                for h in range(4):
                    r, g = head_tile(h)
                    i = take()
                    for tile in range(TT):
                        c = slice(tile * P, (tile + 1) * P)
                        done = psum_group(i, banks[i][:, c], [(k2[r, g, c], q2[r, g, c])], c_done)
                    bank_free[i] = [tt(dve, tiles4(near[:, h, :]), tiles4(banks[i][:, :]), over_tiles(ident),
                                       ALU.mult, done)]
                levels = (32, 16, 8, 4, 2, 1, 64, 128, 256)
                e_free, factors = [None, None], {}

                def factor(n):
                    m, e = levels[n], E2[n % 2]
                    cl, cr, el, er = (halves(flat(ap), m, side) for ap in (c2, e) for side in (False, True))
                    ql, kl = halves(flat(q2), m, True), halves(flat(k2), m, False)
                    nb = SEQ // m
                    if m > 64:
                        right = halves(flat(c2), m // 2, True)
                        last = halves(flat(c2), m // 2, False)[:, :, m // 2 - 1:m // 2]
                        tt(dve, right, right, last.to_broadcast([P, 2 * nb, m // 2]), ALU.add, act.now())
                    border = cl[:, :, m - 1:m].to_broadcast([P, nb, m])
                    made = tt(dve, el, border, cl, ALU.subtract, e_free[n % 2])
                    if m < 64:
                        made = tt(dve, er, cr, border, ALU.subtract)
                        made = copy_act(flat(e), flat(e), made, func=ACT.Exp)
                    else:
                        copy_act(er, cr, made, func=ACT.Exp)
                        made = copy_act(el, el, func=ACT.Exp)
                    left = tt(pool, el, el, kl, ALU.mult, made)
                    right = tt(dve, er, er, ql, ALU.mult, made)
                    factors[n] = (left, right)

                def scores(n):
                    m, e = levels[n], E2[n % 2]
                    for h in range(4):
                        r, g = head_tile(h)
                        i = take()
                        if m <= 64:
                            for tile in range(TT):
                                et = e[r, g, tile * P:(tile + 1) * P]
                                out = banks[i][:, tile * 64:(tile + 1) * 64]
                                done = psum_group(i, out.rearrange("p (n c) -> p n c", c=m),
                                                  [(et, halves(et, m, True))], *factors[n])
                            data = banks[i][:, 0:256].rearrange("p (t n c) -> p t n c", t=TT, c=m)
                            out = halves(near[:, h, :], m, True, "p (t n c) -> p t n c")
                            bank_free[i] = [dve.do(lambda e, o=out, d=data, m=m: e.copy_predicated(
                                o, pair_mask(m).bitcast(I32), d), done)]
                        elif m == 128:
                            for n_far, key in enumerate((0, 2)):
                                done = psum_group(i, banks[i][:, n_far * P:(n_far + 1) * P],
                                                  [(e[r, g, key * P:(key + 1) * P],
                                                    e[r, g, (key + 1) * P:(key + 2) * P])], *factors[n])
                            bank_free[i] = [copy_act(far[:, h, 0:256], banks[i][:, 0:256], done)]
                        else:
                            for key in range(2):
                                done = psum_group(i, banks[i][:, key * 256:(key + 1) * 256],
                                                  [(e[r, g, key * P:(key + 1) * P], e[r, g, 256:512])],
                                                  *factors[n])
                            bank_free[i] = [copy_act(far[:, h, 256:768], banks[i][:, :], done)]
                    e_free[n % 2] = done

                factor(0)
                for n in range(len(levels)):
                    if n + 1 < len(levels):
                        factor(n + 1)
                    if n + 1 < len(levels):
                        fill(n + 1)
                    scores(n)

                scores_done = (dve.now(), act.now())
                fill(len(levels))
                for half in range(2):
                    i = take()
                    for tile in (2 * half, 2 * half + 1):
                        for h in range(4):
                            v_cols = slice(h * 64, (h + 1) * 64)
                            products = [(near[:, h, tile * P:(tile + 1) * P], v2[:, tile, v_cols])]
                            if tile % 2:
                                n_far = tile // 2
                                products.append((far[:, h, n_far * P:(n_far + 1) * P],
                                                 v2[:, tile - 1, v_cols]))
                            if tile >= 2:
                                for key in range(2):
                                    at = 256 + key * 256 + (tile - 2) * P
                                    products.append((far[:, h, at:at + P], v2[:, key, v_cols]))
                            at = (tile % 2) * G + h * 64
                            done = psum_group(i, banks[i][:, at:at + 64], products, *scores_done,
                                              v_done[name])
                    o_done = copy_act(y[:, 2 * half:2 * half + 2, :],
                                      banks[i][:, :].rearrange("p (a b) -> p a b", b=G), done)
                    bank_free[i] = [o_done]
                def finish():
                    squares = flat(k2).rearrange("p (a b) -> p a b", b=G)
                    tt(dve, squares, y, y, ALU.mult, o_done)
                    width = G if name == "hgrn" else 64
                    n_norms = TT * G // width
                    ms = small[:, 128:128 + n_norms]
                    split = lambda ap: ap.rearrange("p t (h d) -> p (t h) d", d=width)
                    reduced = dve.do(lambda e: e.tensor_reduce(ms, split(squares), AX_X, ALU.add))
                    root = copy_act(ms, ms, reduced, func=ACT.Sqrt, scale=1.0 / width, bias=EPS)
                    recip(ms, ms, root)
                    tt(dve, split(y), split(y), ms.unsqueeze(2).to_broadcast([P, n_norms, width]), ALU.mult)
                    tt(dve, y, y, v2[:, :, G:], ALU.mult, weighted[name])

                return finish

            weighted = {}

            def weigh_gate(name):
                gate, gain = operands[name][3][:, :, G:], rows[:, 0 if name == "hgrn" else 3, :]
                gated = copy_act(gate, gate, v_done[name], func=ACT.Sigmoid if name == "hgrn" else ACT.Silu)
                weighted[name] = tt(pool, gate, gate, over_tiles(gain), ALU.mult, gated)

            def value_steps(name):
                yield from token_major(1)
                out, done = token_major_result
                v2 = operands[name][3]
                for tile, i in enumerate(out):
                    v_done[name] = ts(dve, v2[:, tile, :], banks[i][:, :], inv_rms_t[:, tile:tile + 1], None,
                                      ALU.mult, ALU.bypass, done)
                    bank_free[i] = [v_done[name]]
                    held.discard(i)
                yield

            lb, e_lb, keep_lb = small[:, 160:162], small[:, 162:164], small[:, 164:166]
            logits = cols[:, COLS["lb_logits"][0]:COLS["lb_logits"][0] + 2]
            centred = tt(dve, e_lb, logits, logits, ALU.subtract)
            raised = copy_act(e_lb, e_lb, centred, func=ACT.Exp)
            recip(lb, e_lb, raised)
            tt(dve, e_lb, e_lb, lb, ALU.mult)
            tt(dve, lb, e_lb, e_lb, ALU.subtract)
            ts(dve, keep_lb, lb, -1.0, 1.0, ALU.mult, ALU.add)

            q2, k2, c2, _ = operands["hgrn"]
            low = E2[0]
            for f in range(2):
                i, done = projected()
                got = tt(dve, q2[:, f, :], banks[i][:, :], inv_rms, ALU.mult, done)
                bank_free[i] = [got]
                bent = copy_act(q2[:, f, :], q2[:, f, :], got, func=ACT.Silu)
                i, done = projected()
                got = tt(dve, k2[:, f, :], banks[i][:, :], inv_rms, ALU.mult, done)
                bank_free[i] = [got]
                sig = copy_act(c2[:, f, :], k2[:, f, :], got, func=ACT.Sigmoid)
                ts(dve, q2[:, f, :], q2[:, f, :], 0.125, None, ALU.mult, ALU.bypass, bent)
                ts(dve, c2[:, f, :], c2[:, f, :], keep_lb[:, f:f + 1], lb[:, f:f + 1], ALU.mult, ALU.add, sig)
                ts(dve, k2[:, f, :], c2[:, f, :], -1.0, 1.0, ALU.mult, ALU.add)
                ts(dve, low[:, f, :], c2[:, f, :], 2.0 ** -60, None, ALU.max, ALU.bypass)
                ts(dve, c2[:, f, :], c2[:, f, :], 1e-30, 2.0 ** 60, ALU.max, ALU.mult)
                got = ts(dve, c2[:, f, :], c2[:, f, :], 1.0, None, ALU.min, ALU.bypass)
            for q in (pe, dve, act, pool):
                q.wait(mixer_in)
            copy_act(flat(low), flat(low), got, func=ACT.Ln)
            logs = copy_act(flat(c2), flat(c2), func=ACT.Ln)
            tt(dve, c2, c2, low, ALU.add, logs)

            def gla_steps():
                q2, k2, c2, _ = operands["gla"]
                for f in range(2):
                    i, done = projected()
                    bank_free[i] = [stt(q2[:, f, :], banks[i][:, :], 0.125, inv_rms, ALU.mult, ALU.mult,
                                        done)]
                    yield
                    i, done = projected()
                    bank_free[i] = [tt(dve, k2[:, f, :], banks[i][:, :], inv_rms, ALU.mult, done)]
                    yield
                i, done = projected()
                ga = ga_sb[0:16, :]
                ga_done = tt(dve, ga, banks[i][0:16, :], inv_rms[0:16, :], ALU.mult, done)
                bank_free[i] = [ga_done]
                for f in range(2):
                    size = operands["gla"][3][:, f, :]
                    i = take()
                    done = psum_group(i, banks[i][:, :], [(gla_w2[0:16, f * P:(f + 1) * P], ga)], ga_done)
                    low = ts(dve, c2[:, f, :], banks[i][:, :], col("gla_b", f), 0.0, ALU.add, ALU.min, done)
                    sized = copy_act(size, banks[i][:, :], low, func=ACT.Abs, bias=col("gla_b", f))
                    bank_free[i] = [sized]
                    copy_act(size, size, func=ACT.Exp, scale=-1.0)
                    logs = copy_act(size, size, func=ACT.Ln, bias=1.0)
                    tt(dve, c2[:, f, :], c2[:, f, :], size, ALU.subtract, logs)
                    ts(dve, c2[:, f, :], c2[:, f, :], 1.0 / 16, None, ALU.mult, ALU.bypass)
                yield

            values_h, others = value_steps("hgrn"), gla_steps()
            values_g = value_steps("gla")

            def fill_hgrn(n):
                if n == 0:
                    next(values_h)
                    next(values_h)
                    pool_outputs()
                elif n == 7:
                    weigh_gate("hgrn")
                else:
                    next(values_h if n < 3 else others if n < 9 else values_g)

            finish_hgrn = linear_attention("hgrn", y_tok["hgrn"], fill_hgrn)

            region = Region(first_at, second_at)
            mixed = region.room("mixed", 8, SEQ)
            shifted = region.room("shifted", 2, SEQ)
            keep = small[:, 100:108]
            kept = ts(dve, keep, cols[:, COLS["rwkv_mu"][0]:COLS["rwkv_mu"][0] + 8], -1.0, 1.0, ALU.mult,
                      ALU.add)
            mix, own = [None], [None, None]

            def rwkv_steps():
                for f in range(8):
                    i, done = projected()
                    s = shifted[:, f % 2, :]
                    scaled = tt(dve, s, banks[i][:, :], inv_rms, ALU.mult, done, own[f % 2])
                    bank_free[i] = [scaled]
                    own[f % 2] = copy_act(mixed[:, f, :], s, scaled, kept, scale=keep[:, f:f + 1])
                    mix[0] = stt(mixed[:, f, 1:], s[:, 0:SEQ - 1], col("rwkv_mu", f), mixed[:, f, 1:],
                                 ALU.mult, ALU.add, own[f % 2])
                    yield

            projections = rwkv_steps()

            free_xg = Region(xg_at, phase_at)
            kkE, rE, bI, kI = (free_xg.room(n, 2, SEQ) for n in ("kkE", "rE", "bI", "kI"))
            tok_at = free_xg.at
            tokA = free_xg.room("tokA", TT, 512)
            tokB = free_xg.room("tokB", TT, 512)
            over = Region(tok_at, phase_at)
            sigma, cum, a_gate, tmp = (over.room(n, 2, SEQ) for n in ("sigma", "cum", "a_gate", "tmp"))
            eI, kk = rE, bI
            eB = Region(rotary_at, xg_at).room("eB", 2, SEQ)
            kept_bytes = 4 * TT * G
            g_tok = Region(stay.end - kept_bytes, stay.end).room("g_tok", TT, G)
            rr, rk, rv = mixed[:, 0:2, :], mixed[:, 2:4, :], mixed[:, 4:6, :]
            prepared = {}

            def operand_steps():
                mixed_done = mix[0]
                bent = copy_act(mixed[0:64, 6, :], mixed[0:64, 6, :], mixed_done, func=ACT.Tanh)
                gate_in = copy_act(mixed[:, 7, :], mixed[:, 7, :], func=ACT.Sigmoid)
                yield
                for f in range(2):
                    for out, r, bias in ((sigma, slice(0, 64), "rwkv_w0"), (a_gate, slice(64, 128), "rwkv_a0")):
                        i = take()
                        done = psum_group(i, banks[i][:, :],
                                          [(lora[r, 0, f * P:(f + 1) * P], mixed[r, 6, :])], bent)
                        sig = copy_act(out[:, f, :], banks[i][:, :], done, func=ACT.Sigmoid, bias=col(bias, f))
                        bank_free[i] = [sig]
                for f in range(2):
                    ts(dve, kk[:, f, :], rk[:, f, :], col("rwkv_k_k", f), None, ALU.mult, ALU.bypass, sig)
                sq = tt(dve, kI, kk, kk, ALU.mult)
                yield
                for half in range(2):
                    i = take()
                    for j in range(2):
                        tile = 2 * half + j
                        done = psum_group(i, banks[i][:, j * G:(j + 1) * G],
                                          [(mixed[:, 7, tile * P:(tile + 1) * P], lora[:, 1, :])], gate_in)
                    g_done = copy_act(g_tok[:, 2 * half:2 * half + 2, :],
                                      banks[i][:, :].rearrange("p (a b) -> p a b", b=G), done)
                    bank_free[i] = [g_done]
                for f in range(2):
                    i = take()
                    done = psum_group(i, banks[i][:, :], [(same_head, kI[:, f, :])], sq)
                    floored = ts(dve, kI[:, f, :], banks[i][:, :], 1e-24, None, ALU.max, ALU.bypass, done)
                    bank_free[i] = [floored]
                root = copy_act(kI, kI, floored, func=ACT.Sqrt)
                for f in range(2):
                    scanned = dve.do(lambda e, f=f: e.tensor_tensor_scan(
                        cum[:, f, :], table("restart"), sigma[:, f, :], 0.0, ALU.mult, ALU.add), sig)
                before = tt(dve, tmp, cum, sigma, ALU.subtract)
                yield
                copy_act(eB, cum, scanned, func=ACT.Exp, scale=-HALF_E)
                copy_act(eI, cum, scanned, func=ACT.Exp, scale=HALF_E)
                exps = copy_act(tmp, tmp, before, func=ACT.Exp, scale=-HALF_E)
                recip(kI, kI, root)
                tt(dve, kk, kk, kI, ALU.mult)
                yield
                tt(dve, kkE, kk, tmp, ALU.mult, exps)
                tt(dve, bI, kk, a_gate, ALU.mult)
                tt(dve, bI, bI, eI, ALU.mult)
                yield
                for f in range(2):
                    ts(dve, tmp[:, f, :], a_gate[:, f, :], 1.0, col("rwkv_k_a", f), ALU.subtract, ALU.mult)
                    stt(rk[:, f, :], tmp[:, f, :], 1.0, rk[:, f, :], ALU.add, ALU.mult)
                    stt(sigma[:, f, :], rr[:, f, :], col("rwkv_r_k", f), rk[:, f, :], ALU.mult, ALU.mult)
                yield
                tt(dve, kI, rk, eI, ALU.mult)
                scaled = tt(dve, rE, rr, eB, ALU.mult)
                bonus = small[:, 112:128]
                i = take()
                for tile in range(TT):
                    for f in range(2):
                        at = 4 * tile + 2 * f
                        done = psum_group(i, banks[i][:, at:at + 2],
                                          [(sigma[:, f, tile * P:(tile + 1) * P], same_head[:, 0:P:64])],
                                          scaled)
                bonus_done = copy_act(bonus, banks[i][:, 0:16], done)
                bank_free[i] = [bonus_done]
                prepared.update(scaled=scaled, bonus=bonus, bonus_done=bonus_done, g_done=g_done)
                yield

            operand_prep = operand_steps()

            def fill_gla(n):
                if n == 0:
                    next(values_g)
                    finish_hgrn()
                    next(projections)
                elif n < 3:
                    next(values_g)
                    next(projections)
                elif n < 6:
                    next(projections)
                    if n > 3:
                        next(projections, None)
                    if n == 5:
                        pe_used_xg[0] = pe.now()
                else:
                    next(operand_prep)
                    if n == 6:
                        weigh_gate("gla")

            finish_gla = linear_attention("gla", y_tok["gla"], fill_gla)
            for _ in operand_prep:
                pass
            scaled, bonus, bonus_done, g_done = (prepared[n] for n in ("scaled", "bonus", "bonus_done", "g_done"))
            for tile in range(TT):
                c = slice(tile * P, (tile + 1) * P)
                for out, (a, b) in ((tokA, (kkE, kI)), (tokB, (bI, rv))):
                    i = take()
                    done = transposes(i, [(banks[i][:, n * P:(n + 1) * P], s[:, n % 2, c])
                                          for n, s in enumerate((a, a, b, b))], scaled)
                    tok_done = copy_act(out[:, tile, :], banks[i][:, :], done)
                    bank_free[i] = [tok_done]
            finish_gla()

            fence()
            region = Region(first_at, stay.end - kept_bytes)
            M_rk, M_rb = (region.room(n, 4, TT * P) for n in ("M_rk", "M_rb"))
            W2T = region.room("W2T", TT, 2, P)
            y_at = region.at
            XT, AT, X = (region.room(n, 4, TT * P) for n in ("XT", "AT", "X"))
            Gv = region.room("Gv", 4, TT * 64)
            A_ak, CT = (region.room(n, 2, TT * P) for n in ("A_ak", "CT"))
            Pm = region.room("Pm", 4, TT * P)
            W1 = region.room("W1", TT, G)

            def gram(h, left, right):
                r, f = slice(64 * (h % 2), 64 * (h % 2) + 64), h // 2
                i = take()
                for tile in range(TT):
                    c = slice(tile * P, (tile + 1) * P)
                    done = psum_group(i, banks[i][:, c], [(left[r, f, c], right[r, f, c])], scaled)
                return i, done

            def masked(out, h, left, right, mask, *tokens):
                i, done = gram(h, left, right)
                made = tt(dve, tiles4(out), tiles4(banks[i][:, :]), over_tiles(mask), ALU.mult, done,
                          *tokens)
                bank_free[i] = [made]
                return made

            def per_tile(left, right, *tokens, out=lambda b, tile: b[:, tile * P:(tile + 1) * P]):
                i = take()
                for tile in range(TT):
                    done = psum_group(i, out(banks[i], tile), [(left(tile), right(tile))], *tokens)
                return i, done

            def tile_of(ap):
                return lambda tile: ap[:, tile * P:(tile + 1) * P]

            cols64 = lambda b, tile: b[:, tile * 64:(tile + 1) * 64]
            HEADS = range(4)
            x_done, xt_done, ct_free = {}, {}, [None, None]
            below = {}

            def next_below(m, h):
                below[h] = tt(pool, tiles4(CT[:, h % 2, :]), tiles4(AT[:, h, :]), over_tiles(pairs(m)),
                              ALU.mult, xt_done[h], ct_free[h % 2])

            for h in HEADS:
                at_done = masked(AT[:, h, :], h, bI, kkE, table("before"))
                tt(dve, tiles4(XT[:, h, :]), tiles4(AT[:, h, :]), over_tiles(pairs(1)), ALU.mult, at_done)
                xt_done[h] = stt(tiles4(XT[:, h, :]), tiles4(XT[:, h, :]), -1.0, over_tiles(ident),
                                 ALU.mult, ALU.add)
                if h < 2:
                    next_below(2, h)
                masked(X[:, h, :], h, kkE, bI, table("pairs_ts"))
                x_done[h] = stt(tiles4(X[:, h, :]), tiles4(X[:, h, :]), -1.0, over_tiles(ident), ALU.mult,
                                ALU.add)

            def side_products():
                used = [None, None]
                for h in HEADS:
                    made = masked(A_ak[:, h % 2, :], h, kI, kkE, table("before"), used[h % 2])
                    yield
                    v_cols = slice(G + h * 64, G + (h + 1) * 64)
                    i, used[h % 2] = per_tile(tile_of(A_ak[:, h % 2, :]), lambda tile: tokB[:, tile, v_cols],
                                              made, tok_done, out=cols64)
                    gv_done[h] = copy_act(Gv[:, h, :], banks[i][:, 0:TT * 64], used[h % 2])
                    bank_free[i] = [gv_done[h]]
                    m_done.append(masked(M_rk[:, h, :], h, kI, rE, table("upto")))
                    yield
                    m_done.append(masked(M_rb[:, h, :], h, bI, rE, table("upto")))
                    yield

            gv_done, m_done = {}, []
            side = side_products()
            for m in (2, 4, 8, 16, 32):
                p_done = {}
                half_of = lambda ap, right, m=m: lambda tile: halves(tile_of(ap)(tile), m, right)
                compact = lambda b, tile, m=m: b[:, tile * 64:(tile + 1) * 64].rearrange(
                    "p (n c) -> p n c", c=m)

                def update(ap, right, i, done, m=m):
                    part = halves(ap, m, right)
                    bank_free[i] = [tt(dve, part, part, banks[i][:, 0:256].rearrange(
                        "p (n c) -> p n c", c=m), ALU.subtract, done)]
                    return bank_free[i][0]

                def product(h):
                    i, done = per_tile(tile_of(CT[:, h % 2, :]), tile_of(X[:, h, :]), below[h], x_done[h])
                    ct_free[h % 2] = done
                    p_done[h] = copy_act(Pm[:, h, :], banks[i][:, :], done)
                    bank_free[i] = [p_done[h]]
                    if h < 2:
                        next_below(m, h + 2)
                    elif m < 32:
                        next_below(2 * m, h - 2)

                def updates(h):
                    if m < 32:
                        i, done = per_tile(tile_of(XT[:, h, :]), half_of(Pm[:, h, :], False), p_done[h],
                                           xt_done[h], out=compact)
                        x_done[h] = update(X[:, h, :], False, i, done)
                    i, done = per_tile(tile_of(Pm[:, h, :]), half_of(XT[:, h, :], True), p_done[h],
                                       xt_done[h], out=compact)
                    xt_done[h] = update(XT[:, h, :], True, i, done)

                product(0)
                product(1)
                for h in HEADS:
                    if h + 2 < 4:
                        updates(h)
                        product(h + 2)
                    else:
                        next(side, None)
                        updates(h)
                next(side, None)
            for _ in side:
                pass
            for h in HEADS:
                i, done = per_tile(tile_of(XT[:, h, :]), lambda tile: Gv[:, h, tile * 64:(tile + 1) * 64],
                                   gv_done[h], xt_done[h], out=cols64)
                w1_done = copy_act(W1[:, :, h * 64:(h + 1) * 64],
                                   banks[i][:, 0:TT * 64].rearrange("p (a b) -> p a b", b=64), done,
                                   scale=-1.0)
                bank_free[i] = [w1_done]
                r = slice(64 * (h % 2), 64 * (h % 2) + 64)
                i, done = per_tile(lambda tile: tokA[:, tile, h * 64:(h + 1) * 64], tile_of(XT[:, h, :]),
                                   out=lambda b, tile: b[r, tile * P:(tile + 1) * P])
                w2_done = ts(dve, W2T[r, :, h // 2, :], tiles4(banks[i][r, :]), 1.0, None, ALU.mult,
                             ALU.bypass, done)
                bank_free[i] = [w2_done]

            fence()
            region = Region(y_at, stay.end - kept_bytes)
            y_high, y_low = (region.room(part, KT, SEQ, dt=F32R) for part in ("y_high", "y_low"))
            offset = region.room("offset", TT, G)
            free_k = kI.rearrange("p a b -> p (a b)")
            S, S1, *fades = (free_k[:, n * 256:(n + 1) * 256].rearrange("p (a b) -> p a b", b=P)
                             for n in range(4))
            s_done = dve.do(lambda e: e.memset(S, 0.0))
            y_made = []
            for f in range(2):
                rounded = copy_act(y_high[:, f, :], y_pool[:, f, :])
                y_made.append(tt(dve, y_low[:, f, :], y_pool[:, f, :], y_high[:, f, :].bitcast(F32),
                                 ALU.subtract, rounded))
            for name in ("hgrn", "gla"):
                for f in range(2):
                    y_made.append(to_token(y_tok[name], f, len(y_made)))
            for tile in range(TT):
                heads = lambda ap: ap.rearrange("p (h d) -> p h d", d=64)
                tt(pool, heads(offset[:, tile, :]), heads(tokB[:, tile, G:]),
                   bonus[:, 4 * tile:4 * tile + 4].unsqueeze(2).to_broadcast([P, 4, 64]), ALU.mult, bonus_done)
            tt(pool, offset, offset, over_tiles(rows[:, 2, :]), ALU.add)
            tt(pool, offset, offset, g_tok, ALU.mult, g_done)
            gate_ready = tt(pool, g_tok, g_tok, over_tiles(rows[:, 1, :]), ALU.mult)

            def output_parts():
                for f in range(KT):
                    i = take()
                    held.add(i)
                    pe.wait(*bank_free[i])
                    slot, (high, low, ready) = next_unit()
                    pe.wait(ready)
                    for k in range(6):
                        c = slice(k * P, (k + 1) * P)
                        pe.wait(y_made[k])
                        emits = list(three_passes(banks[i][:, :], (high[:, c], low[:, c]),
                                                  (y_high[:, k, :], y_low[:, k, :]), k == 0, k == 5))
                        if k < 5:
                            for emit in emits:
                                pe.quiet(emit)
                        if k == 2:
                            yield
                    done = run_products(slot, emits)
                    bank_free[i] = [tt(dve, x[:, f, :], x[:, f, :], banks[i][:, :], ALU.add, done)]
                    held.discard(i)
                    yield

            filler = output_parts()

            U = kkE.rearrange("p a b -> p (a b)").rearrange("p (a b) -> p a b", b=G)
            out_r = y_tok["rwkv"]
            fade_free = [None, None]
            n_chunks = SEQ // CHUNK
            o_bank = None

            def finish_tile(tile, o_done):
                out, squares = out_r[:, tile, :], U[:, tile, :]
                mean, var = small[:, 128 + 8 * tile:132 + 8 * tile], small[:, 132 + 8 * tile:136 + 8 * tile]
                per_head = lambda ap: ap.unsqueeze(2).to_broadcast([P, 4, 64])
                dve.do(lambda e: e.tensor_reduce(mean, heads(out), AX_X, ALU.add), o_done)
                ts(dve, mean, mean, 1.0 / 64, None, ALU.mult, ALU.bypass)
                tt(dve, heads(out), heads(out), per_head(mean), ALU.subtract)
                tt(dve, squares, out, out, ALU.mult)
                summed = dve.do(lambda e: e.tensor_reduce(var, heads(squares), AX_X, ALU.add))
                root = copy_act(var, var, summed, func=ACT.Sqrt, scale=1.0 / 64, bias=GN_EPS)
                yield
                recip(var, var, root)
                tt(dve, heads(out), heads(out), per_head(var), ALU.mult)
                tt(dve, out, out, g_tok[:, tile, :], ALU.mult, gate_ready)
                gated = tt(dve, out, out, offset[:, tile, :], ALU.add)
                yield
                i = take()
                done = transposes(i, [(banks[i][:, f * P:(f + 1) * P], out[:, f * P:(f + 1) * P])
                                      for f in range(2)], gated)
                part = (slice(None), slice(6, 8), slice(tile * P, (tile + 1) * P))
                src = banks[i][:, 0:G].rearrange("p (f c) -> p f c", c=P)
                rounded = copy_act(y_high[part], src, done)
                bank_free[i] = [tt(dve, y_low[part], src, y_high[part].bitcast(F32), ALU.subtract, rounded)]
                y_rwkv.append(bank_free[i][0])
                yield

            y_rwkv, finishing = [], iter(())
            for c in range(n_chunks):
                tile, r = c // 2, slice(64 * (c % 2), 64 * (c % 2) + 64)
                fade = fades[c % 2]
                for f in range(2):
                    faded = copy_act(fade[:, f, :], same_head, fade_free[c % 2],
                                     scale=eB[:, f, 64 * c + 63:64 * c + 64])
                i = take()
                for f in range(2):
                    done = psum_group(i, banks[i][r, f * P:(f + 1) * P],
                                      [(W2T[:, tile, f, 64 * (c % 2):64 * (c % 2) + 64], S[:, f, :])],
                                      s_done, w2_done)
                u_done = stt(U[r, tile, :], banks[i][r, 0:G], -1.0, W1[r, tile, :], ALU.mult, ALU.add, done,
                             w1_done)
                bank_free[i] = [u_done]
                if c % 2 == 0:
                    o_bank = take()
                    held.add(o_bank)
                    pe.wait(*bank_free[o_bank])
                for f in range(2):
                    emit = (lambda e, o=banks[o_bank][r, f * P:(f + 1) * P],
                            l=rE[:, f, 64 * c:64 * c + 64], s=S[:, f, :], first=(f == 0):
                            e.matmul(o, l, s, start=first, stop=False, skip_group_check=True))
                    if f == 0:
                        pe.quiet(emit)
                    else:
                        s_read = pe.do(emit)
                next(filler, None)
                if c < n_chunks - 1:
                    i = take()
                    for f in range(2):
                        lo, hi = slice(f * P, (f + 1) * P), slice(G + f * P, G + (f + 1) * P)
                        done = psum_group(i, banks[i][:, lo],
                                          [(tokA[r, tile, hi], tokB[r, tile, hi]),
                                           (tokB[r, tile, lo], U[r, tile, lo])], u_done)
                    tt(dve, S1, banks[i][:, 0:G].rearrange("p (a b) -> p a b", b=P), S, ALU.add, done)
                    s_done = tt(dve, S, S1, fade, ALU.mult, faded, s_read)
                    fade_free[c % 2] = s_done
                    bank_free[i] = [s_done]
                next(finishing, None)
                if c % 2 == 1:
                    pe.wait(u_done, *m_done)
                    for h in HEADS:
                        v_cols, o_cols = slice(G + h * 64, G + (h + 1) * 64), slice(h * 64, (h + 1) * 64)
                        m_cols = slice(tile * P, (tile + 1) * P)
                        pe.quiet(lambda e, o=banks[o_bank][:, o_cols], l=M_rk[:, h, m_cols],
                                 v=tokB[:, tile, v_cols]:
                                 e.matmul(o, l, v, start=False, stop=False, skip_group_check=True))
                        done = pe.do(lambda e, o=banks[o_bank][:, o_cols], l=M_rb[:, h, m_cols],
                                     v=U[:, tile, o_cols]:
                                     e.matmul(o, l, v, start=False, stop=True, skip_group_check=True))
                    o_done = copy_act(out_r[:, tile, :], banks[o_bank][:, 0:G], done)
                    bank_free[o_bank] = [o_done]
                    held.discard(o_bank)
                    for _ in finishing:
                        pass
                    finishing = finish_tile(tile, o_done)
                    if c == n_chunks - 1:
                        next(finishing)
                        next(finishing)
                next(filler, None)
            for _ in filler:
                pass
            for _ in finishing:
                pass

            for f in range(KT):
                if f % 4 == 0:
                    slot, (high, low, ready) = next_unit()
                    pe.wait(ready)
                i = take()
                pe.wait(*bank_free[i], *y_rwkv)
                emits = []
                for k in range(2):
                    at = (2 * (f % 4) + k) * P
                    emits += three_passes(banks[i][:, :], (high[:, at:at + P], low[:, at:at + P]),
                                          (y_high[:, 6 + k, :], y_low[:, 6 + k, :]), k == 0, k == 1)
                done = run_products(slot, emits)
                added = tt(dve, x[:, f, :], x[:, f, :], banks[i][:, :], ALU.add, done)
                bank_free[i] = [added]
                gained(f, "norm_ffn2", added, pe_used_xg[0])
                square_in(f, added)

        feed_forward(0, "norm_mix")
        mixers()
        feed_forward(1, None)

        rms_done, _ = finish_norm()
        out_sem = sem("out_stored")
        sent = [0]

        def send(f, token):
            sent[0] += 1
            q = (sp, act)[f % 2]
            q.dma(lambda e: e.dma_start(t["outT"][:, f, :], x[:, f, :]), out_sem, 0, token)

        normalise("norm_final", send, rms_done)
        sp.wait((out_sem, 16 * sent[0]))

        block = ctx.enter_context(nc.Block())
        block.tensor(pe.run)
        block.vector(dve.run)
        block.scalar(act.run)
        block.gpsimd(pool.run)
        block.sync(sp.run)


def constants():
    f32 = np.float32
    shared = np.zeros((P, N_SHARED), f32)
    shared[:, 0:128] = np.eye(P)
    lin = np.linspace(0.0, 1.0, RET_DIM // 2, dtype=f32)
    shared[:, 128:192] = (f32(1.0) / np.power(f32(10000.0), lin)).astype(f32)
    j, i = np.arange(P)[:, None], np.arange(SEQ)[None, :]
    decays = np.zeros((P, RET_HEADS, SEQ), f32)
    for h in range(RET_HEADS):
        log_g = np.log1p(-(2.0 ** (-5.0 - h)))
        decays[:, h] = np.where(i // CHUNK >= j // CHUNK, RET_DIM ** -0.5 * np.exp(np.abs(i - j) * log_g), 0)
    r, c = np.arange(P)[:, None], np.arange(P)[None, :]
    mixer = np.zeros((P, N_MIXER), f32)

    def put(name, a):
        at, n = MIXER[name]
        mixer[:, at:at + n] = a.reshape(a.shape[0], n)

    put("same_head", (r // 64 == c // 64).astype(f32))
    put("before", ((r // 64 == c // 64) & (r < c)).astype(f32))
    put("upto", ((r // 64 == c // 64) & (r <= c)).astype(f32))
    pair = lambda m, s, t: ((s // (2 * m) == t // (2 * m)) & (s // m % 2 == 0) & (t // m % 2 == 1))
    put("pairs", np.stack([pair(m, r, c) for m in LEVELS], 1).astype(f32))
    put("pairs_ts", pair(1, c, r).astype(f32))
    tokens = np.arange(SEQ)
    put("restart", np.broadcast_to((tokens % CHUNK != 0).astype(f32), (P, SEQ)))
    windows = np.array([[2, 8], [4, 16]])[np.arange(P) // 64]
    count = np.minimum(tokens[None, None, :] + 1, windows[:, :, None])
    return shared, decays, mixer, (1.0 / count).astype(f32)


def layouts(inputs):
    a = {k: np.asarray(v) for k, v in inputs.items()}

    def tiles(w, m=P):
        k, n = w.shape
        return w.reshape(k // P, P, n // m, m).transpose(2, 1, 0, 3).reshape(n // m, P, -1)

    def groups(w):
        k, n = w.shape
        return w.reshape(k // 256, 2, P, n // 512, 512).transpose(3, 0, 2, 1, 4).reshape(
            n // 512, k // 256, P, 1024)

    out = {"xT": a["x"][0].T.reshape(KT, P, SEQ).transpose(1, 0, 2),
           "positions": a["positions"].astype(np.int32).reshape(TT, P).T}
    w_in = a["w_in"]
    out["w_qk"] = np.stack([tiles(w[:, 0:1024]) for w in w_in])
    order = (4, 5, 2, 3, 6, 7)
    out["w_tok"] = np.stack([np.concatenate([groups(w[:, 512 * g:512 * g + 512]) for g in order])
                             for w in w_in])
    out["w_out"] = np.stack([tiles(w) for w in a["w_out"]])
    r = a["rel_bias"]
    distance = np.arange(P)[:, None] + (SEQ - P) - np.arange(SEQ)[None, :]
    strips = r[:, :, np.clip(distance, -CLIP, CLIP) + CLIP]
    out["strips"] = strips
    ffn = [(a["ffn1_w_in_2"][0], a["ffn1_w_out_2"][0]), (a["ffn2_w_in_2"][0], a["ffn2_w_out_2"][0])]
    out["w_ffn_in"] = np.stack([np.stack([tiles(w[:, :D_FF]), tiles(w[:, D_FF:])], 1)
                                .reshape(2 * FT, P, UNIT) for w, _ in ffn])
    out["w_ffn_out"] = np.stack([tiles(w) for _, w in ffn])
    named = {"gain0": a["norm_gain"][0], "gain1": a["norm_gain"][1], "final_gain": a["final_gain"],
             "norm_ffn1": a["norm_ffn1_2"], "norm_mix": a["norm_mix_2"], "norm_ffn2": a["norm_ffn2_2"],
             "norm_final": a["norm_final_2"], "pool_b": a["pool_b_2"], "pool_scale": a["pool_scale_2"],
             "rwkv_mu": a["rwkv_mu_2"], "rwkv_w0": a["rwkv_w0_2"], "rwkv_a0": a["rwkv_a0_2"],
             "rwkv_k_k": a["rwkv_k_k_2"], "rwkv_k_a": a["rwkv_k_a_2"], "rwkv_r_k": a["rwkv_r_k_2"],
             "gla_b": a["gla_b_2"], "lb_logits": a["hgrn_lb_logits_2"]}
    out["cols"] = np.concatenate([named[k].reshape(n, P).T for k, (_, n) in COLS.items()], axis=1)
    out["shared"], out["decays"], out["mixer"], out["inv_count"] = constants()
    w = a["w_in_2"][0]
    feature_cols = ((0, 256), (1280, 2304), (256, 512), (512, 768), (2304, 2560), (2560, 2816))
    out["w_mix_f"] = np.concatenate([tiles(w[:, lo:hi]) for lo, hi in feature_cols])
    out["w_mix_ga"] = tiles(np.pad(w[:, 3328:], ((0, 0), (0, P - 16))))[0]
    out["w_mix_tok"] = np.concatenate([groups(w[:, 768:1280]), groups(w[:, 2816:3328])])
    w = a["w_out_2"][0]
    out["w_mix_out"] = tiles(np.concatenate([w[0:512], w[768:1024]]))
    out["w_mix_out_rwkv"] = tiles(w[512:768], 512).reshape(2, P, 2, 4, P).transpose(
        0, 1, 3, 2, 4).reshape(2, P, UNIT)
    out["rows"] = np.stack([np.broadcast_to(a[k][0], (P, G)) for k in
                            ("hgrn_norm_2", "rwkv_ln_w_2", "rwkv_ln_b_2", "gla_norm_2")], axis=1)
    out["lora"] = np.stack([np.concatenate([a["rwkv_w2_2"][0], a["rwkv_a2_2"][0]]), a["rwkv_g2_2"][0]], 1)
    out["gla_w2"] = a["gla_w2_2"][0]
    out["pool_w"] = a["pool_w_2"][0].reshape(2, P, 64).transpose(1, 0, 2)
    return {k: np.ascontiguousarray(v) for k, v in out.items()}


def kernel(**inputs):
    import concourse.bacc as bacc
    from concourse.bass_utils import run_bass_kernel_spmd

    nc = bacc.Bacc("TRN2", target_bir_lowering=False, num_devices=1)
    arrays = layouts(inputs)
    t = {k: nc.dram_tensor(k, v.shape, mybir.dt.from_np(v.dtype), kind="ExternalInput").ap()
         for k, v in arrays.items()}
    t["outT"] = nc.dram_tensor("outT", (P, KT, SEQ), F32, kind="ExternalOutput").ap()
    build(nc, t)
    got = run_bass_kernel_spmd(nc, [arrays], core_ids=[0]).results[0]["outT"]
    return got.transpose(2, 1, 0).reshape(1, SEQ, D)
```
